# Optimizing a Trainium2 kernel written in Bass

```python
import jax, jax.numpy as jnp
from jax import lax
import numpy as np

D_MODEL = 1024
BATCH = 1
SEQ = 2048
DEPTH = 1
DEC_BATCH = 1
DEC_SEQ = 32
PAST_LEN = 128

CHUNK = 64
QBLK = 128
MIX_WIDTH = D_MODEL
MLA_HEADS = 8
MLA_NOPE = 64
MLA_ROPE = 32
MLA_V = 64
Q_LORA = 384
KV_LORA = 256
ROPE_BASE = 10000.0
MLA_OUT = MLA_HEADS * MLA_V
MLA_IN = Q_LORA + KV_LORA + MLA_ROPE
MLA_SCALE = (MLA_NOPE + MLA_ROPE) ** -0.5
RWKV_HEADS = 8
RWKV_N = 64
RWKV_DIM = RWKV_HEADS * RWKV_N
DECAY_LORA = 64
AAA_LORA = 64
GATE_LORA = 128
RWKV_IN = 3 * RWKV_DIM + DECAY_LORA + AAA_LORA + GATE_LORA
IN_WIDTH = MLA_IN + RWKV_IN
N_GROUPS = 4
EXPERTS_PER_GROUP = 8
N_EXPERTS = N_GROUPS * EXPERTS_PER_GROUP
TOP_K = 2
D_EXPERT = 256
MOE_BLK = 256
LN_EPS = 1e-5
RMS_EPS = 1e-6
GN_EPS = 64e-5
NEG_INF = -1e30
DN_ALPHA = (2 * DEPTH) ** 0.25
DN_BETA = (8 * DEPTH) ** -0.25

kernel_name = "hybrid_mla_rwkv7_hmoe_stream_step"

F32 = jnp.float32

def rms_norm(x, g):
    xf = x.astype(F32)
    y = xf * lax.rsqrt(jnp.mean(xf * xf, -1, keepdims=True) + RMS_EPS)
    return (y * g.astype(F32)).astype(x.dtype)

def layer_norm(x, g, b):
    xf = x.astype(F32)
    xc = xf - jnp.mean(xf, -1, keepdims=True)
    var = jnp.mean(xc * xc, -1, keepdims=True)
    return (xc * lax.rsqrt(var + LN_EPS) * g.astype(F32) + b.astype(F32)).astype(x.dtype)

def rope_tables(pos):
    inv = ROPE_BASE ** (-jnp.arange(0, MLA_ROPE, 2, dtype=F32) / MLA_ROPE)
    ang = pos.astype(F32)[:, None] * inv[None, :]
    return jnp.cos(ang), jnp.sin(ang)

def apply_rope(x, cos, sin):
    half = MLA_ROPE // 2
    xf = x.astype(F32)
    x1, x2 = xf[..., :half], xf[..., half:]
    return jnp.concatenate([x1 * cos - x2 * sin, x1 * sin + x2 * cos], -1).astype(x.dtype)

def chunk_mask(qpos, kpos):
    return (kpos // CHUNK)[None, :] <= (qpos // CHUNK)[:, None]

def mla_block_attend(qn, qp, kn, kp, v, qpos, kpos):
    s = jnp.einsum('bqhd,bkhd->bhqk', qn, kn) + jnp.einsum('bqhr,bkr->bhqk', qp, kp)
    s = jnp.where(chunk_mask(qpos, kpos), s.astype(F32) * MLA_SCALE, NEG_INF)
    p = jax.nn.softmax(s, axis=-1).astype(v.dtype)
    return jnp.einsum('bhqk,bkhd->bqhd', p, v)

def mla_prompt(q_nope, q_pe, ckv, kpe, w_ukv, pos):
    kv = jnp.einsum('bsl,lhe->bshe', ckv, w_ukv)
    k_nope, v = kv[..., :MLA_NOPE], kv[..., MLA_NOPE:]
    outs = []
    for i in range(q_nope.shape[1] // QBLK):
        lo, hi = i * QBLK, (i + 1) * QBLK
        outs.append(mla_block_attend(q_nope[:, lo:hi], q_pe[:, lo:hi], k_nope[:, :hi], kpe[:, :hi],
                                     v[:, :hi], pos[lo:hi], pos[:hi]))
    return jnp.concatenate(outs, axis=1)

def mla_sample(q_nope, q_pe, ckv, kpe, past_ckv, past_kpe, w_ukv, pos):
    ckv_all = jnp.concatenate([past_ckv.astype(ckv.dtype), ckv], axis=1)
    kpe_all = jnp.concatenate([past_kpe.astype(kpe.dtype), kpe], axis=1)
    kpos = jnp.arange(ckv_all.shape[1], dtype=jnp.int32)
    w_uk, w_uv = w_ukv[..., :MLA_NOPE], w_ukv[..., MLA_NOPE:]
    q_lat = jnp.einsum('bqhd,lhd->bqhl', q_nope, w_uk)
    s = jnp.einsum('bqhl,bkl->bhqk', q_lat, ckv_all) + jnp.einsum('bqhr,bkr->bhqk', q_pe, kpe_all)
    s = jnp.where(chunk_mask(pos, kpos), s.astype(F32) * MLA_SCALE, NEG_INF)
    p = jax.nn.softmax(s, axis=-1).astype(ckv_all.dtype)
    o_lat = jnp.einsum('bhqk,bkl->bqhl', p, ckv_all)
    return jnp.einsum('bqhl,lhd->bqhd', o_lat, w_uv)

def wkv_scan(r, w, k, v, a, b, s0):
    def step(s, inp):
        rt, wt, kt, vt, at, bt = inp
        sa = jnp.einsum('bhij,bhj->bhi', s, at)
        s = s * wt[:, :, None, :] + sa[..., None] * bt[:, :, None, :] + vt[..., None] * kt[:, :, None, :]
        return s, jnp.einsum('bhij,bhj->bhi', s, rt)
    xs = tuple(jnp.moveaxis(t.astype(F32), 1, 0) for t in (r, w, k, v, a, b))
    s_fin, y = lax.scan(step, s0.astype(F32), xs, unroll=8)
    return s_fin, jnp.moveaxis(y, 0, 1)

def rwkv7_mixer(pr, wkv0, shift0, mu_shift, w0, w2, a0, a2, g2, k_k, k_a, r_k, lnx_g, lnx_b):
    B, S, _ = pr.shape
    prev = jnp.concatenate([shift0[:, None, :].astype(pr.dtype), pr[:, :-1]], axis=1)
    u = pr + mu_shift * (prev - pr)
    o1, o2, o3 = RWKV_DIM, 2 * RWKV_DIM, 3 * RWKV_DIM
    o4, o5 = o3 + DECAY_LORA, o3 + DECAY_LORA + AAA_LORA
    r, k, v = u[..., :o1], u[..., o1:o2], u[..., o2:o3]
    w_lo, a_lo, g_lo = u[..., o3:o4], u[..., o4:o5], u[..., o5:]
    wl = (w0 + jnp.tanh(w_lo) @ w2).astype(F32)
    decay = jnp.exp(-jnp.exp(-jax.nn.softplus(-wl) - 0.5))
    a = jax.nn.sigmoid((a0 + a_lo @ a2).astype(F32))
    g = jax.nn.sigmoid(g_lo) @ g2
    hs = (B, S, RWKV_HEADS, RWKV_N)
    kf = k.astype(F32)
    kk = (kf * k_k).reshape(hs)
    kk = kk / jnp.maximum(jnp.sqrt(jnp.sum(kk * kk, -1, keepdims=True)), 1e-12)
    kh = (kf * (1.0 + (a - 1.0) * k_a)).reshape(hs)
    rf = r.astype(F32).reshape(hs)
    vh = v.astype(F32).reshape(hs)
    s_fin, y = wkv_scan(rf, decay.reshape(hs), kh, vh, -kk, kk * a.reshape(hs), wkv0)
    yc = y - jnp.mean(y, -1, keepdims=True)
    y = yc * lax.rsqrt(jnp.mean(yc * yc, -1, keepdims=True) + GN_EPS)
    y = y.reshape(B, S, RWKV_DIM) * lnx_g + lnx_b
    bonus = jnp.sum(rf * kh * r_k, -1, keepdims=True) * vh
    y = y + bonus.reshape(B, S, RWKV_DIM)
    return (y * g.astype(F32)).astype(pr.dtype), s_fin

def token_mixers(x, pos0, past_ckv, past_kpe, wkv0, shift0, mix_w):
    (w_in, q_norm_g, kv_norm_g, w_uq, w_ukv, mu_shift, w0, w2, a0, a2, g2,
     k_k, k_a, r_k, lnx_g, lnx_b, w_o) = mix_w
    B, S, _ = x.shape
    proj = jnp.einsum('bsd,de->bse', x, w_in)
    c_q = proj[..., :Q_LORA]
    c_kv = proj[..., Q_LORA:Q_LORA + KV_LORA]
    k_pe = proj[..., Q_LORA + KV_LORA:MLA_IN]
    pr = proj[..., MLA_IN:]
    q = jnp.einsum('bsl,lhe->bshe', rms_norm(c_q, q_norm_g), w_uq)
    ckv = rms_norm(c_kv, kv_norm_g)
    pos = pos0 + jnp.arange(S, dtype=jnp.int32)
    cos, sin = rope_tables(pos)
    q_nope = q[..., :MLA_NOPE]
    q_pe = apply_rope(q[..., MLA_NOPE:], cos[:, None, :], sin[:, None, :])
    kpe = apply_rope(k_pe, cos, sin)
    if past_ckv is None:
        attn = mla_prompt(q_nope, q_pe, ckv, kpe, w_ukv, pos)
    else:
        attn = mla_sample(q_nope, q_pe, ckv, kpe, past_ckv, past_kpe, w_ukv, pos)
    rw, wkv_fin = rwkv7_mixer(pr, wkv0, shift0, mu_shift, w0, w2, a0, a2, g2,
                              k_k, k_a, r_k, lnx_g, lnx_b)
    mixed = jnp.concatenate([attn.reshape(B, S, MLA_OUT).astype(x.dtype), rw], axis=-1)
    out = jnp.einsum('bsm,md->bsd', mixed, w_o)
    return out, ckv, kpe, wkv_fin, pr[:, -1]

def hier_moe(h, moe_w):
    w_gr, b_gr, w_er, b_er, w_eg, w_eu, w_ed = moe_w
    T, D = h.shape
    g_logits = (h @ w_gr + b_gr).astype(F32)
    g_prob = jax.nn.softmax(g_logits, -1)
    grp = jnp.argmax(g_logits, -1).astype(jnp.int32)
    p_grp = jnp.take_along_axis(g_prob, grp[:, None], axis=-1)
    e_logits = (h @ w_er + b_er).astype(F32).reshape(T, N_GROUPS, EXPERTS_PER_GROUP)
    e_in = jnp.take_along_axis(e_logits, grp[:, None, None], axis=1)[:, 0]
    top_p, top_i = lax.top_k(jax.nn.softmax(e_in, -1), TOP_K)
    gate = top_p / jnp.sum(top_p, -1, keepdims=True) * p_grp
    expert = grp[:, None] * EXPERTS_PER_GROUP + top_i.astype(jnp.int32)
    A = T * TOP_K
    flat_e = expert.reshape(A)
    order = jnp.argsort(flat_e)
    e_sorted = flat_e[order]
    tok = order // TOP_K
    counts = jnp.zeros((N_EXPERTS,), jnp.int32).at[flat_e].add(1)
    blocks_per_e = (counts + MOE_BLK - 1) // MOE_BLK
    blk_end = jnp.cumsum(blocks_per_e)
    blk_start = blk_end - blocks_per_e
    row_start = jnp.cumsum(counts) - counts
    dest = blk_start[e_sorted] * MOE_BLK + (jnp.arange(A, dtype=jnp.int32) - row_start[e_sorted])
    n_blk = -(-A // MOE_BLK) + N_EXPERTS
    block_e = jnp.minimum(jnp.searchsorted(blk_end, jnp.arange(n_blk, dtype=jnp.int32), side='right'),
                          N_EXPERTS - 1)
    xs = jnp.zeros((n_blk * MOE_BLK, D), h.dtype).at[dest].set(h[tok])

    def run_block(args):
        xb, e = args
        return (jax.nn.silu(xb @ w_eg[e]) * (xb @ w_eu[e])) @ w_ed[e]

    ys = lax.map(run_block, (xs.reshape(n_blk, MOE_BLK, D), block_e)).reshape(n_blk * MOE_BLK, D)
    y_a = ys[dest] * gate.reshape(A)[order][:, None].astype(h.dtype)
    return jnp.zeros((T, D), h.dtype).at[tok].add(y_a)

def trunk_layer(x, pos0, past_ckv, past_kpe, wkv0, shift0, mix_w, moe_w, ln1_g, ln1_b, ln2_g, ln2_b):
    m, ckv, kpe, wkv, sh = token_mixers(x, pos0, past_ckv, past_kpe, wkv0, shift0, mix_w)
    h = layer_norm(DN_ALPHA * x + m, ln1_g, ln1_b)
    B, S, D = h.shape
    f = hier_moe(h.reshape(B * S, D), moe_w).reshape(B, S, D)
    y = layer_norm(DN_ALPHA * h + f, ln2_g, ln2_b)
    return y, ckv, kpe, wkv, sh

def setup_inputs(seed: int = 0) -> dict:
    key = jax.random.key(seed)
    ks = iter(jax.random.split(key, 48))

    def nrm(shape, scale):
        return jax.random.normal(next(ks), shape, F32) * scale

    def unif(shape, lo, hi):
        return jax.random.uniform(next(ks), shape, F32, lo, hi)

    L = DEPTH
    return {
        "x_prompt": nrm((BATCH, SEQ, D_MODEL), 1.0),
        "x_sample": nrm((DEC_BATCH, DEC_SEQ, D_MODEL), 1.0),
        "cache_ckv": nrm((L, DEC_BATCH, PAST_LEN, KV_LORA), 1.0),
        "cache_kpe": nrm((L, DEC_BATCH, PAST_LEN, MLA_ROPE), 1.0),
        "state_wkv": nrm((L, DEC_BATCH, RWKV_HEADS, RWKV_N, RWKV_N), 0.3),
        "state_shift": nrm((L, DEC_BATCH, RWKV_IN), 1.0),
        "w_in": nrm((L, D_MODEL, IN_WIDTH), D_MODEL ** -0.5),
        "q_norm_g": 1.0 + nrm((L, Q_LORA), 0.05),
        "kv_norm_g": 1.0 + nrm((L, KV_LORA), 0.05),
        "w_uq": nrm((L, Q_LORA, MLA_HEADS, MLA_NOPE + MLA_ROPE), Q_LORA ** -0.5),
        "w_ukv": nrm((L, KV_LORA, MLA_HEADS, MLA_NOPE + MLA_V), KV_LORA ** -0.5),
        "mu_shift": unif((L, RWKV_IN), 0.0, 1.0),
        "w0": unif((L, RWKV_DIM), -6.0, -1.5),
        "w2": nrm((L, DECAY_LORA, RWKV_DIM), 0.5 * DECAY_LORA ** -0.5),
        "a0": nrm((L, RWKV_DIM), 0.5),
        "a2": nrm((L, AAA_LORA, RWKV_DIM), AAA_LORA ** -0.5),
        "g2": nrm((L, GATE_LORA, RWKV_DIM), GATE_LORA ** -0.5),
        "k_k": 0.85 + nrm((L, RWKV_DIM), 0.05),
        "k_a": 1.0 + nrm((L, RWKV_DIM), 0.05),
        "r_k": nrm((L, RWKV_HEADS, RWKV_N), 0.1),
        "lnx_g": 1.0 + nrm((L, RWKV_DIM), 0.05),
        "lnx_b": nrm((L, RWKV_DIM), 0.01),
        "w_o": nrm((L, MIX_WIDTH, D_MODEL), MIX_WIDTH ** -0.5 * DN_BETA),
        "ln1_g": 1.0 + nrm((L, D_MODEL), 0.05),
        "ln1_b": nrm((L, D_MODEL), 0.01),
        "w_gr": nrm((L, D_MODEL, N_GROUPS), D_MODEL ** -0.5),
        "b_gr": nrm((L, N_GROUPS), 0.01),
        "w_er": nrm((L, D_MODEL, N_EXPERTS), D_MODEL ** -0.5),
        "b_er": nrm((L, N_EXPERTS), 0.01),
        "w_eg": nrm((L, N_EXPERTS, D_MODEL, D_EXPERT), D_MODEL ** -0.5),
        "w_eu": nrm((L, N_EXPERTS, D_MODEL, D_EXPERT), D_MODEL ** -0.5),
        "w_ed": nrm((L, N_EXPERTS, D_EXPERT, D_MODEL), D_EXPERT ** -0.5 * DN_BETA),
        "ln2_g": 1.0 + nrm((L, D_MODEL), 0.05),
        "ln2_b": nrm((L, D_MODEL), 0.01),
    }

def reference(x_prompt, x_sample, cache_ckv, cache_kpe, state_wkv, state_shift,
              w_in, q_norm_g, kv_norm_g, w_uq, w_ukv, mu_shift, w0, w2, a0, a2, g2,
              k_k, k_a, r_k, lnx_g, lnx_b, w_o, ln1_g, ln1_b,
              w_gr, b_gr, w_er, b_er, w_eg, w_eu, w_ed, ln2_g, ln2_b):
    B = x_prompt.shape[0]
    past = cache_ckv.shape[2]
    hp, hs = x_prompt, x_sample
    p_ckv, p_kpe, p_wkv, p_sh = [], [], [], []
    s_ckv, s_kpe, s_wkv, s_sh = [], [], [], []
    for l in range(DEPTH):
        mix_w = (w_in[l], q_norm_g[l], kv_norm_g[l], w_uq[l], w_ukv[l], mu_shift[l], w0[l], w2[l],
                 a0[l], a2[l], g2[l], k_k[l], k_a[l], r_k[l], lnx_g[l], lnx_b[l], w_o[l])
        moe_w = (w_gr[l], b_gr[l], w_er[l], b_er[l], w_eg[l], w_eu[l], w_ed[l])
        wkv_zero = jnp.zeros((B, RWKV_HEADS, RWKV_N, RWKV_N), F32)
        sh_zero = jnp.zeros((B, RWKV_IN), hp.dtype)
        hp, c1, k1, w1_, s1 = trunk_layer(hp, 0, None, None, wkv_zero, sh_zero, mix_w, moe_w,
                                          ln1_g[l], ln1_b[l], ln2_g[l], ln2_b[l])
        hs, c2, k2, w2_, s2 = trunk_layer(hs, past, cache_ckv[l], cache_kpe[l], state_wkv[l],
                                          state_shift[l], mix_w, moe_w,
                                          ln1_g[l], ln1_b[l], ln2_g[l], ln2_b[l])
        p_ckv.append(c1); p_kpe.append(k1); p_wkv.append(w1_); p_sh.append(s1)
        s_ckv.append(c2); s_kpe.append(k2); s_wkv.append(w2_); s_sh.append(s2)
    return (hp, hs,
            jnp.stack(p_ckv), jnp.stack(p_kpe), jnp.stack(p_wkv), jnp.stack(p_sh),
            jnp.stack(s_ckv), jnp.stack(s_kpe), jnp.stack(s_wkv), jnp.stack(s_sh))


_drawn_inputs = setup_inputs


def setup_inputs(seed=0):
    import zlib

    import numpy as np

    out = dict(_drawn_inputs(seed))
    spreads = {}
    factors = {'q_norm_g': 4.84,
     'lnx_g': 3.332,
     'lnx_b': 21.748,
     'ln1_b': 3.813,
     'b_gr': 8.0,
     'b_er': 15.241,
     'ln2_b': 5.682}
    for name, (base, spread) in spreads.items():
        noise = np.random.default_rng([zlib.crc32(name.encode()), seed]).standard_normal(out[name].shape)
        drawn = base * np.exp(spread * noise) if base else spread * noise
        out[name] = __import__('jax').numpy.asarray(drawn.astype(out[name].dtype))
    for name, factor in factors.items():
        out[name] = (out[name] * factor).astype(out[name].dtype)
    return out
```

```python
from contextlib import ExitStack

import numpy as np

import concourse.bass as bass
from concourse import mybir

F32 = mybir.dt.float32
I32 = mybir.dt.int32
ALU = mybir.AluOpType
ACT = mybir.ActivationFunctionType
AX = mybir.AxisListType
P = 128
D = 1024
SEQ, DEC, PAST = 2048, 32, 128
NT = SEQ // P + 1
TOK = NT * P
H = 8
NOPE, ROPE, VD = 64, 32, 64
QK = NOPE + ROPE
QL, KVL = 384, 256
CQ, CKV = QL // P, KVL // P
NPR = 14
WCOL = QL + KVL + NPR * P + 2 * ROPE
KC = D // P
NG, EPG, FE = 4, 8, 256
NE = NG * EPG
NR = NG + NE
ASSIGN = 2 * (SEQ + DEC)
NBLK = (ASSIGN + NE * (P - 1)) // P
ALPHA = 2.0 ** 0.25
SCALE = float(QK) ** -0.5
LN_EPS, RMS_EPS, GN_EPS = 1e-5, 1e-6, 64e-5
LOGW = float(np.exp(-0.5))
LEVELS = 6

STEPS = {
    "mixer_tensor": (
        "x_transposed0 x_transposed1 pr_proj0 pr_proj1 pr_proj2 pr_proj3 cq_proj ckv_proj rms_sums lora_w lora_a lora_g "
        "kk_norm q_nope q_pe ckv_tokens v_tokens bonus_sum gram_b0 gram_b1 gram_b2 gram_b3 gram_k0 gram_k1 gram_k2 "
        "gram_k3 gram_l0 gram_l1 Z1_0 Z1_1 U1_0 T1_0 U1_1 T1_1 Z2_0 Z2_1 U2_0 T2_0 U2_1 T2_1 Z3_0 Z3_1 U3_0 T3_0 U3_1 "
        "T3_1 Z4_0 Z4_1 U4_0 T4_0 U4_1 T4_1 Z5_0 Z5_1 U5_0 T5_0 U5_1 T5_1 Z6_0 Z6_1 U6_0 U6_1 b_tokens k_tokens G SA y "
        "state_add y_mean y_var "
    ).split(),
    "mixer_vector": (
        "pr_edge u_diff_low u_mu_low u_low a_lo g_sig u_diff_rkv u_mu_rkv u_rkv kk rms cq_normed ckv_normed kpe_cos "
        "kpe_sin kpe_roped log_w cum mid a_sig a_ka kh kk_norm2 kk_rs kk_normed a_hat en_masked b_gate b_hat k_hat "
        "q_rope_cos q_rope_sin q_roped bonus state_in state_mid RB0 RB1 RB2 RB3 MK0 MK1 MK2 MK3 L0 L1 U0 Z1_0 Z1_1 U1_0 "
        "T1_0 U1_1 T1_1 Z2_0 Z2_1 U2_0 T2_0 U2_1 T2_1 Z3_0 Z3_1 U3_0 T3_0 U3_1 T3_1 Z4_0 Z4_1 U4_0 T4_0 U4_1 T4_1 Z5_0 "
        "Z5_1 U5_0 T5_0 U5_1 T5_1 Z6_0 Z6_1 U6_0 U6_1 state_sum state y_centred y_rs y_normed y_gain y_bias y_bonus "
        "gated "
    ).split(),
    "mixer_scalar": (
        "xT0 xT1 pr0 pr1 pr2 pr3 edges cq_sq ckv_sq rms_root w_lo g_lo w_tanh a_tanh kk_sq kk_root exp_pos exp_neg em "
        "g_out q_nope ckv_tokens v_tokens b_tokens k_tokens G SA y y_sq y_root "
    ).split(),
    "mixer_gpsimd": (
        "r_hat rk rkr T_level0 T_start "
    ).split(),
    "attention_tensor": (
        "K0 K1 K2 K3 K4 V0 V1 V2 S0_0 S1_0 maxrow0 S2_0 ST0_0 PV0_0 maxrow1 S3_0 ST1_0 PV1_0 maxrow2 S4_0 S4_1 ST2_0 "
        "PV2_0 maxrow3 S5_0 S5_1 ST3_0 PV3_0 maxrow4 S6_0 S6_1 ST4_0 ST4_1 PV4_0 PV4_1 maxrow5 S7_0 S7_1 ST5_0 ST5_1 "
        "PV5_0 PV5_1 maxrow6 S8_0 S8_1 S8_2 ST6_0 ST6_1 PV6_0 PV6_1 maxrow7 S9_0 S9_1 S9_2 ST7_0 ST7_1 PV7_0 PV7_1 "
        "maxrow8 S10_0 S10_1 S10_2 ST8_0 ST8_1 PV8_0 ST8_2 PV8_1 PV8_2 maxrow9 S11_0 S11_1 S11_2 ST9_0 ST9_1 PV9_0 "
        "ST9_2 PV9_1 PV9_2 maxrow10 S12_0 S12_1 S12_2 S12_3 ST10_0 ST10_1 PV10_0 ST10_2 PV10_1 PV10_2 maxrow11 S13_0 "
        "S13_1 S13_2 S13_3 ST11_0 ST11_1 PV11_0 ST11_2 PV11_1 PV11_2 maxrow12 S14_0 S14_1 S14_2 S14_3 ST12_0 ST12_1 "
        "PV12_0 ST12_2 PV12_1 ST12_3 PV12_2 PV12_3 maxrow13 S15_0 S15_1 S15_2 S15_3 ST13_0 ST13_1 PV13_0 ST13_2 PV13_1 "
        "ST13_3 PV13_2 PV13_3 maxrow14 S16_0 ST14_0 ST14_1 PV14_0 ST14_2 PV14_1 ST14_3 PV14_2 PV14_3 maxrow15 ST15_0 "
        "ST15_1 PV15_0 ST15_2 PV15_1 ST15_3 PV15_2 PV15_3 maxrow16 ST16_0 PV16_0 "
    ).split(),
    "attention_vector": (
        "V0 V1 V2 max0_0 negmax0 max1_0 negmax1 maxrow0 max2_0 negmax2 sum_0 out_0 maxrow1 max3_0 negmax3 sum_1 out_1 "
        "maxrow2 max4_0 max4_1 negmax4 sum_2 out_2 maxrow3 max5_0 max5_1 negmax5 sum_3 out_3 maxrow4 max6_0 max6_1 "
        "negmax6 sum_4 out_4 maxrow5 max7_0 max7_1 negmax7 sum_5 out_5 maxrow6 max8_0 max8_1 max8_2 negmax8 sum_6 out_6 "
        "maxrow7 max9_0 max9_1 max9_2 negmax9 sum_7 out_7 maxrow8 max10_0 max10_1 max10_2 negmax10 sum_8 out_8 maxrow9 "
        "max11_0 max11_1 max11_2 negmax11 sum_9 out_9 maxrow10 max12_0 max12_1 max12_2 max12_3 negmax12 sum_10 out_10 "
        "maxrow11 max13_0 max13_1 max13_2 max13_3 negmax13 sum_11 out_11 maxrow12 max14_0 max14_1 max14_2 max14_3 "
        "negmax14 sum_12 out_12 maxrow13 max15_0 max15_1 max15_2 max15_3 negmax15 sum_13 out_13 maxrow14 max16_0 "
        "negmax16 sum_14 out_14 maxrow15 sum_15 out_15 maxrow16 sum_16 out_16 "
    ).split(),
    "attention_scalar": (
        "K0 K1 K2 K3 K4 exp0_0 exp1_0 exp2_0 exp3_0 exp4_0 exp4_1 exp5_0 exp5_1 exp6_0 exp6_1 exp7_0 exp7_1 exp8_0 "
        "exp8_1 exp8_2 exp9_0 exp9_1 exp9_2 exp10_0 exp10_1 exp10_2 exp11_0 exp11_1 exp11_2 exp12_0 exp12_1 exp12_2 "
        "exp12_3 exp13_0 exp13_1 exp13_2 exp13_3 exp14_0 exp14_1 exp14_2 exp14_3 exp15_0 exp15_1 exp15_2 exp15_3 "
        "exp16_0 "
    ).split(),
    "attention_gpsimd": (
        "hidden0 hidden1 hidden2 hidden3 hidden4 hidden5 hidden6 hidden7 hidden8 hidden9 hidden10 hidden11 hidden12 "
        "hidden13 hidden14 hidden15 "
    ).split(),
    "router_tensor": (
        "attn_T out_proj h_T0 h_T1 logits counts "
    ).split(),
    "router_vector": (
        "residual half_stats stats rstd normed gain h logits group_max group_max_pos group_prio group_prio_max "
        "group_one_hot group_prob in_group expert_logits top0 top_prio0 top_prio_max0 top_one_hot0 without_first top1 "
        "top_prio1 top_prio_max1 top_one_hot1 gap gate_sum gate_rec gate0 gate1_share gate1 group_valid one_hot0 "
        "one_hot1 one_hots one_hots_kept ranks counts rank_of0 rank0 rank_of1 rank1 "
    ).split(),
    "router_scalar": (
        "attn_T root h_T0 h_T1 group_exp gap_exp "
    ).split(),
    "experts_tensor": (
        "x_T00 x_T01 up0 down0 x_T10 x_T11 up1 down1 "
    ).split(),
    "experts_vector": (
        "silu0 hidden0 silu1 hidden1 "
    ).split(),
    "experts_scalar": (
        "x_T00 x_T01 tanh0 y0 x_T10 x_T11 tanh1 y1 "
    ).split(),
    "experts_gpsimd": (
        "idx0 idx1 "
    ).split(),
    "combine_vector": (
        "gates first second residual half_stats stats rstd normed gain y "
    ).split(),
    "combine_scalar": (
        "root "
    ).split(),
    "combine_gpsimd": (
        "idx "
    ).split(),
}


class Steps:

    def __init__(self, nc, ctx, name):
        self.sem = ctx.enter_context(nc.semaphore(name))
        self.name, self.names, self.seen = name, STEPS.get(name, ()), 0
        self.per = len(self.names)

    def mark(self, ins, name):
        assert self.names[self.seen] == name, (self.name, self.seen, name)
        self.seen += 1
        ins.then_inc(self.sem, 1)

    def done(self, turn, name):
        return self.per * (turn + 1) + self.names.index(name) + 1


class Dmas:

    def __init__(self, nc, ctx, name, n, start=0):
        self.sem = ctx.enter_context(nc.semaphore(name))
        self.n, self.start = n, start

    def go(self, ins):
        ins.then_inc(self.sem, 16)

    def done(self, turn):
        return 16 * self.n * (turn + 1 + self.start)


class Turn:

    def __init__(self, eng, own, i):
        self.eng, self.own, self.i = eng, own, i
        self.known = {}

    def ahead(self, *values):
        for counts, name, turn in values:
            v = counts.done(self.i + turn, name) if name else counts.done(self.i + turn)
            reg = self.eng.alloc_register(f"v{len(self.known)}_{counts.sem.name}")
            self.eng.reg_mov(reg, v)
            self.known[counts.sem.name, name, turn] = reg

    def _wait(self, counts, name, turn):
        v = self.known.get((counts.sem.name, name, turn))
        if v is None:
            v = counts.done(self.i + turn, name) if name else counts.done(self.i + turn)
        self.eng.wait_ge(counts.sem, v)

    def do(self, ins, name):
        self.own.mark(ins, name)
        self.eng.wait_ge(self.own.sem, self.own.done(self.i, name))

    def mark(self, ins, name):
        self.own.mark(ins, name)

    def w(self, steps, name):
        self._wait(steps, name, 0)

    def w0(self, steps, name):
        self._wait(steps, name, -1)

    def arrived(self, dmas):
        self._wait(dmas, None, 0)

    def left(self, dmas):
        self._wait(dmas, None, -1)


def engine_loop(eng, own, count, body):
    if own is not None:
        eng.sem_inc(own.sem, own.per)
    with eng.Fori(0, count) as i:
        body(Turn(eng, own, i))
    if own is not None:
        assert own.seen == own.per, (own.name, own.seen, own.per)


def bc(ap, n):
    return ap.unsqueeze(2).to_broadcast([ap.shape[0], ap.shape[1], n])


def bm(ap, n):
    return ap.unsqueeze(1).to_broadcast([ap.shape[0], n, ap.shape[1]])


def mixer(nc, io, scr):
    with ExitStack() as ctx:
        def sb(name, shape, dt=F32):
            return ctx.enter_context(nc.sbuf_tensor("mx_" + name, shape, dt))

        bank = [ctx.enter_context(nc.psum_tensor(f"mx_bank{b}", [P, 512], F32)) for b in range(8)]
        b4 = [b[:, :].rearrange("p (a n) -> p a n", a=4) for b in bank]

        w_in = sb("w_in", [P, KC, WCOL])
        w_uq = sb("w_uq", [P, CQ, 1024])
        w_wa = sb("w_wa", [P, 2, 512])
        w_g = sb("w_g", [P, 512])
        par = sb("par", [P, 64])
        ident = sb("ident", [P, P])
        cst = sb("cst", [P, 7, P])
        bones, bmean, strict, incl, low, lev0, lev0T = (cst[:, k, :] for k in range(7))
        upper2 = cst[:, 2:4, :]
        levs = sb("levs", [P, LEVELS, P])
        negh = sb("negh", [P, 8])
        rmsw = sb("rmsw", [P, 2, P])
        mu, qg, kvg = par[:, 0:14], par[:, 14:17], par[:, 17:19]
        w0c, a0c, kkc, kac, rkc, lxg, lxb = (par[:, 20 + 4 * k:24 + 4 * k] for k in range(7))

        x = sb("x", [P, D])
        rope = sb("rope", [P, 2, P])
        tile_c = sb("tile_c", [P, 2 * P + 15])
        vm, valid = tile_c[:, 0:P], tile_c[:, P:2 * P]
        keep, shift0 = tile_c[:, 2 * P:2 * P + 1], tile_c[:, 2 * P + 1:2 * P + 15]
        s_init = sb("s_init", [P, 4, VD])
        xT = sb("xT", [P, KC, P])
        pr = sb("pr", [P, NPR, P + 1])
        edge = sb("edge", [P, 2, NPR])
        u = sb("u", [P, NPR, P])
        ckv = sb("ckv", [P, CKV, P])
        msr = sb("msr", [P, 2, P])
        kpe2 = sb("kpe2", [64, P])
        kpe = sb("kpe", [32, P])
        qn = sb("qn", [P, 4, P])
        qp = sb("qp", [P, 2, P])
        ckt = sb("ckt", [P, KVL + ROPE])
        lo = sb("lo", [P, P])
        sg = sb("sg", [P, P])
        lw = sb("lw", [P, 4, P])
        cum = sb("cum", [P, 4, P + 1])
        nm = sb("nm", [P, 4])
        ep = sb("ep", [P, 4, P + 1])
        en = sb("en", [P, 4, P + 1])
        em = sb("em", [P, 4])
        aa = sb("aa", [P, 4, P])
        gg = sb("gg", [P, 4, P])
        kk = sb("kk", [P, 4, P])
        t1 = sb("t1", [P, 4, P])
        kh = sb("kh", [P, 4, P])
        AR = sb("AR", [P, 4, 2, 2, P])
        vt = sb("vt", [P, 4, P])
        RB = sb("RB", [P, H, P])
        MK = sb("MK", [P, H, 2, P])
        L = sb("L", [P, H, P])
        U = sb("U", [P, H, P])
        T = sb("T", [P, H, P])
        Z = sb("Z", [P, H, P])
        S = sb("S", [P, 4, VD])
        Sp = sb("Sp", [P, 4, VD])
        ys = sb("ys", [P, 4, P])
        bon, yq, qr, bh = aa, cum[:, :, 1:P + 1], lw[:, 0:2, :], u[:, 4:8, :]
        sq5, cq = Z[:, 0:5, :], Z[:, 5:8, :]
        bt, kt = L[:, 0:4, :], L[:, 4:8, :]
        Gs, SA = (Z[:, 4 * k:4 * k + 4, :].rearrange("p a n -> p (a n)") for k in range(2))
        ones = sb("ones", [P, P])

        ten, vec, act, pol = (Steps(nc, ctx, "mixer_" + n) for n in ("tensor", "vector", "scalar", "gpsimd"))
        consts = Dmas(nc, ctx, "mx_consts", 12)
        setup = ctx.enter_context(nc.semaphore("mx_setup"))
        biases = ctx.enter_context(nc.semaphore("mx_biases"))
        x_in = Dmas(nc, ctx, "mx_x_in", 1)
        tile_in = Dmas(nc, ctx, "mx_tile_in", 3)
        mla_out = Dmas(nc, ctx, "mx_mla_out", 10, 1)
        rwkv_out = Dmas(nc, ctx, "mx_rwkv_out", 1, 1)
        edge_out = Dmas(nc, ctx, "mx_edge_out", 1, 1)
        state_out = Dmas(nc, ctx, "mx_state_out", 1, 1)
        block = ctx.enter_context(nc.Block())

        def row(ap, i):
            return ap[bass.ds(i, 1)].rearrange("a p n -> p (a n)")

        @block.sync
        def _(sp):
            for dst, src in ((w_in, io["w_in"]), (w_uq, io["w_uq"]), (w_wa, io["w_wa"]), (levs, io["levs"]),
                             (cst, io["cst"]), (rmsw, io["rmsw"])):
                n = dst.shape[1]
                sp.dma_start(dst[:], src.rearrange("p (a n) -> p a n", a=n)).then_inc(consts.sem, 16)
            for dst, src in ((w_g, io["w_g"]), (par, io["par"]), (ident, io["ident"])):
                sp.dma_start(dst[:], src).then_inc(consts.sem, 16)
            for d in (mla_out, rwkv_out, edge_out, state_out):
                sp.sem_inc(d.sem, 16 * d.n)

            def turn(t):
                i = t.i
                t.ahead((ten, "x_transposed1", -1), (vec, "state_in", -1), (vec, "kpe_roped", 0), (vec, "ckv_normed", 0), (act, "ckv_tokens", 0),
                        (act, "q_nope", 0), (vec, "q_roped", 0), (act, "edges", 0), (vec, "state", 0),
                        (vec, "gated", 0))
                col = bass.ds(sp.snap(i * P), P)
                t.w0(ten, "x_transposed1")
                x_in.go(sp.dma_start(x[:], row(io["x"], i)))
                t.w0(vec, "state_in")
                tile_in.go(sp.dma_start(tile_c[:], row(io["tile_c"], i)))
                tile_in.go(sp.dma_start(rope[:], row(io["rope"], i).rearrange("p (a n) -> p a n", a=2)))
                tile_in.go(sp.dma_start(s_init[:], row(io["s_init"], i).rearrange("p (a n) -> p a n", a=4)))
                t.w(vec, "kpe_roped")
                mla_out.go(sp.dma_start(scr["kpeT"][:, col], kpe[:]))
                t.w(vec, "ckv_normed")
                mla_out.go(sp.dma_start(scr["ckvT"].rearrange("(c p) n -> p c n", p=P)[:, :, col], ckv[:]))
                t.w(act, "ckv_tokens")
                mla_out.go(sp.dma_start(row(io["ckv_out"], i), ckt[:, 0:KVL]))
                mla_out.go(sp.dma_start(row(io["kpe_out"], i), ckt[:, KVL:KVL + ROPE]))
                t.w(act, "q_nope")
                qd = scr["qT"]
                for h2 in range(2):
                    mla_out.go(sp.dma_start(qd.rearrange("(c b) d n -> b d c n", b=2)[h2, 0:NOPE, :, col],
                                            qn[h2 * 64:h2 * 64 + 64]))
                t.w(vec, "q_roped")
                for h4 in range(4):
                    mla_out.go(sp.dma_start(qd.rearrange("(c b) d n -> b d c n", b=4)[h4, NOPE:QK, :, col],
                                            qp[h4 * 32:h4 * 32 + 32]))
                t.w(act, "edges")
                edge_out.go(sp.dma_start(row(io["edge_out"], i), edge[:].rearrange("p a n -> p (a n)")))
                t.w(vec, "state")
                state_out.go(sp.dma_start(row(io["state_out"], i), S[:].rearrange("p a n -> p (a n)")))
                t.w(vec, "gated")
                rwkv_out.go(sp.dma_start(scr["rwT"].rearrange("(c p) n -> p c n", p=P)[:, :, col], ys[:]))

            engine_loop(sp, None, NT, turn)
            for d in (mla_out, rwkv_out, edge_out, state_out):
                sp.wait_ge(d.sem, d.done(NT - 1))

        @block.gpsimd
        def _(g):
            g.memset(AR[:], 0.0).then_inc(setup, 1)
            g.memset(cum[:], 0.0).then_inc(setup, 1)
            g.memset(pr[:], 0.0).then_inc(setup, 1)
            g.memset(S[:], 0.0).then_inc(setup, 1)
            g.memset(ones[:], 1.0).then_inc(setup, 1)
            g.wait_ge(setup, 5)
            g.wait_ge(consts.sem, 16 * 9)

            def turn(t):
                t.w(act, "exp_pos")
                t.w(vec, "u_rkv")
                t.w0(ten, "y")
                for h in range(2):
                    hs = slice(h * 64, h * 64 + 64)
                    ins = g.tensor_tensor(AR[hs, :, h, 1, :], u[hs, 0:4, :], ep[hs, :, 1:P + 1], ALU.mult)
                t.do(ins, "r_hat")
                t.w(vec, "kk_normed")
                t.do(g.tensor_tensor(t1[:], u[:, 0:4, :], kh[:], ALU.mult), "rk")
                t.do(g.tensor_tensor(t1[:], t1[:], bc(rkc, P), ALU.mult), "rkr")
                t.w(vec, "L1")
                t.w0(ten, "U6_1")
                t.do(g.tensor_tensor(T[:], L[:], bm(lev0T, H), ALU.mult), "T_level0")
                t.do(g.tensor_tensor(T[:], T[:], bm(ident[:, :], H), ALU.add), "T_start")

            engine_loop(g, pol, NT, turn)

        @block.scalar
        def _(a):
            a.wait_ge(consts.sem, 16 * 9)
            a.activation(negh[:], par[:, 20:28], ACT.Copy, scale=0.5).then_inc(biases, 1)
            a.wait_ge(biases, 1)
            a.wait_ge(setup, 5)

            def turn(t):
                for k in range(2):
                    t.w(ten, f"x_transposed{k}")
                    t.mark(a.activation(xT[:, 4 * k:4 * k + 4, :], b4[k], ACT.Copy), f"xT{k}")
                t.w(vec, "pr_edge")
                for k in range(4):
                    n = min(4, NPR - 4 * k)
                    t.w(ten, f"pr_proj{k}")
                    t.mark(a.activation(pr[:, 4 * k:4 * k + n, 1:P + 1], b4[2 + k][:, 0:n, :], ACT.Copy), f"pr{k}")
                t.w(act, "pr3")
                t.left(edge_out)
                a.activation(edge[:, 0, :], pr[:, :, DEC], ACT.Copy)
                t.mark(a.activation(edge[:, 1, :], pr[:, :, P], ACT.Copy), "edges")
                t.w(ten, "cq_proj")
                t.mark(a.activation(sq5[:, 0:3, :], b4[6][:, 0:3, :], ACT.Square), "cq_sq")
                t.w(ten, "ckv_proj")
                t.do(a.activation(sq5[:, 3:5, :], b4[7][:, 0:2, :], ACT.Square), "ckv_sq")
                t.w(ten, "rms_sums")
                t.w0(vec, "ckv_normed")
                t.mark(a.activation(msr[:], b4[7][:, 2:4, :], ACT.Sqrt, bias=par[:, 48:49]), "rms_root")
                t.w(vec, "u_low")
                t.w0(ten, "lora_a")
                t.mark(a.activation(lo[0:64, :], u[0:64, 12, :], ACT.Tanh), "w_lo")
                t.w0(ten, "lora_g")
                t.do(a.activation(sg[:], u[:, 13, :], ACT.Tanh, scale=0.5), "g_lo")
                t.w(ten, "lora_w")
                t.w0(vec, "q_roped")
                for c in range(4):
                    ins = a.activation(lw[:, c, :], b4[2][:, c, :], ACT.Tanh, bias=negh[:, c:c + 1], scale=0.5)
                t.mark(ins, "w_tanh")
                t.w(ten, "lora_a")
                t.w0(vec, "y_bonus")
                for c in range(4):
                    ins = a.activation(aa[:, c, :], b4[3][:, c, :], ACT.Tanh, bias=negh[:, 4 + c:5 + c], scale=0.5)
                t.mark(ins, "a_tanh")
                t.w(vec, "kk")
                t.w0(ten, "bonus_sum")
                t.mark(a.activation(t1[:], kk[:], ACT.Square), "kk_sq")
                t.w(vec, "kk_norm2")
                t.mark(a.activation(t1[:], t1[:], ACT.Sqrt), "kk_root")
                t.w(vec, "mid")
                t.w0(pol, "r_hat")
                for c in range(4):
                    ins = a.activation(ep[:, c, :], cum[:, c, :], ACT.Exp, bias=nm[:, c:c + 1])
                t.mark(ins, "exp_pos")
                t.w0(vec, "k_hat")
                for c in range(4):
                    ins = a.activation(en[:, c, :], cum[:, c, :], ACT.Exp, bias=cum[:, c, 64:65], scale=-1.0)
                t.do(ins, "exp_neg")
                t.w0(vec, "state_mid")
                t.mark(a.activation(em[:], en[:, :, 0], ACT.Copy), "em")
                t.w(ten, "lora_g")
                t.w0(vec, "gated")
                t.mark(a.activation(gg[:], b4[4], ACT.Copy), "g_out")
                t.w(ten, "q_nope")
                t.left(mla_out)
                t.mark(a.activation(qn[:], b4[0], ACT.Copy), "q_nope")
                t.w(ten, "ckv_tokens")
                t.mark(a.activation(ckt[:], bank[6][:, 0:KVL + ROPE], ACT.Copy), "ckv_tokens")
                t.w(ten, "v_tokens")
                t.mark(a.activation(vt[:], b4[7], ACT.Copy), "v_tokens")
                t.w(ten, "b_tokens")
                t.mark(a.activation(bt, b4[0], ACT.Copy), "b_tokens")
                t.w(ten, "k_tokens")
                t.mark(a.activation(kt, b4[1], ACT.Copy), "k_tokens")
                t.w(ten, "G")
                t.mark(a.activation(Gs, bank[2][:, :], ACT.Copy), "G")
                t.w(ten, "SA")
                t.mark(a.activation(SA, bank[3][:, :], ACT.Copy), "SA")
                t.w(ten, "y")
                t.left(rwkv_out)
                t.mark(a.activation(ys[:], b4[4], ACT.Copy), "y")
                t.w(vec, "y_centred")
                t.mark(a.activation(yq, ys[:], ACT.Square), "y_sq")
                t.w(ten, "y_var")
                t.mark(a.activation(yq, b4[3], ACT.Sqrt, bias=par[:, 49:50]), "y_root")

            engine_loop(a, act, NT, turn)

        @block.tensor
        def _(pe):
            pe.wait_ge(consts.sem, 16 * 9)
            pe.wait_ge(setup, 5)

            def proj(dst, col, n=P):
                for k in range(KC):
                    ins = pe.matmul(dst, w_in[:, k, col:col + n], xT[:, k, :], start=(k == 0), stop=(k == KC - 1))
                return ins

            def turn(t):
                t.arrived(x_in)
                t.w0(act, "b_tokens")
                for k in range(2):
                    if k == 1:
                        t.w0(act, "k_tokens")
                    for c in range(4):
                        ins = pe.transpose(b4[k][:, c, :], x[:, (4 * k + c) * P:(4 * k + c + 1) * P], ident[:, :])
                    t.mark(ins, f"x_transposed{k}")
                t.w(act, "xT1")
                t.w0(vec, "y_normed")
                for k in range(4):
                    for c in range(min(4, NPR - 4 * k)):
                        ins = proj(b4[2 + k][:, c, :], QL + KVL + (4 * k + c) * P)
                    t.mark(ins, f"pr_proj{k}")
                for c in range(CQ):
                    proj(b4[6][:, c, :], c * P)
                t.mark(proj(b4[6][0:64, 3, :], WCOL - 64, 64), "cq_proj")
                for c in range(CKV):
                    ins = proj(b4[7][:, c, :], QL + c * P)
                t.mark(ins, "ckv_proj")
                t.w(act, "ckv_sq")
                for c in range(CQ):
                    pe.matmul(b4[7][:, 2, :], rmsw[:, 0, :], sq5[:, c, :], start=(c == 0), stop=(c == CQ - 1))
                for c in range(CKV):
                    ins = pe.matmul(b4[7][:, 3, :], rmsw[:, 1, :], sq5[:, CQ + c, :], start=(c == 0), stop=(c == CKV - 1))
                t.mark(ins, "rms_sums")
                t.w(act, "g_lo")
                t.w(vec, "a_lo")
                for c in range(4):
                    ins = pe.matmul(b4[2][:, c, :], w_wa[:, 0, c * P:(c + 1) * P], lo[:], start=True, stop=True)
                t.mark(ins, "lora_w")
                for c in range(4):
                    ins = pe.matmul(b4[3][:, c, :], w_wa[:, 1, c * P:(c + 1) * P], lo[:], start=True, stop=True)
                t.mark(ins, "lora_a")
                t.w(vec, "g_sig")
                for c in range(4):
                    ins = pe.matmul(b4[4][:, c, :], w_g[:, c * P:(c + 1) * P], sg[:], start=True, stop=True)
                t.mark(ins, "lora_g")
                t.w(act, "kk_sq")
                t.mark(pe.matmul(bank[5][:, :], bones, t1[:].rearrange("p a n -> p (a n)"), start=True, stop=True),
                       "kk_norm")
                t.w(vec, "cq_normed")
                for c in range(4):
                    for k in range(CQ):
                        ins = pe.matmul(b4[0][:, c, :], w_uq[:, k, c * P:(c + 1) * P], cq[:, k, :],
                                        start=(k == 0), stop=(k == CQ - 1))
                t.mark(ins, "q_nope")
                for c in range(4):
                    for k in range(CQ):
                        ins = pe.matmul(b4[1][:, c, :], w_uq[:, k, 512 + c * P:512 + (c + 1) * P], cq[:, k, :],
                                        start=(k == 0), stop=(k == CQ - 1))
                t.mark(ins, "q_pe")
                t.w(vec, "kpe_roped")
                for c in range(CKV):
                    pe.transpose(bank[6][:, c * P:(c + 1) * P], ckv[:, c, :], ident[:, :])
                t.mark(pe.transpose(bank[6][:, KVL:KVL + ROPE], kpe[:], ident[0:32, 0:32]), "ckv_tokens")
                for c in range(4):
                    ins = pe.transpose(b4[7][:, c, :], u[:, 8 + c, :], ident[:, :])
                t.mark(ins, "v_tokens")
                t.w(pol, "rkr")
                t.w(act, "ckv_tokens")
                t.mark(pe.matmul(bank[6][:, :], bones, t1[:].rearrange("p a n -> p (a n)"), start=True, stop=True),
                       "bonus_sum")
                t.w(vec, "b_hat")
                t.w(pol, "r_hat")
                t.w(act, "g_out")
                for q in range(4):
                    for h in range(2):
                        ins = pe.matmul(bank[2 + q][:, h * 256:(h + 1) * 256], bh[:, q, :],
                                        AR[:, q, h].rearrange("p a n -> p (a n)"), start=True, stop=True)
                    t.mark(ins, f"gram_b{q}")
                t.w(vec, "bonus")
                t.w(act, "v_tokens")
                for q in range(4):
                    b = (6, 7, 0, 1)[q]
                    for h in range(2):
                        ins = pe.matmul(bank[b][:, h * 256:(h + 1) * 256], kh[:, q, :],
                                        AR[:, q, h].rearrange("p a n -> p (a n)"), start=True, stop=True)
                    t.mark(ins, f"gram_k{q}")
                for g in range(2):
                    t.w(vec, f"RB{g}")
                    for h in range(4):
                        hh = 4 * g + h
                        ins = pe.matmul(b4[2 + g][:, h, :], AR[:, hh // 2, hh % 2, 0, :], bh[:, hh // 2, :],
                                        start=True, stop=True)
                    t.mark(ins, f"gram_l{g}")
                t.w(pol, "T_start")
                for lev in range(1, LEVELS + 1):
                    for g in range(2):
                        t.w(vec, f"U{lev - 1}_{g}" if lev > 1 else "U0")
                        for h in range(4 * g, 4 * g + 4):
                            ins = pe.matmul(b4[4 + g][:, h % 4, :], L[:, h, :], U[:, h, :], start=True, stop=True)
                        t.mark(ins, f"Z{lev}_{g}")
                    for g in range(2):
                        t.w(vec, f"Z{lev}_{g}")
                        for h in range(4 * g, 4 * g + 4):
                            ins = pe.matmul(b4[6 + g][:, h % 4, :], T[:, h, :], Z[:, h, :], start=True, stop=True)
                        t.mark(ins, f"U{lev}_{g}")
                        if lev < LEVELS:
                            for h in range(4 * g, 4 * g + 4):
                                ins = pe.matmul(b4[g][:, h % 4, :], Z[:, h, :], T[:, h, :], start=True, stop=True)
                            t.mark(ins, f"T{lev}_{g}")
                for c in range(4):
                    ins = pe.transpose(b4[0][:, c, :], bh[:, c, :], ident[:, :])
                t.mark(ins, "b_tokens")
                t.w(vec, "T5_1")
                for c in range(4):
                    ins = pe.transpose(b4[1][:, c, :], kh[:, c, :], ident[:, :])
                t.mark(ins, "k_tokens")
                for h in range(H):
                    q, hs = h // 2, slice(h % 2 * 64, h % 2 * 64 + 64)
                    o = bank[2][:, h * 64:h * 64 + 64]
                    pe.matmul(o, AR[:, q, h % 2, 0, :], Sp[:, q, :], start=True, stop=False)
                    ins = pe.matmul(o, MK[:, h, 0, :], vt[:, q, hs], start=False, stop=True)
                t.mark(ins, "G")
                t.w(act, "G")
                t.w(vec, f"U{LEVELS}_1")
                for h in range(H):
                    ins = pe.matmul(bank[3][:, h * 64:h * 64 + 64], U[:, h, :], Gs[:, h * 64:h * 64 + 64],
                                    start=True, stop=True)
                t.mark(ins, "SA")
                t.w(act, "SA")
                for h in range(H):
                    q, hs = h // 2, slice(h % 2 * 64, h % 2 * 64 + 64)
                    o = b4[4][hs, q, :]
                    pe.matmul(o, Sp[:, q, :], AR[:, q, h % 2, 1, :], start=True, stop=False)
                    pe.matmul(o, SA[:, h * 64:h * 64 + 64], RB[:, h, :], start=False, stop=False)
                    ins = pe.matmul(o, vt[:, q, hs], MK[:, h, 1, :], start=False, stop=True)
                t.mark(ins, "y")
                t.w(act, "k_tokens")
                for h in range(H):
                    q, hs = h // 2, slice(h % 2 * 64, h % 2 * 64 + 64)
                    o = bank[5][hs, q * 64:q * 64 + 64]
                    pe.matmul(o, bt[:, q, hs], SA[:, h * 64:h * 64 + 64], start=True, stop=False)
                    ins = pe.matmul(o, kt[:, q, hs], vt[:, q, hs], start=False, stop=True)
                t.mark(ins, "state_add")
                t.w(act, "y")
                t.mark(pe.matmul(bank[2][:, :], bmean, ys[:].rearrange("p a n -> p (a n)"), start=True, stop=True),
                       "y_mean")
                t.w(act, "y_sq")
                t.mark(pe.matmul(b4[3], bmean, yq, start=True, stop=True),
                       "y_var")

            engine_loop(pe, ten, NT, turn)

        @block.vector
        def _(v):
            v.wait_ge(consts.sem, 16 * 9)
            v.wait_ge(setup, 5)

            def turn(t):
                do = t.do
                t.arrived(tile_in)
                t.w0(act, "edges")
                do(v.scalar_tensor_tensor(out=pr[:, :, 0], in0=pr[:, :, P], scalar=keep, in1=shift0,
                                          op0=ALU.mult, op1=ALU.add), "pr_edge")
                t.w(act, "pr3")
                t.w0(ten, "b_tokens")
                t.w0(pol, "rk")
                for name, c0, c1 in (("low", 12, 14), ("rkv", 0, 12)):
                    do(v.tensor_tensor(u[:, c0:c1, :], pr[:, c0:c1, 0:P], pr[:, c0:c1, 1:P + 1], ALU.subtract), "u_diff_" + name)
                    do(v.tensor_tensor(u[:, c0:c1, :], u[:, c0:c1, :], bc(mu[:, c0:c1], P), ALU.mult), "u_mu_" + name)
                    do(v.tensor_tensor(u[:, c0:c1, :], u[:, c0:c1, :], pr[:, c0:c1, 1:P + 1], ALU.add), "u_" + name)
                    if name == "low":
                        t.w0(ten, "lora_a")
                        t.mark(v.tensor_copy(lo[64:128, :], u[64:128, 12, :]), "a_lo")
                        t.w(act, "g_lo")
                        t.mark(v.tensor_scalar(sg[:], sg[:], 0.5, 0.5, ALU.mult, ALU.add), "g_sig")
                t.w0(act, "kk_sq")
                do(v.tensor_tensor(kk[:], u[:, 4:8, :], bc(kkc, P), ALU.mult), "kk")
                t.w(act, "rms_root")
                do(v.reciprocal(msr[:], msr[:]), "rms")
                for c in range(CQ):
                    ins = v.scalar_tensor_tensor(out=cq[:, c, :], in0=b4[6][:, c, :], scalar=qg[:, c:c + 1],
                                                 in1=msr[:, 0, :], op0=ALU.mult, op1=ALU.mult)
                do(ins, "cq_normed")
                t.left(mla_out)
                for c in range(CKV):
                    ins = v.scalar_tensor_tensor(out=ckv[:, c, :], in0=b4[7][:, c, :], scalar=kvg[:, c:c + 1],
                                                 in1=msr[:, 1, :], op0=ALU.mult, op1=ALU.mult)
                do(ins, "ckv_normed")
                do(v.tensor_tensor(kpe2[0:32, :], b4[6][0:32, 3, :], rope[0:32, 0, :], ALU.mult), "kpe_cos")
                do(v.tensor_tensor(kpe[:], b4[6][32:64, 3, :], rope[32:64, 1, :], ALU.mult), "kpe_sin")
                do(v.tensor_tensor(kpe[:], kpe[:], kpe2[0:32, :], ALU.add), "kpe_roped")
                t.w(act, "w_tanh")
                do(v.scalar_tensor_tensor(out=lw[:], in0=lw[:], scalar=1.0, in1=bm(vm, 4), op0=ALU.add, op1=ALU.mult),
                   "log_w")
                t.w0(act, "exp_neg")
                for c in range(4):
                    ins = v.tensor_tensor_scan(cum[:, c, 1:P + 1], ones[:], lw[:, c, :], 0.0, ALU.mult, ALU.add)
                do(ins, "cum")
                do(v.tensor_scalar(nm[:], cum[:, :, 64], -1.0, None, ALU.mult), "mid")
                t.w(act, "a_tanh")
                do(v.tensor_scalar(aa[:], aa[:], 0.5, 0.5, ALU.mult, ALU.add), "a_sig")
                t.w0(ten, "k_tokens")
                t.w0(pol, "rk")
                do(v.scalar_tensor_tensor(out=kh[:], in0=aa[:], scalar=-1.0, in1=bc(kac, P), op0=ALU.add, op1=ALU.mult),
                   "a_ka")
                do(v.scalar_tensor_tensor(out=kh[:], in0=kh[:], scalar=1.0, in1=u[:, 4:8, :], op0=ALU.add, op1=ALU.mult),
                   "kh")
                t.w(ten, "kk_norm")
                do(v.tensor_scalar(t1[:], b4[5], 1e-24, None, ALU.max), "kk_norm2")
                t.w(act, "kk_root")
                do(v.reciprocal(t1[:], t1[:]), "kk_rs")
                do(v.tensor_tensor(kk[:], kk[:], t1[:], ALU.mult), "kk_normed")
                t.w(act, "em")
                t.w0(ten, "y")
                for h in range(2):
                    hs = slice(h * 64, h * 64 + 64)
                    ins = v.scalar_tensor_tensor(out=AR[hs, :, h, 0, :], in0=kk[hs], scalar=-1.0, in1=ep[hs, :, 0:P],
                                                 op0=ALU.mult, op1=ALU.mult)
                do(ins, "a_hat")
                do(v.tensor_tensor(en[:, :, 1:P + 1], en[:, :, 1:P + 1], bm(valid, 4), ALU.mult), "en_masked")
                do(v.tensor_tensor(bh, kk[:], aa[:], ALU.mult), "b_gate")
                do(v.tensor_tensor(bh, bh, en[:, :, 1:P + 1], ALU.mult), "b_hat")
                t.w(pol, "rk")
                do(v.tensor_tensor(kh[:], kh[:], en[:, :, 1:P + 1], ALU.mult), "k_hat")
                t.w(ten, "q_pe")
                do(v.tensor_tensor(qp[:], b4[1][:, 0:2, :], bm(rope[:, 0, :], 2), ALU.mult), "q_rope_cos")
                do(v.tensor_tensor(qr, b4[1][:, 2:4, :], bm(rope[:, 1, :], 2), ALU.mult), "q_rope_sin")
                do(v.tensor_tensor(qp[:], qp[:], qr, ALU.add), "q_roped")
                t.w(ten, "bonus_sum")
                do(v.tensor_tensor(bon[:], b4[6], u[:, 8:12, :], ALU.mult), "bonus")
                t.left(state_out)
                do(v.scalar_tensor_tensor(out=S[:], in0=S[:], scalar=keep, in1=s_init[:], op0=ALU.mult, op1=ALU.add),
                   "state_in")
                t.w0(ten, "y")
                do(v.tensor_tensor(Sp[:], S[:], bc(em[:], VD), ALU.mult), "state_mid")
                for q in range(4):
                    t.w(ten, f"gram_b{q}")
                    two = slice(2 * q, 2 * q + 2)
                    g4 = bank[2 + q][:, :].rearrange("p (h a n) -> p h a n", h=2, a=2)
                    v.tensor_tensor(U[:, two, :], g4[:, :, 0, :], bm(lev0, 2), ALU.mult)
                    t.mark(v.tensor_tensor(RB[:, two, :], g4[:, :, 1, :], bm(incl, 2), ALU.mult), f"RB{q}")
                for q in range(4):
                    t.w(ten, f"gram_k{q}")
                    g4 = bank[(6, 7, 0, 1)[q]][:, :].rearrange("p (h a n) -> p h a n", h=2, a=2)
                    t.mark(v.tensor_tensor(MK[:, 2 * q:2 * q + 2], g4, upper2.unsqueeze(1).to_broadcast([P, 2, 2, P]),
                                           ALU.mult), f"MK{q}")
                for g in range(2):
                    t.w(ten, f"gram_l{g}")
                    t.mark(v.tensor_tensor(L[:, 4 * g:4 * g + 4, :], b4[2 + g], bm(low, 4), ALU.mult), f"L{g}")
                t.w(vec, "RB3")
                t.mark(v.tensor_tensor(U[:], U[:], bm(ident[:, :], H), ALU.add), "U0")
                for lev in range(1, LEVELS + 1):
                    for g in range(2):
                        hs = slice(4 * g, 4 * g + 4)
                        t.w(ten, f"Z{lev}_{g}")
                        t.mark(v.tensor_tensor(Z[:, hs, :], b4[4 + g], bm(levs[:, lev - 1, :], 4), ALU.mult), f"Z{lev}_{g}")
                    for g in range(2):
                        hs = slice(4 * g, 4 * g + 4)
                        t.w(ten, f"U{lev}_{g}")
                        t.mark(v.tensor_tensor(U[:, hs, :], b4[6 + g], U[:, hs, :], ALU.add), f"U{lev}_{g}")
                        if lev < LEVELS:
                            t.w(ten, f"T{lev}_{g}")
                            t.mark(v.tensor_tensor(T[:, hs, :], b4[g], T[:, hs, :], ALU.add), f"T{lev}_{g}")
                t.w(ten, "state_add")
                do(v.tensor_tensor(S[:], bank[5][:, 0:256].rearrange("p (a n) -> p a n", a=4), Sp[:], ALU.add),
                   "state_sum")
                do(v.tensor_tensor(S[:], S[:], ep[:, :, P:P + 1].to_broadcast([P, 4, VD]), ALU.mult), "state")
                t.w(ten, "y_mean")
                do(v.tensor_tensor(ys[:], ys[:], b4[2], ALU.subtract), "y_centred")
                t.w(act, "y_root")
                do(v.reciprocal(yq, yq), "y_rs")
                do(v.tensor_tensor(ys[:], ys[:], yq, ALU.mult), "y_normed")
                do(v.tensor_tensor(ys[:], ys[:], bc(lxg, P), ALU.mult), "y_gain")
                do(v.tensor_tensor(ys[:], ys[:], bc(lxb, P), ALU.add), "y_bias")
                do(v.tensor_tensor(ys[:], ys[:], bon[:], ALU.add), "y_bonus")
                do(v.tensor_tensor(ys[:], ys[:], gg[:], ALU.mult), "gated")

            engine_loop(v, vec, NT, turn)


def attention(nc, io, scr):
    KT = SEQ // P + 2
    with ExitStack() as ctx:
        def sb(name, shape, dt=F32):
            return ctx.enter_context(nc.sbuf_tensor("at_" + name, shape, dt))

        bank = [ctx.enter_context(nc.psum_tensor(f"at_bank{b}", [P, 512], F32)) for b in range(8)]
        ident = sb("ident", [P, P])
        lat = sb("lat", [P, CKV, KT * P])
        kT = sb("kT", [P, KT * P])
        qT = sb("qT", [P, TOK])
        w = sb("w", [P, CKV, P])
        vals = sb("vals", [P, KT, VD + 1])
        mx = sb("mx", [P, 5])
        nm = sb("nm", [P, NT])
        rec = sb("rec", [P, 1])
        zero = sb("zero", [P, 64])
        NPT = 3
        PT = sb("PT", [P, NPT, 4, P])
        o_sb = sb("o_sb", [P, NT, VD])

        ten, vec, act, pol = (Steps(nc, ctx, "attention_" + n) for n in ("tensor", "vector", "scalar", "gpsimd"))
        latents = Dmas(nc, ctx, "at_latents", 7)
        setup = ctx.enter_context(nc.semaphore("at_setup"))
        w_in = Dmas(nc, ctx, "at_w_in", 1)
        q_in = Dmas(nc, ctx, "at_q_in", 1)
        o_out = Dmas(nc, ctx, "at_o_out", 1, 1)
        block = ctx.enter_context(nc.Block())

        def groups(j):
            if j == NT - 1:
                return [(KT - 2, 2, DEC)]
            return [(k, min(4, j + 1 - k), P) for k in range(0, j + 1, 4)]

        chunks = [(j, g) for j in range(NT) for g in range(len(groups(j)))]
        order = {c: n for n, c in enumerate(chunks)}

        @block.sync
        def _(sp):
            n = SEQ
            lt = scr["ckvT"].rearrange("(c p) n -> p c n", p=P)
            sp.dma_start(lat[:, :, 0:n], lt[:, :, 0:n]).then_inc(latents.sem, 16)
            sp.dma_start(lat[:, :, n:n + P], io["past_ckvT"].rearrange("p (c n) -> p c n", c=CKV)).then_inc(latents.sem, 16)
            sp.dma_start(lat[:, :, n + P:n + 2 * P], lt[:, :, n:n + P]).then_inc(latents.sem, 16)
            sp.dma_start(kT[NOPE:QK, 0:n], scr["kpeT"][:, 0:n]).then_inc(latents.sem, 16)
            sp.dma_start(kT[NOPE:QK, n:n + P], io["past_kpeT"]).then_inc(latents.sem, 16)
            sp.dma_start(kT[NOPE:QK, n + P:n + 2 * P], scr["kpeT"][:, n:n + P]).then_inc(latents.sem, 16)
            sp.dma_start(ident[:], io["ident"]).then_inc(latents.sem, 16)
            sp.sem_inc(o_out.sem, 16)

            def turn(t):
                t.ahead((ten, "V2", -1), (vec, "out_16", 0), (ten, "ST16_0", -1))
                hs = bass.ds(sp.snap(t.i * VD), VD)
                t.w0(ten, "V2")
                w_in.go(sp.dma_start(w[:], io["w_ukv"][bass.ds(t.i, 1)].rearrange("a p (c n) -> p (a c) n", c=CKV)))
                t.w0(ten, "ST16_0")
                q_in.go(sp.dma_start(qT[0:QK, :], scr["qT"][bass.ds(t.i, 1)].rearrange("a d n -> d (a n)")))
                t.w(vec, "out_16")
                o_out.go(sp.dma_start(scr["attn"].rearrange("(t p) c -> p t c", p=P)[:, :, hs], o_sb[:]))

            engine_loop(sp, None, H, turn)
            sp.wait_ge(o_out.sem, o_out.done(H - 1))

        @block.gpsimd
        def _(g):
            g.memset(kT[QK:QK + 1, :], 1.0).then_inc(setup, 1)
            g.wait_ge(setup, 1)
            g.memset(vals[:], 1.0).then_inc(setup, 1)
            g.memset(mx[:], -3e38).then_inc(setup, 1)
            g.memset(zero[:], 0.0).then_inc(setup, 1)
            g.wait_ge(setup, 4)

            def turn(t):
                for j in range(NT - 1):
                    gi = len(groups(j)) - 1
                    t.w(act, f"exp{j}_{gi}")
                    k0, k, _ = groups(j)[gi]
                    s = order[j, gi] % NPT
                    t.mark(g.tensor_tensor(PT[64:P, s, k - 1, 0:64], zero[64:P, :], zero[64:P, :], ALU.add), f"hidden{j}")

            engine_loop(g, pol, H, turn)

        @block.scalar
        def _(a):
            a.wait_ge(setup, 4)

            def turn(t):
                for n in range(5):
                    t.w(ten, f"K{n}")
                    wd = min(512, KT * P - 512 * n)
                    t.mark(a.activation(kT[0:NOPE, 512 * n:512 * n + wd], bank[n][0:NOPE, 0:wd], ACT.Copy), f"K{n}")
                for j, gi in chunks:
                    k0, k, last = groups(j)[gi]
                    n = order[j, gi]
                    t.w(ten, f"ST{j}_{gi}")
                    b = bank[3 + n % 3]
                    if last == P:
                        ins = a.activation(PT[:, n % NPT, 0:k, :], b[:, 0:k * P].rearrange("p (a n) -> p a n", a=k),
                                           ACT.Exp, scale=SCALE)
                    else:
                        a.activation(PT[:, n % NPT, 0, :], b[:, 0:P], ACT.Exp, scale=SCALE)
                        ins = a.activation(PT[0:last, n % NPT, 1, :], b[0:last, P:2 * P], ACT.Exp, scale=SCALE)
                    t.mark(ins, f"exp{j}_{gi}")

            engine_loop(a, act, H, turn)

        @block.tensor
        def _(pe):
            pe.wait_ge(latents.sem, latents.done(0))
            pe.wait_ge(setup, 4)

            def scores(t, j):
                for gi, (k0, k, last) in enumerate(groups(j)):
                    n = order[j, gi]
                    if n >= 3:
                        pj, pg = chunks[n - 3]
                        t.w(vec, f"max{pj}_{pg}")
                    wd = (k - 1) * P + last
                    t.mark(pe.matmul(bank[n % 3][:, 0:wd], qT[0:QK, j * P:(j + 1) * P], kT[0:QK, k0 * P:k0 * P + wd],
                                     start=True, stop=True), f"S{j}_{gi}")

            def turn(t):
                t.arrived(w_in)
                t.w0(vec, "out_16")
                t.w0(act, "exp16_0")
                for n in range(5):
                    wd = min(512, KT * P - 512 * n)
                    for c in range(CKV):
                        ins = pe.matmul(bank[n][0:NOPE, 0:wd], w[:, c, 0:NOPE], lat[:, c, 512 * n:512 * n + wd],
                                        start=(c == 0), stop=(c == CKV - 1))
                    t.mark(ins, f"K{n}")
                for n in range(3):
                    b = bank[5 + n]
                    for k in range(8 * n, min(8 * n + 8, KT)):
                        for c in range(CKV):
                            ins = pe.matmul(b[:, (k % 8) * VD:(k % 8 + 1) * VD], lat[:, c, k * P:(k + 1) * P],
                                            w[:, c, NOPE:P], start=(c == 0), stop=(c == CKV - 1))
                    t.mark(ins, f"V{n}")
                t.w(act, "K4")
                t.w(vec, "V2")
                t.arrived(q_in)
                scores(t, 0)
                scores(t, 1)
                for j in range(NT):
                    gs = groups(j)
                    t.w(vec, f"negmax{j}")
                    t.mark(pe.matmul(bank[7][QK:QK + 1, 0:P], nm[:, j:j + 1], ident[:, :], start=True, stop=True), f"maxrow{j}")
                    if j + 2 < NT:
                        scores(t, j + 2)
                    t.w(vec, f"maxrow{j}")

                    def pv(gi):
                        k0, k, last = gs[gi]
                        n = order[j, gi]
                        if gi == 0 and j >= 2:
                            t.w(vec, f"out_{j - 2}")
                        t.w(act, f"exp{j}_{gi}")
                        if last == P and gi == len(gs) - 1:
                            t.w(pol, f"hidden{j}")
                        for s in range(k):
                            rows = last if s == k - 1 else P
                            ins = pe.matmul(bank[6][:, 256 * (j % 2):256 * (j % 2) + VD + 1], PT[0:rows, n % NPT, s, :],
                                            vals[0:rows, k0 + s, :], start=(gi == 0 and s == 0),
                                            stop=(gi == len(gs) - 1 and s == k - 1))
                        t.mark(ins, f"PV{j}_{gi}")

                    for gi, (k0, k, last) in enumerate(gs):
                        n = order[j, gi]
                        if n >= 3:
                            pj, pg = chunks[n - 3]
                            t.w(act, f"exp{pj}_{pg}")
                        for s in range(k):
                            rows = last if s == k - 1 else P
                            c0 = (k0 + s) * P
                            ins = pe.matmul(bank[3 + n % 3][0:rows, s * P:(s + 1) * P], kT[0:QK + 1, c0:c0 + rows],
                                            qT[0:QK + 1, j * P:(j + 1) * P], start=True, stop=True)
                        t.mark(ins, f"ST{j}_{gi}")
                        if gi >= 1:
                            pv(gi - 1)
                    pv(len(gs) - 1)

            engine_loop(pe, ten, H, turn)

        @block.vector
        def _(v):
            v.wait_ge(setup, 4)

            def maxima(t, j):
                gs = groups(j)
                for gi, (k0, k, last) in enumerate(gs):
                    n = order[j, gi]
                    t.w(ten, f"S{j}_{gi}")
                    b = bank[n % 3]
                    wd = (k - 1) * P + last
                    if gi == len(gs) - 1 and j < NT - 1:
                        v.tensor_reduce(mx[64:P, 0:1], b[64:P, wd - 64:wd], AX.X, ALU.max)
                        wd -= 64
                    elif gi == 0 and j == NT - 1:
                        v.tensor_reduce(mx[64:P, 0:1], b[64:P, 0:64], AX.X, ALU.max)
                    t.mark(v.tensor_reduce(mx[:, 1 + gi:2 + gi], b[:, 0:wd], AX.X, ALU.max), f"max{j}_{gi}")
                t.w(vec, f"max{j}_{len(gs) - 1}")
                t.do(v.tensor_reduce(nm[:, j:j + 1], mx[:, 0:1 + len(gs)], AX.X, ALU.max, negate=True), f"negmax{j}")

            def turn(t):
                for n in range(3):
                    t.w(ten, f"V{n}")
                    k = min(8, KT - 8 * n)
                    t.mark(v.tensor_copy(vals[:, 8 * n:8 * n + k, 0:VD],
                                         bank[5 + n][:, 0:k * VD].rearrange("p (a n) -> p a n", a=k)), f"V{n}")
                maxima(t, 0)
                maxima(t, 1)
                for j in range(NT):
                    t.w(ten, f"maxrow{j}")
                    t.mark(v.tensor_copy(qT[QK:QK + 1, j * P:(j + 1) * P], bank[7][QK:QK + 1, 0:P]), f"maxrow{j}")
                    if j + 2 < NT:
                        maxima(t, j + 2)
                    t.w(ten, f"PV{j}_{len(groups(j)) - 1}")
                    if j == 0:
                        t.left(o_out)
                    o = bank[6][:, 256 * (j % 2):256 * (j % 2) + VD + 1]
                    t.do(v.reciprocal(rec[:], o[:, VD:VD + 1]), f"sum_{j}")
                    t.mark(v.tensor_scalar(o_sb[:, j, :], o[:, 0:VD], rec[:, 0:1], None, ALU.mult), f"out_{j}")

            engine_loop(v, vec, H, turn)


def router(nc, io, scr, keep):
    oh, rank, gate, base = keep["onehot"], keep["rank"], keep["gate"], keep["counts"]
    with ExitStack() as ctx:
        def sb(name, shape, dt=F32):
            return ctx.enter_context(nc.sbuf_tensor("ro_" + name, shape, dt))

        bank = [ctx.enter_context(nc.psum_tensor(f"ro_bank{b}", [P, 512], F32)) for b in range(8)]
        b4 = [b[:, :].rearrange("p (a n) -> p a n", a=4) for b in bank]
        w_o = sb("w_o", [P, KC, D])
        w_r = sb("w_r", [P, KC, NR])
        rows = sb("rows", [P, 2, D])
        small = sb("small", [P, NR + NG + EPG])
        bias, prio4, prio8 = small[:, 0:NR], small[:, NR:NR + NG], small[:, NR + NG:]
        cst = sb("cst", [P, 3, P])
        ident = cst[:, 0, :]
        eps = sb("eps", [P, 1])
        vcol = sb("vcol", [P, NT])
        at = sb("at", [P, 512])
        mix = sb("mix", [P, KC, P])
        x = sb("x", [P, D])
        r = sb("r", [P, D])
        h = sb("h", [P, D])
        hT = sb("hT", [P, KC, P])
        st = sb("st", [P, 2, 6])
        mv = sb("mv", [P, 2])
        rstd = sb("rstd", [P, 1])
        lg = sb("lg", [P, NR])
        t36 = sb("t36", [P, NR])
        s1 = sb("s1", [P, 16])
        ohg = sb("ohg", [P, NG])
        ein = sb("ein", [P, EPG])
        e2 = sb("e2", [P, EPG])
        pr8 = sb("pr8", [P, EPG])
        o1 = sb("o1", [P, EPG])
        o2 = sb("o2", [P, EPG])
        ohs = sb("ohs", [P, 3, NE])
        ranks = sb("ranks", [P, NE])

        ten, vec, act = (Steps(nc, ctx, "router_" + n) for n in ("tensor", "vector", "scalar"))
        consts = Dmas(nc, ctx, "ro_consts", 7)
        zeroed = ctx.enter_context(nc.semaphore("ro_zeroed"))
        mix_in = Dmas(nc, ctx, "ro_mix_in", 2)
        x_in = Dmas(nc, ctx, "ro_x_in", 1)
        h_out = Dmas(nc, ctx, "ro_h_out", 1, 1)
        block = ctx.enter_context(nc.Block())

        @block.sync
        def _(sp):
            for dst, src, n in ((w_o, io["w_o"], KC), (w_r, io["w_r"], KC), (cst, io["cst3"], 3)):
                sp.dma_start(dst[:], src.rearrange("p (a n) -> p a n", a=n)).then_inc(consts.sem, 16)
            sp.dma_start(rows[:], io["ln1"].rearrange("(o a) n -> o a n", o=1).to_broadcast([P, 2, D])).then_inc(consts.sem, 16)
            sp.dma_start(small[:], io["small"].to_broadcast([P, NR + NG + EPG])).then_inc(consts.sem, 16)
            sp.dma_start(eps[:], io["eps"]).then_inc(consts.sem, 16)
            sp.dma_start(vcol[:], io["vcol"]).then_inc(consts.sem, 16)
            sp.sem_inc(h_out.sem, 16)

            def turn(t):
                t.ahead((ten, "attn_T", -1), (ten, "out_proj", -1), (vec, "residual", -1), (vec, "h", 0))
                col = bass.ds(sp.snap(t.i * P), P)
                one = bass.ds(sp.snap(t.i), 1)
                t.w0(ten, "out_proj")
                mix_in.go(sp.dma_start(at[:], scr["attn"][col, :]))
                mix_in.go(sp.dma_start(mix[:, 4:8, :], scr["rwT"].rearrange("(c p) n -> p c n", p=P)[:, :, col]))
                t.w0(vec, "residual")
                x_in.go(sp.dma_start(x[:], io["x"][one].rearrange("a p n -> p (a n)")))
                t.w(vec, "h")
                h_out.go(sp.dma_start(scr["h"][col, :], h[:]))

            engine_loop(sp, None, NT, turn)
            sp.wait_ge(h_out.sem, h_out.done(NT - 1))

        @block.scalar
        def _(a):
            a.wait_ge(consts.sem, consts.done(0))

            def turn(t):
                t.w(ten, "attn_T")
                t.mark(a.activation(mix[:, 0:4, :], b4[0], ACT.Copy), "attn_T")
                t.w(vec, "stats")
                t.mark(a.activation(rstd[:], mv[:, 1:2], ACT.Sqrt, bias=eps[:, 0:1]), "root")
                for k in range(2):
                    t.w(ten, f"h_T{k}")
                    t.mark(a.activation(hT[:, 4 * k:4 * k + 4, :], b4[3 + k], ACT.Copy), f"h_T{k}")
                t.w(vec, "group_max")
                t.mark(a.activation(t36[:, 0:NG], lg[:, 0:NG], ACT.Exp, bias=s1[:, 0:1], accum_out=s1[:, 1:2]), "group_exp")
                t.w(vec, "gap")
                t.mark(a.activation(s1[:, 8:9], s1[:, 7:8], ACT.Exp), "gap_exp")

            engine_loop(a, act, NT, turn)

        @block.tensor
        def _(pe):
            pe.wait_ge(consts.sem, consts.done(0))

            def turn(t):
                t.arrived(mix_in)
                for c in range(4):
                    ins = pe.transpose(b4[0][:, c, :], at[:, c * P:(c + 1) * P], ident)
                t.mark(ins, "attn_T")
                t.w(act, "attn_T")
                t.w0(vec, "residual")
                for n in range(2):
                    for k in (4, 5, 6, 7, 0, 1, 2, 3):
                        ins = pe.matmul(bank[1 + n][:, :], mix[:, k, :], w_o[:, k, n * 512:(n + 1) * 512],
                                        start=(k == 4), stop=(k == 3))
                t.mark(ins, "out_proj")
                t.w(vec, "h")
                for k in range(2):
                    for c in range(4):
                        ins = pe.transpose(b4[3 + k][:, c, :], h[:, (4 * k + c) * P:(4 * k + c + 1) * P], ident)
                    t.mark(ins, f"h_T{k}")
                t.w(act, "h_T1")
                for k in range(KC):
                    ins = pe.matmul(bank[5][:, 0:NR], hT[:, k, :], w_r[:, k, :], start=(k == 0), stop=(k == KC - 1))
                t.mark(ins, "logits")
                t.w(vec, "one_hots")
                pe.matmul(bank[6][:, 0:NE], cst[:, 1, :], ohs[:, 2, :], start=True, stop=True)
                t.mark(pe.matmul(bank[6][:, NE:2 * NE], cst[:, 2, :], ohs[:, 2, :], start=True, stop=True), "counts")

            engine_loop(pe, ten, NT, turn)

        @block.vector
        def _(v):
            v.wait_ge(consts.sem, consts.done(0))
            v.memset(base[:], 0.0).then_inc(zeroed, 1)
            v.wait_ge(zeroed, 1)

            def turn(t):
                do = t.do
                t.w(ten, "out_proj")
                t.arrived(x_in)
                for n in range(2):
                    s = slice(n * 512, n * 512 + 512)
                    ins = v.scalar_tensor_tensor(out=r[:, s], in0=x[:, s], scalar=ALPHA, in1=bank[1 + n][:, :],
                                                 op0=ALU.mult, op1=ALU.add)
                do(ins, "residual")
                for n in range(2):
                    ins = v.bn_stats(st[:, n, :], r[:, n * 512:n * 512 + 512])
                do(ins, "half_stats")
                v.tensor_copy(rstd[:], st[:, 0, 0:1])
                do(v.bn_aggr(mv[:], st[:]), "stats")
                t.w(act, "root")
                do(v.reciprocal(rstd[:], rstd[:]), "rstd")
                t.left(h_out)
                t.w0(ten, "h_T1")
                do(v.tensor_scalar(r[:], r[:], mv[:, 0:1], rstd[:, 0:1], ALU.subtract, ALU.mult), "normed")
                do(v.tensor_tensor(r[:], r[:], rows[:, 0, :], ALU.mult), "gain")
                do(v.tensor_tensor(h[:], r[:], rows[:, 1, :], ALU.add), "h")
                t.w(ten, "logits")
                do(v.tensor_tensor(lg[:], bank[5][:, 0:NR], bias, ALU.add), "logits")
                do(v.tensor_reduce(s1[:, 0:1], lg[:, 0:NG], AX.X, ALU.max, negate=True), "group_max")
                do(v.tensor_reduce(s1[:, 2:3], lg[:, 0:NG], AX.X, ALU.max), "group_max_pos")
                do(v.scalar_tensor_tensor(out=ohg[:], in0=lg[:, 0:NG], scalar=s1[:, 2:3], in1=prio4,
                                          op0=ALU.is_equal, op1=ALU.mult), "group_prio")
                do(v.tensor_reduce(s1[:, 3:4], ohg[:], AX.X, ALU.max), "group_prio_max")
                do(v.tensor_scalar(ohg[:], ohg[:], s1[:, 3:4], None, ALU.is_equal), "group_one_hot")
                t.w(act, "group_exp")
                do(v.reciprocal(s1[:, 1:2], s1[:, 1:2]), "group_prob")
                g8 = t36[:, NG:NR].rearrange("p (g e) -> p g e", g=NG)
                do(v.tensor_tensor(g8, lg[:, NG:NR].rearrange("p (g e) -> p g e", g=NG), bc(ohg[:], EPG), ALU.mult),
                   "in_group")
                do(v.tensor_reduce(ein[:], g8.rearrange("p g e -> p e g"), AX.X, ALU.add), "expert_logits")
                for n, (src, dst) in enumerate(((ein, o1), (e2, o2))):
                    m = s1[:, 4 + n:5 + n]
                    do(v.tensor_reduce(m, src[:], AX.X, ALU.max), f"top{n}")
                    do(v.scalar_tensor_tensor(out=pr8[:], in0=src[:], scalar=m, in1=prio8,
                                              op0=ALU.is_equal, op1=ALU.mult), f"top_prio{n}")
                    do(v.tensor_reduce(s1[:, 6:7], pr8[:], AX.X, ALU.max), f"top_prio_max{n}")
                    do(v.tensor_scalar(dst[:], pr8[:], s1[:, 6:7], None, ALU.is_equal), f"top_one_hot{n}")
                    if n == 0:
                        do(v.scalar_tensor_tensor(out=e2[:], in0=o1[:], scalar=-1e30, in1=ein[:],
                                                  op0=ALU.mult, op1=ALU.add), "without_first")
                do(v.tensor_tensor(s1[:, 7:8], s1[:, 5:6], s1[:, 4:5], ALU.subtract), "gap")
                t.w(act, "gap_exp")
                do(v.tensor_scalar(s1[:, 9:10], s1[:, 8:9], 1.0, None, ALU.add), "gate_sum")
                do(v.reciprocal(s1[:, 9:10], s1[:, 9:10]), "gate_rec")
                do(v.tensor_tensor(gate[:, bass.ds(t.i, 1)], s1[:, 9:10], s1[:, 1:2], ALU.mult), "gate0")
                do(v.tensor_tensor(s1[:, 10:11], s1[:, 8:9], s1[:, 9:10], ALU.mult), "gate1_share")
                do(v.tensor_tensor(gate[:, bass.ds(t.i + NT, 1)], s1[:, 10:11], s1[:, 1:2], ALU.mult), "gate1")
                t.w0(ten, "counts")
                do(v.tensor_scalar(ohg[:], ohg[:], vcol[:, bass.ds(t.i, 1)], None, ALU.mult), "group_valid")
                for n, o in enumerate((o1, o2)):
                    do(v.tensor_tensor(ohs[:, n, :].rearrange("p (g e) -> p g e", g=NG), bc(ohg[:], EPG),
                                       bm(o[:], NG), ALU.mult), f"one_hot{n}")
                do(v.tensor_tensor(ohs[:, 2, :], ohs[:, 0, :], ohs[:, 1, :], ALU.add), "one_hots")
                for n in range(2):
                    ins = v.tensor_copy(oh[:, bass.ds(t.i * NE + n * NT * NE, NE)], ohs[:, n, :])
                t.mark(ins, "one_hots_kept")
                t.w(ten, "counts")
                do(v.tensor_tensor(ranks[:], bank[6][:, 0:NE], base[:], ALU.add), "ranks")
                do(v.tensor_tensor(base[:], bank[6][:, NE:2 * NE], base[:], ALU.add), "counts")
                for n in range(2):
                    do(v.tensor_tensor(t36[:, 0:NE], ranks[:], ohs[:, n, :], ALU.mult), f"rank_of{n}")
                    do(v.tensor_reduce(rank[:, bass.ds(t.i + n * NT, 1)], t36[:, 0:NE], AX.X, ALU.add), f"rank{n}")

            engine_loop(v, vec, NT, turn)


def dispatch(nc, io, scr, keep):
    oh, rank, counts = keep["onehot"], keep["rank"], keep["counts"]
    table = scr["table"]
    with ExitStack() as ctx:
        def sb(name, shape, dt=F32):
            return ctx.enter_context(nc.sbuf_tensor("di_" + name, shape, dt))

        KB = SEQ // P + 1
        ps = ctx.enter_context(nc.psum_tensor("di_ps", [P, 512], F32))
        nums = sb("nums", [P, KB + NBLK])
        cols = sb("cols", [P, 3, NT])
        ident = sb("ident", [P, P])
        ones = sb("ones", [P, NE])
        cmp1 = sb("cmp1", [P, NE, KB])
        cmp2 = sb("cmp2", [P, NBLK, NE])
        blocks = sb("blocks", [P, NE])
        ends = sb("ends", [P, NE])
        starts = sb("starts", [P, NE])
        be = sb("be", [P, NBLK])
        tmp = sb("tmp", [P, NT, NE])
        dest = sb("dest", [P, 2, NT])
        desti = sb("desti", [P, 2 * NT], I32)
        zero = sb("zero", [NBLK + 2, P])
        tok = sb("tok", [NBLK, P])

        vec = ctx.enter_context(nc.semaphore("di_vec"))
        consts = ctx.enter_context(nc.semaphore("di_consts"))
        cleared = ctx.enter_context(nc.semaphore("di_cleared"))
        scattered = ctx.enter_context(nc.semaphore("di_scattered"))
        tok_in = ctx.enter_context(nc.semaphore("di_tok_in"))
        turned = ctx.enter_context(nc.semaphore("di_turned"))
        DEST = 16
        block = ctx.enter_context(nc.Block())

        @block.sync
        def _(sp):
            sp.dma_start(nums[:], io["nums"].to_broadcast([P, KB + NBLK])).then_inc(consts, 16)
            sp.dma_start(cols[:], io["cols"].rearrange("p (a n) -> p a n", a=3)).then_inc(consts, 16)
            sp.dma_start(ident[:], io["ident"]).then_inc(consts, 16)
            sp.wait_ge(vec, 1)
            sp.dma_start(table.rearrange("(b p) o -> b (p o)", p=P), zero[:]).then_inc(cleared, 16)
            sp.wait_ge(scattered, 16 * 2 * NT)
            sp.dma_start(tok[:], table[0:NBLK * P].rearrange("(b p) o -> b (p o)", p=P)).then_inc(tok_in, 16)
            sp.wait_ge(tok_in, 16)

        @block.gpsimd
        def _(g):
            g.wait_ge(cleared, 16)
            g.wait_ge(vec, DEST)
            for n in range(2 * NT):
                g.indirect_dma_start(table, bass.IndirectOffsetOnAxis(ap=desti[:, n:n + 1], axis=0),
                                     cols[:, 0, n % NT:n % NT + 1], None).then_inc(scattered, 16)
            g.wait_ge(scattered, 16 * 2 * NT)

        @block.tensor
        def _(pe):
            pe.wait_ge(tok_in, 16)
            pe.transpose(ps[:, 0:NBLK], tok[:], ident[0:NBLK, 0:NBLK]).then_inc(turned, 1)

        @block.vector
        def _(v):
            n = [0]

            def do(ins):
                n[0] += 1
                ins.then_inc(vec, 1)
                v.wait_ge(vec, n[0])

            do(v.memset(zero[:], 0.0))
            do(v.memset(ones[:], 1.0))
            v.wait_ge(consts, 48)
            do(v.tensor_tensor(cmp1[:], bc(counts[:], KB), bm(nums[:, 0:KB], NE), ALU.is_gt))
            do(v.tensor_reduce(blocks[:], cmp1[:], AX.X, ALU.add))
            do(v.tensor_tensor_scan(ends[:], ones[:], blocks[:], 0.0, ALU.mult, ALU.add))
            do(v.tensor_tensor(starts[:], ends[:], blocks[:], ALU.subtract))
            do(v.tensor_scalar(starts[:], starts[:], float(P), None, ALU.mult))
            for s in range(2):
                o = oh[:, s * NT * NE:(s + 1) * NT * NE].rearrange("p (t e) -> p t e", e=NE)
                do(v.tensor_tensor(tmp[:], o, bm(starts[:], NT), ALU.mult))
                do(v.tensor_reduce(dest[:, s, :], tmp[:], AX.X, ALU.add))
            do(v.tensor_tensor(dest[:], dest[:], rank[:].rearrange("p (a n) -> p a n", a=2), ALU.add))
            do(v.tensor_copy(keep["rows"][:], dest[:].rearrange("p a n -> p (a n)")))
            do(v.tensor_tensor(dest[:], dest[:], bm(cols[:, 1, :], 2), ALU.add))
            do(v.tensor_scalar(dest[:, 1, NT - 1:NT], dest[:, 1, NT - 1:NT], cols[:, 2, 0:1], None, ALU.add))
            do(v.tensor_copy(desti[:], dest[:].rearrange("p a n -> p (a n)")))
            assert n[0] == DEST, n[0]
            do(v.tensor_tensor(cmp2[:], bm(ends[:], NBLK), bc(nums[:, KB:KB + NBLK], NE), ALU.is_le))
            do(v.tensor_reduce(be[:], cmp2[:], AX.X, ALU.add))
            do(v.tensor_scalar(be[:], be[:], float(NE - 1), None, ALU.min))
            do(v.tensor_copy(keep["block_expert"][:], be[:]))
            v.wait_ge(turned, 1)
            do(v.tensor_copy(keep["tokens"][:], ps[:, 0:NBLK]))


def experts(nc, io, scr, keep):
    with ExitStack() as ctx:
        def sb(name, shape, dt=F32):
            return ctx.enter_context(nc.sbuf_tensor("ex_" + name, shape, dt))

        FC = FE // P
        bank = [ctx.enter_context(nc.psum_tensor(f"ex_bank{b}", [P, 512], F32)) for b in range(8)]
        b4 = [b[:, :].rearrange("p (a n) -> p a n", a=4) for b in bank]
        ident = sb("ident", [P, P])
        nought = sb("nought", [P, 1])
        spare = [sb(f"spare{s}", [P, 1]) for s in range(2)]
        started = ctx.enter_context(nc.semaphore("ex_started"))
        wg, wu, wd, idx, x, xT, th, hid, y = ([sb(f"{n}{s}", shape, dt) for s in range(2)] for n, shape, dt in (
            ("wg", [P, KC, FE], F32), ("wu", [P, KC, FE], F32), ("wd", [P, FC, D], F32), ("idx", [P, 1], I32),
            ("x", [P, D], F32), ("xT", [P, KC, P], F32), ("th", [P, FC, P], F32), ("hid", [P, FC, P], F32),
            ("y", [P, D], F32)))

        ten, vec, act, pol = (Steps(nc, ctx, "experts_" + n) for n in ("tensor", "vector", "scalar", "gpsimd"))
        const = Dmas(nc, ctx, "ex_const", 1)
        up_in = [Dmas(nc, ctx, f"ex_up_in{s}", 2) for s in range(2)]
        down_in = [Dmas(nc, ctx, f"ex_down_in{s}", 1) for s in range(2)]
        x_in = [Dmas(nc, ctx, f"ex_x_in{s}", 1) for s in range(2)]
        y_out = [Dmas(nc, ctx, f"ex_y_out{s}", 1, 1) for s in range(2)]
        block = ctx.enter_context(nc.Block())
        turns = NBLK // 2

        @block.sync
        def _(sp):
            sp.dma_start(ident[:], io["ident"]).then_inc(const.sem, 16)

            def turn(t):
                es = [sp.value_load(keep["block_expert"][0:1, bass.ds(t.i * 2 + s, 1)], min_val=0, max_val=NE - 1)
                      for s in range(2)]
                es = [bass.ds(sp.snap(e), 1) for e in es]
                t.ahead(*[(ten, f"{n}{s}", -1) for n in ("up", "down") for s in range(2)])
                for s, e in enumerate(es):
                    t.w0(ten, f"up{s}")
                    up_in[s].go(sp.dma_start(wg[s][:], io["w_eg"][e].rearrange("a (p k) n -> (a p) k n", k=KC)))
                    up_in[s].go(sp.dma_start(wu[s][:], io["w_eu"][e].rearrange("a (p k) n -> (a p) k n", k=KC)))
                    t.w0(ten, f"down{s}")
                    down_in[s].go(sp.dma_start(wd[s][:], io["w_ed"][e].rearrange("a (p k) n -> (a p) k n", k=FC)))

            engine_loop(sp, None, turns, turn)

        @block.gpsimd
        def _(g):
            g.memset(nought[:], 0.0).then_inc(started, 1)
            g.wait_ge(started, 1)

            def turn(t):
                for s in range(2):
                    t.w0(ten, f"x_T{s}1")
                    t.do(g.tensor_copy(idx[s][:], keep["tokens"][:, bass.ds(t.i * 2 + s, 1)]), f"idx{s}")
                    g.tensor_tensor(spare[s][:], nought[:], nought[:], ALU.add)
                    x_in[s].go(g.indirect_dma_start(x[s][:], None, scr["h"],
                                                    bass.IndirectOffsetOnAxis(ap=idx[s][:, 0:1], axis=0)))

            engine_loop(g, pol, turns, turn)

        @block.scalar
        def _(a):
            a.sem_inc(y_out[0].sem, 16)
            a.sem_inc(y_out[1].sem, 16)

            def turn(t):
                for s in range(2):
                    for k in range(2):
                        t.w(ten, f"x_T{s}{k}")
                        t.mark(a.activation(xT[s][:, 4 * k:4 * k + 4, :], b4[k], ACT.Copy), f"x_T{s}{k}")
                    t.w(ten, f"up{s}")
                    t.mark(a.activation(th[s][:], b4[2 + s][:, 0:FC, :], ACT.Tanh, scale=0.5), f"tanh{s}")
                    t.w(ten, f"down{s}")
                    t.left(y_out[s])
                    a.activation(y[s][:, 0:512], bank[4 + 2 * s][:, :], ACT.Copy)
                    t.do(a.activation(y[s][:, 512:D], bank[5 + 2 * s][:, :], ACT.Copy), f"y{s}")
                    y_out[s].go(a.dma_start(scr["ys"][bass.ds((t.i * 2 + s) * P, P), :], y[s][:]))

            engine_loop(a, act, turns, turn)
            for s in range(2):
                a.wait_ge(y_out[s].sem, y_out[s].done(turns - 1))

        @block.tensor
        def _(pe):
            pe.wait_ge(const.sem, 16)

            def turn(t):
                for s in range(2):
                    t.arrived(x_in[s])
                    (t.w0 if s == 0 else t.w)(act, f"x_T{1 - s}1")
                    xv = x[s][:, :].rearrange("t (p k) -> t k p", k=KC)
                    for k in range(2):
                        for c in range(4):
                            ins = pe.transpose(b4[k][:, c, :], xv[:, 4 * k + c, :], ident[:, :])
                        t.mark(ins, f"x_T{s}{k}")
                    t.arrived(up_in[s])
                    t.w(act, f"x_T{s}1")
                    t.w0(vec, f"hidden{s}")
                    for w, o in ((wg[s], 0), (wu[s], FC)):
                        for m in range(FC):
                            for k in range(KC):
                                ins = pe.matmul(b4[2 + s][:, o + m, :], w[:, k, m:FE:FC], xT[s][:, k, :],
                                                start=(k == 0), stop=(k == KC - 1))
                    t.mark(ins, f"up{s}")
                    t.arrived(down_in[s])
                    t.w(vec, f"hidden{s}")
                    t.w0(act, f"y{s}")
                    for n in range(2):
                        for m in range(FC):
                            ins = pe.matmul(bank[4 + 2 * s + n][:, :], hid[s][:, m, :], wd[s][:, m, n * 512:(n + 1) * 512],
                                            start=(m == 0), stop=(m == FC - 1))
                    t.mark(ins, f"down{s}")

            engine_loop(pe, ten, turns, turn)

        @block.vector
        def _(v):
            def turn(t):
                for s in range(2):
                    t.w(act, f"tanh{s}")
                    t.w0(ten, f"down{s}")
                    b = b4[2 + s]
                    t.do(v.scalar_tensor_tensor(out=th[s][:], in0=th[s][:], scalar=1.0, in1=b[:, 0:FC, :],
                                                op0=ALU.add, op1=ALU.mult), f"silu{s}")
                    t.mark(v.scalar_tensor_tensor(out=hid[s][:], in0=th[s][:], scalar=0.5, in1=b[:, FC:2 * FC, :],
                                                  op0=ALU.mult, op1=ALU.mult), f"hidden{s}")

            engine_loop(v, vec, turns, turn)


def combine(nc, io, scr, keep):
    with ExitStack() as ctx:
        def sb(name, shape, dt=F32):
            return ctx.enter_context(nc.sbuf_tensor("co_" + name, shape, dt))

        rows = sb("rows", [P, 2, D])
        eps = sb("eps", [P, 1])
        idx = [sb(f"idx{s}", [P, 1], I32) for s in range(2)]
        y = [sb(f"y{s}", [P, D]) for s in range(2)]
        h = sb("h", [P, D])
        r = sb("r", [P, D])
        o = sb("o", [P, D])
        st = sb("st", [P, 2, 6])
        mv = sb("mv", [P, 2])
        rstd = sb("rstd", [P, 1])
        gates = sb("gates", [P, 2])
        nought, spare = sb("nought", [P, 1]), sb("spare", [P, 1])
        started = ctx.enter_context(nc.semaphore("co_started"))
        gate = keep["gate"]

        vec, act, pol = (Steps(nc, ctx, "combine_" + n) for n in ("vector", "scalar", "gpsimd"))
        consts = Dmas(nc, ctx, "co_consts", 2)
        y_in = Dmas(nc, ctx, "co_y_in", 2)
        h_in = Dmas(nc, ctx, "co_h_in", 1)
        out = Dmas(nc, ctx, "co_out", 1, 1)
        block = ctx.enter_context(nc.Block())

        @block.sync
        def _(sp):
            sp.dma_start(rows[:], io["ln2"].rearrange("(o a) n -> o a n", o=1).to_broadcast([P, 2, D])).then_inc(consts.sem, 16)
            sp.dma_start(eps[:], io["eps"]).then_inc(consts.sem, 16)
            sp.sem_inc(out.sem, 16)

            def turn(t):
                t.ahead((vec, "residual", -1), (vec, "y", 0))
                col = bass.ds(sp.snap(t.i * P), P)
                t.w0(vec, "residual")
                h_in.go(sp.dma_start(h[:], scr["h"][col, :]))
                t.w(vec, "y")
                out.go(sp.dma_start(io["y_out"][col, :], o[:]))

            engine_loop(sp, None, NT, turn)
            sp.wait_ge(out.sem, out.done(NT - 1))

        @block.gpsimd
        def _(g):
            g.memset(nought[:], 0.0).then_inc(started, 1)
            g.wait_ge(started, 1)

            def turn(t):
                t.w0(vec, "second")
                g.tensor_copy(idx[0][:], keep["rows"][:, bass.ds(t.i, 1)])
                t.do(g.tensor_copy(idx[1][:], keep["rows"][:, bass.ds(t.i + NT, 1)]), "idx")
                g.tensor_tensor(spare[:], nought[:], nought[:], ALU.add)
                for s in range(2):
                    y_in.go(g.indirect_dma_start(y[s][:], None, scr["ys"],
                                                 bass.IndirectOffsetOnAxis(ap=idx[s][:, 0:1], axis=0)))

            engine_loop(g, pol, NT, turn)

        @block.scalar
        def _(a):
            a.wait_ge(consts.sem, consts.done(0))

            def turn(t):
                t.w(vec, "stats")
                t.mark(a.activation(rstd[:], mv[:, 1:2], ACT.Sqrt, bias=eps[:, 0:1]), "root")

            engine_loop(a, act, NT, turn)

        @block.vector
        def _(v):
            v.wait_ge(consts.sem, consts.done(0))

            def turn(t):
                do = t.do
                v.tensor_copy(gates[:, 0:1], gate[:, bass.ds(t.i, 1)])
                do(v.tensor_copy(gates[:, 1:2], gate[:, bass.ds(t.i + NT, 1)]), "gates")
                t.arrived(y_in)
                do(v.tensor_scalar(r[:], y[0][:], gates[:, 0:1], None, ALU.mult), "first")
                do(v.scalar_tensor_tensor(out=r[:], in0=y[1][:], scalar=gates[:, 1:2], in1=r[:],
                                          op0=ALU.mult, op1=ALU.add), "second")
                t.arrived(h_in)
                do(v.scalar_tensor_tensor(out=r[:], in0=h[:], scalar=ALPHA, in1=r[:], op0=ALU.mult, op1=ALU.add),
                   "residual")
                for n in range(2):
                    ins = v.bn_stats(st[:, n, :], r[:, n * 512:n * 512 + 512])
                do(ins, "half_stats")
                v.tensor_copy(rstd[:], st[:, 0, 0:1])
                do(v.bn_aggr(mv[:], st[:]), "stats")
                t.w(act, "root")
                do(v.reciprocal(rstd[:], rstd[:]), "rstd")
                do(v.tensor_scalar(r[:], r[:], mv[:, 0:1], rstd[:, 0:1], ALU.subtract, ALU.mult), "normed")
                do(v.tensor_tensor(r[:], r[:], rows[:, 0, :], ALU.mult), "gain")
                t.left(out)
                do(v.tensor_tensor(o[:], r[:], rows[:, 1, :], ALU.add), "y")

            engine_loop(v, vec, NT, turn)


def _shape_constants():
    k, t = np.arange(P)[:, None], np.arange(P)[None, :]
    head = (k // 64 == t // 64)
    f = np.float32

    def off(size):
        return (k // size % 2 == 0) & (t // size == k // size + 1)

    cst = np.stack([head, head / 64.0, k < t, k <= t, k > t, off(1), off(1).T], 1).astype(f).reshape(P, 7 * P)
    levs = np.stack([off(2 ** n) for n in range(1, LEVELS + 1)], 1).astype(f).reshape(P, LEVELS * P)
    rms = np.stack([np.full((P, P), 1.0 / QL), np.full((P, P), 1.0 / KVL)], 1).astype(f).reshape(P, 2 * P)
    half = ROPE // 2
    inv = (f(10000.0) ** (-np.arange(0, ROPE, 2, dtype=f) / f(ROPE))).astype(f)
    pos = np.zeros((NT, P), f)
    pos[:NT - 1] = np.arange(SEQ, dtype=f).reshape(NT - 1, P)
    pos[NT - 1] = PAST + np.arange(P, dtype=f)
    ang = (pos[:, :, None] * inv).astype(f).astype(np.float64)
    cos, sin = np.cos(ang), np.sin(ang)
    both = np.stack([np.concatenate([cos, cos], -1), np.concatenate([-sin, sin], -1)], 2)
    rope = np.tile(both.transpose(0, 3, 2, 1), (1, 4, 1, 1)).astype(f).reshape(NT, P, 2 * P)
    assert half * 2 == ROPE
    valid = np.ones((NT, P), f)
    valid[NT - 1, DEC:] = 0
    return dict(cst=cst, levs=levs, rmsw=rms, rope=rope, ident=np.eye(P, dtype=f)), valid


def _by_channel(v):
    return np.moveaxis(v.reshape(v.shape[:-1] + (v.shape[-1] // P, P)), -1, 0)


def _layout(a):
    c, valid = _shape_constants()
    f = np.float32
    w = {k: np.asarray(v) for k, v in a.items()}

    def rows(m):
        return np.ascontiguousarray(m.reshape(-1, P, m.shape[1]).transpose(1, 0, 2)).reshape(P, -1)

    x = np.zeros((NT, P, D), f)
    x[:NT - 1] = w["x_prompt"].reshape(NT - 1, P, D)
    x[NT - 1, :DEC] = w["x_sample"][0]
    c["x"] = x
    wi = w["w_in"][0]
    swap = np.r_[ROPE // 2:ROPE, 0:ROPE // 2]
    kpe = wi[:, QL + KVL:QL + KVL + ROPE]
    c["w_in"] = rows(np.concatenate([wi[:, :QL + KVL], wi[:, QL + KVL + ROPE:], kpe, kpe[:, swap]], 1))
    uq = w["w_uq"][0]
    pe = uq[:, :, NOPE:]
    c["w_uq"] = rows(np.concatenate([uq[:, :, :NOPE].reshape(QL, -1), pe.reshape(QL, -1),
                                     pe[:, :, swap].reshape(QL, -1)], 1))
    wa = np.zeros((P, 2, 512), f)
    wa[:64, 0], wa[64:, 1] = w["w2"][0], w["a2"][0]
    c["w_wa"] = wa.reshape(P, 1024)
    c["w_g"] = w["g2"][0]
    par = np.zeros((P, 64), f)
    vecs = [(0, "mu_shift"), (14, "q_norm_g"), (17, "kv_norm_g"), (20, "w0"), (24, "a0"), (28, "k_k"), (32, "k_a"),
            (36, "r_k"), (40, "lnx_g"), (44, "lnx_b")]
    for at, name in vecs:
        v = _by_channel(w[name][0].reshape(-1))
        par[:, at:at + v.shape[1]] = v
    par[:, 48], par[:, 49], par[:, 50] = RMS_EPS, GN_EPS, LN_EPS
    c["par"] = par
    tile_c = np.zeros((NT, P, 2 * P + 15), f)
    tile_c[:, :, 0:P] = (-LOGW / 2) * valid[:, None, :]
    tile_c[:, :, P:2 * P] = valid[:, None, :]
    tile_c[:NT - 1, :, 2 * P] = 1
    tile_c[NT - 1, :, 2 * P + 1:] = _by_channel(w["state_shift"][0, 0])
    c["tile_c"] = tile_c
    s_init = np.zeros((NT, 2, 64, 4, 64), f)
    s_init[NT - 1] = w["state_wkv"][0, 0].reshape(4, 2, 64, 64).transpose(1, 3, 0, 2)
    c["s_init"] = s_init.reshape(NT, P, 256)
    c["past_ckvT"] = rows(w["cache_ckv"][0, 0].T)
    c["past_kpeT"] = w["cache_kpe"][0, 0].T
    c["w_ukv"] = w["w_ukv"][0].reshape(CKV, P, H, P).transpose(2, 1, 0, 3).reshape(H, P, CKV * P)
    c["w_o"] = rows(w["w_o"][0])
    c["w_r"] = rows(np.concatenate([w["w_gr"][0], w["w_er"][0]], 1))
    c["ln1"] = np.stack([w["ln1_g"][0], w["ln1_b"][0]])
    c["ln2"] = np.stack([w["ln2_g"][0], w["ln2_b"][0]])
    c["small"] = np.concatenate([w["b_gr"][0], w["b_er"][0], np.arange(NG, 0, -1, dtype=f),
                                 np.arange(EPG, 0, -1, dtype=f)])[None]
    before = (np.arange(P)[:, None] < np.arange(P)[None, :]).astype(f)
    c["eps"] = np.full((P, 1), LN_EPS, f)
    c["cst3"] = np.stack([np.eye(P, dtype=f), before, np.ones((P, P), f)], 1).reshape(P, 3 * P)
    c["vcol"] = valid.T.copy()
    kb = SEQ // P + 1
    c["nums"] = np.concatenate([P * np.arange(kb), np.arange(NBLK)]).astype(f)[None]
    tok = np.arange(TOK).reshape(NT, P).T
    dump = (1 - valid.T) * (NBLK * P + np.arange(P)[:, None])
    again = np.tile((1 - valid[NT - 1])[:, None] * P, (1, NT))
    c["cols"] = np.stack([tok, dump, again], 1).astype(f).reshape(P, 3 * NT)
    for name in ("w_eg", "w_eu", "w_ed"):
        c[name] = w[name][0]
    return c


def program(nc, io, scr):
    with ExitStack() as ctx:
        def kept(name, cols, dt=F32):
            return ctx.enter_context(nc.sbuf_tensor("kept_" + name, [P, cols], dt))

        keep = dict(onehot=kept("onehot", 2 * NT * NE), rank=kept("rank", 2 * NT), gate=kept("gate", 2 * NT),
                    counts=kept("counts", NE), rows=kept("rows", 2 * NT, I32), tokens=kept("tokens", NBLK, I32),
                    block_expert=kept("block_expert", NBLK, I32))
        mixer(nc, io, scr)
        attention(nc, io, scr)
        router(nc, io, scr, keep)
        dispatch(nc, io, scr, keep)
        experts(nc, io, scr, keep)
        combine(nc, io, scr, keep)


_SCRATCH = dict(kpeT=(ROPE, TOK), ckvT=(KVL, TOK), qT=(H, QK, TOK), rwT=(512, TOK), attn=(TOK, 512), h=(TOK, D),
                table=((NBLK + 2) * P, 1), ys=(NBLK * P, D))
_OUTS = dict(y_out=(TOK, D), ckv_out=(NT, P, KVL), kpe_out=(NT, P, ROPE), edge_out=(NT, P, 2 * NPR),
             state_out=(NT, P, 256))
_SCRATCH_KIND = "Internal"


def _outputs(r):
    y, ckv, kpe, edge, state = (r["out_" + n] for n in _OUTS)
    ckv, kpe = ckv.reshape(TOK, KVL), kpe.reshape(TOK, ROPE)
    shift = [edge[t].reshape(P, 2, NPR)[:, e].T.reshape(1, 1, -1) for t, e in ((NT - 2, 1), (NT - 1, 0))]
    wkv = [state[t].reshape(2, 64, 4, 64).transpose(2, 0, 3, 1).reshape(1, 1, H, 64, 64) for t in (NT - 2, NT - 1)]
    s = slice(SEQ, SEQ + DEC)
    return (y[:SEQ][None], y[s][None], ckv[:SEQ][None, None], kpe[:SEQ][None, None], wkv[0], shift[0],
            ckv[s][None, None], kpe[s][None, None], wkv[1], shift[1])


def kernel(**inputs):
    import concourse.bacc as _bacc
    from concourse.bass_utils import run_bass_kernel_spmd as _run

    nc = _bacc.Bacc("TRN2", target_bir_lowering=False, num_devices=1)
    io, arrays = {}, {}
    for name, a in _layout(inputs).items():
        arrays["in_" + name] = np.ascontiguousarray(a)
        io[name] = nc.dram_tensor("in_" + name, a.shape, mybir.dt.from_np(a.dtype), kind="ExternalInput").ap()
    for name, shape in _OUTS.items():
        io[name] = nc.dram_tensor("out_" + name, shape, F32, kind="ExternalOutput").ap()
    scr = {name: nc.dram_tensor("scr_" + name, shape, F32, kind=_SCRATCH_KIND).ap() for name, shape in _SCRATCH.items()}
    program(nc, io, scr)
    return _outputs(_run(nc, [arrays], core_ids=[0]).results[0])
```

```python
from contextlib import ExitStack

import numpy as np

import concourse.bass as bass
from concourse import mybir

F32 = mybir.dt.float32
I32 = mybir.dt.int32
ALU = mybir.AluOpType
ACT = mybir.ActivationFunctionType
AX = mybir.AxisListType
P = 128
D = 1024
SEQ, DEC, PAST = 2048, 32, 128
NT = SEQ // P + 1
TOK = NT * P
H = 8
NOPE, ROPE, VD = 64, 32, 64
QK = NOPE + ROPE
QL, KVL = 384, 256
CQ, CKV = QL // P, KVL // P
NPR = 14
WCOL = QL + KVL + NPR * P + 2 * ROPE
KC = D // P
NG, EPG, FE = 4, 8, 256
NE = NG * EPG
NR = NG + NE
ASSIGN = 2 * (SEQ + DEC)
NBLK = (ASSIGN + NE * (P - 1)) // P
SLOTS = 4
ALPHA = 2.0 ** 0.25
SCALE = float(QK) ** -0.5
LN_EPS, RMS_EPS, GN_EPS = 1e-5, 1e-6, 64e-5
LOGW = float(np.exp(-0.5))
LEVELS = 6

PE_ORDER = "abaabaaabababababbbb"
ACT_ORDER = "abababaaabaab"
VEC_ORDER = "bababbbbabbbb"

STEPS = {
    "project_tensor": (
        "x_transposed0 x_transposed1 pr_proj0 pr_proj1 pr_proj2 pr_proj3 cq_proj ckv_proj rms_sums q_nope q_pe "
        "ckv_tokens "
    ).split(),
    "project_vector": (
        "pr_edge rms cq_normed ckv_normed kpe_cos kpe_sin kpe_roped q_rope_cos q_rope_sin q_roped "
    ).split(),
    "project_scalar": (
        "xT0 xT1 pr0 pr1 pr2 pr3 edges cq_sq ckv_sq rms_root q_nope ckv_tokens "
    ).split(),
    "rwkv_tensor": (
        "lora_w lora_a lora_g kk_norm v_tokens bonus_sum gram_l0 gram_l1 gram_b0 gram_b1 gram_k0 gram_k1 gram_k2 "
        "gram_k3 U0 Z1_0 Z1_1 U1_0 T1_0 U1_1 T1_1 Z2_0 Z2_1 U2_0 T2_0 U2_1 T2_1 Z3_0 Z3_1 U3_0 T3_0 U3_1 T3_1 Z4_0 Z4_1 "
        "U4_0 T4_0 U4_1 T4_1 Z5_0 Z5_1 U5_0 T5_0 U5_1 T5_1 Z6_0 Z6_1 U6_0 U6_1 b_tokens k_tokens G SA y state_add "
        "y_mean y_var "
    ).split(),
    "rwkv_vector": (
        "u_low a_lo u_k g_sig kk u_r u_v log_w cum mid a_sig a_ka kh kk_norm2 kk_rs kk_normed a_hat en_masked b_gate "
        "b_hat k_hat bonus T_level0_0 T_level0_1 L1 RB0 RB1 state_in state_mid MK0 MK1 MK2 MK3 Z1_0 Z1_1 U1_0 T1_0 U1_1 "
        "T1_1 Z2_0 Z2_1 U2_0 T2_0 U2_1 T2_1 Z3_0 Z3_1 U3_0 T3_0 U3_1 T3_1 Z4_0 Z4_1 U4_0 T4_0 U4_1 T4_1 Z5_0 Z5_1 U5_0 "
        "T5_0 U5_1 T5_1 Z6_0 Z6_1 U6_0 U6_1 state_sum state y_centred y_rs y_normed y_bonus gated "
    ).split(),
    "rwkv_scalar": (
        "u_own_low u_own_k u_own_r u_own_v g_lo w_tanh a_tanh kk_sq g_out exp_pos exp_neg em kk_root v_tokens U0 "
        "b_tokens k_tokens G SA y y_sq y_root y_gain "
    ).split(),
    "rwkv_gpsimd": (
        "r_hat rk rkr T_start0 T_start1 Z_clear1 Z_clear2 Z_clear3 Z_clear4 Z_clear5 "
    ).split(),
    "attention_tensor": (
        "K0 K1 K2 K3 K4 V0 V1 V2 S0_0 S1_0 maxrow0 S2_0 ST0_0 PV0_0 maxrow1 S3_0 ST1_0 PV1_0 maxrow2 S4_0 S4_1 ST2_0 "
        "PV2_0 maxrow3 S5_0 S5_1 ST3_0 PV3_0 maxrow4 S6_0 S6_1 ST4_0 ST4_1 PV4_0 PV4_1 maxrow5 S7_0 S7_1 ST5_0 ST5_1 "
        "PV5_0 PV5_1 maxrow6 S8_0 S8_1 S8_2 ST6_0 ST6_1 PV6_0 PV6_1 maxrow7 S9_0 S9_1 S9_2 ST7_0 ST7_1 PV7_0 PV7_1 "
        "maxrow8 S10_0 S10_1 S10_2 ST8_0 ST8_1 PV8_0 ST8_2 PV8_1 PV8_2 maxrow9 S11_0 S11_1 S11_2 ST9_0 ST9_1 PV9_0 "
        "ST9_2 PV9_1 PV9_2 maxrow10 S12_0 S12_1 S12_2 S12_3 ST10_0 ST10_1 PV10_0 ST10_2 PV10_1 PV10_2 maxrow11 S13_0 "
        "S13_1 S13_2 S13_3 ST11_0 ST11_1 PV11_0 ST11_2 PV11_1 PV11_2 maxrow12 S14_0 S14_1 S14_2 S14_3 ST12_0 ST12_1 "
        "PV12_0 ST12_2 PV12_1 ST12_3 PV12_2 PV12_3 maxrow13 S15_0 S15_1 S15_2 S15_3 ST13_0 ST13_1 PV13_0 ST13_2 PV13_1 "
        "ST13_3 PV13_2 PV13_3 maxrow14 S16_0 ST14_0 ST14_1 PV14_0 ST14_2 PV14_1 ST14_3 PV14_2 PV14_3 maxrow15 ST15_0 "
        "ST15_1 PV15_0 ST15_2 PV15_1 ST15_3 PV15_2 PV15_3 maxrow16 ST16_0 PV16_0 "
    ).split(),
    "attention_vector": (
        "V0 V1 V2 max0_0 negmax0 max1_0 negmax1 maxrow0 max2_0 negmax2 sum_0 out_0 maxrow1 max3_0 negmax3 sum_1 out_1 "
        "maxrow2 max4_0 max4_1 negmax4 sum_2 out_2 maxrow3 max5_0 max5_1 negmax5 sum_3 out_3 maxrow4 max6_0 max6_1 "
        "negmax6 sum_4 out_4 maxrow5 max7_0 max7_1 negmax7 sum_5 out_5 maxrow6 max8_0 max8_1 max8_2 negmax8 sum_6 out_6 "
        "maxrow7 max9_0 max9_1 max9_2 negmax9 sum_7 out_7 maxrow8 max10_0 max10_1 max10_2 negmax10 sum_8 out_8 maxrow9 "
        "max11_0 max11_1 max11_2 negmax11 sum_9 out_9 maxrow10 max12_0 max12_1 max12_2 max12_3 negmax12 sum_10 out_10 "
        "maxrow11 max13_0 max13_1 max13_2 max13_3 negmax13 sum_11 out_11 maxrow12 max14_0 max14_1 max14_2 max14_3 "
        "negmax14 sum_12 out_12 maxrow13 max15_0 max15_1 max15_2 max15_3 negmax15 sum_13 out_13 maxrow14 max16_0 "
        "negmax16 sum_14 out_14 maxrow15 sum_15 out_15 maxrow16 sum_16 out_16 "
    ).split(),
    "attention_scalar": (
        "K0 K1 K2 K3 K4 exp0_0 exp1_0 exp2_0 exp3_0 exp4_0 exp4_1 exp5_0 exp5_1 exp6_0 exp6_1 exp7_0 exp7_1 exp8_0 "
        "exp8_1 exp8_2 exp9_0 exp9_1 exp9_2 exp10_0 exp10_1 exp10_2 exp11_0 exp11_1 exp11_2 exp12_0 exp12_1 exp12_2 "
        "exp12_3 exp13_0 exp13_1 exp13_2 exp13_3 exp14_0 exp14_1 exp14_2 exp14_3 exp15_0 exp15_1 exp15_2 exp15_3 "
        "exp16_0 "
    ).split(),
    "attention_gpsimd": (
        "hidden0 hidden1 hidden2 hidden3 hidden4 hidden5 hidden6 hidden7 hidden8 hidden9 hidden10 hidden11 hidden12 "
        "hidden13 hidden14 hidden15 "
    ).split(),
    "router_tensor": (
        "attn_T out_proj h_T0 h_T1 logits counts "
    ).split(),
    "router_vector": (
        "residual half_stats stats rstd normed gain h logits group_max group_max_pos group_prio group_prio_max "
        "group_one_hot group_prob in_group expert_logits top0 top_prio0 top_prio_max0 top_one_hot0 without_first top1 "
        "top_prio1 top_prio_max1 top_one_hot1 gap gate_sum gate_rec gate0 gate1_share gate1 group_valid one_hot0 "
        "one_hot1 one_hots one_hots_kept ranks counts rank_of0 rank0 rank_of1 rank1 "
    ).split(),
    "router_scalar": (
        "attn_T root h_T0 h_T1 group_exp gap_exp "
    ).split(),
    "up_tensor": (
        "x_T00 x_T01 x_T10 x_T11 gate0 up0 gate1 up1 "
    ).split(),
    "up_vector": (
        "silu0 hidden0 silu1 hidden1 "
    ).split(),
    "up_scalar": (
        "x_T00 x_T01 x_T10 x_T11 tanh0 tanh1 "
    ).split(),
    "up_gpsimd": (
        "idx0 idx1 "
    ).split(),
    "down_tensor": (
        "h_T0 down0 h_T1 down1 "
    ).split(),
    "down_scalar": (
        "h_T0 y0 h_T1 y1 "
    ).split(),
    "combine_vector": (
        "gates first second residual half_stats stats rstd normed gain y "
    ).split(),
    "combine_scalar": (
        "root "
    ).split(),
    "combine_gpsimd": (
        "idx "
    ).split(),
}


class Steps:

    def __init__(self, nc, ctx, name):
        self.sem = ctx.enter_context(nc.semaphore(name))
        self.name, self.names, self.seen = name, STEPS.get(name, ()), 0
        self.per = len(self.names)

    def mark(self, ins, name):
        assert self.names[self.seen] == name, (self.name, self.seen, name)
        self.seen += 1
        ins.then_inc(self.sem, 1)

    def whole(self):
        assert self.seen == self.per, (self.name, self.seen, self.per)
        self.seen = 0

    def done(self, turn, name):
        return self.per * (turn + 1) + self.names.index(name) + 1


class Dmas:

    def __init__(self, nc, ctx, name, n, start=0):
        self.sem = ctx.enter_context(nc.semaphore(name))
        self.n, self.start = n, start

    def go(self, ins):
        ins.then_inc(self.sem, 16)

    def done(self, turn):
        return 16 * self.n * (turn + 1 + self.start)


class Turn:

    def __init__(self, eng, own, i):
        self.eng, self.own, self.i = eng, own, i
        self.known = {}

    def ahead(self, *values):
        for counts, name, turn in values if not isinstance(self.i, int) else ():
            v = counts.done(self.i + turn, name) if name else counts.done(self.i + turn)
            reg = self.eng.alloc_register(f"v{len(self.known)}_{counts.sem.name}")
            self.eng.reg_mov(reg, v)
            self.known[counts.sem.name, name, turn] = reg

    def _wait(self, counts, name, turn):
        v = self.known.get((counts.sem.name, name, turn))
        if v is None:
            v = counts.done(self.i + turn, name) if name else counts.done(self.i + turn)
        self.eng.wait_ge(counts.sem, v)

    def do(self, ins, name):
        self.own.mark(ins, name)
        self.eng.wait_ge(self.own.sem, self.own.done(self.i, name))

    def mark(self, ins, name):
        self.own.mark(ins, name)

    def w(self, steps, name):
        self._wait(steps, name, 0)

    def w0(self, steps, name):
        self._wait(steps, name, -1)

    def next_done(self, steps, name):
        self._wait(steps, name, 1)

    def arrived(self, dmas):
        self._wait(dmas, None, 0)

    def left(self, dmas):
        self._wait(dmas, None, -1)


def engine_loop(eng, own, count, body):
    if own is not None:
        eng.sem_inc(own.sem, own.per)
    with eng.Fori(0, count) as i:
        body(Turn(eng, own, i))
    if own is not None:
        own.whole()


def woven(eng, count, a_steps, b_steps, front, back, order):
    def run(gens, turns, text):
        for c in text:
            next(gens[c], None)
        for g in gens.values():
            for _ in g:
                pass
        for t in turns:
            if t.own is not None:
                t.own.whole()

    for st in (a_steps, b_steps):
        if st is not None:
            eng.sem_inc(st.sem, st.per)
    if front is not None:
        t = Turn(eng, a_steps, 0)
        run({"a": front(t, False)}, [t], "")
    with eng.Fori(0, count - 1) as i:
        gens, turns = {}, []
        if front is not None:
            turns.append(Turn(eng, a_steps, i + 1))
            gens["a"] = front(turns[-1], True)
        if back is not None:
            turns.append(Turn(eng, b_steps, i))
            gens["b"] = back(turns[-1], True)
        run(gens, turns, order)
    if back is not None:
        t = Turn(eng, b_steps, count - 1)
        run({"b": back(t, False)}, [t], "")


def bc(ap, n):
    return ap.unsqueeze(2).to_broadcast([ap.shape[0], ap.shape[1], n])


def bm(ap, n):
    return ap.unsqueeze(1).to_broadcast([ap.shape[0], n, ap.shape[1]])


def mixer(nc, io, scr):
    with ExitStack() as ctx:
        def sb(name, shape, dt=F32):
            return ctx.enter_context(nc.sbuf_tensor("mx_" + name, shape, dt))

        bank = [ctx.enter_context(nc.psum_tensor(f"mx_bank{b}", [P, 512], F32)) for b in range(8)]
        b4 = [b[:, :].rearrange("p (a n) -> p a n", a=4) for b in bank]

        w_in = sb("w_in", [P, KC, WCOL])
        w_uq = sb("w_uq", [P, CQ, 1024])
        w_wa = sb("w_wa", [P, 2, 512])
        w_g = sb("w_g", [P, 512])
        par = sb("par", [P, 64])
        ident = sb("ident", [P, P])
        cst = sb("cst", [P, 7, P])
        bones, bmean, strict, incl, low, lev0, lev0T = (cst[:, k, :] for k in range(7))
        upper2 = cst[:, 2:4, :]
        levs = sb("levs", [P, LEVELS, 64])
        negh = sb("negh", [P, 8])
        rmsw = sb("rmsw", [P, 2, P])
        mu, qg, kvg = par[:, 0:14], par[:, 14:17], par[:, 17:19]
        w0c, a0c, kkc, kac, rkc, lxg, lxb = (par[:, 20 + 4 * k:24 + 4 * k] for k in range(7))

        x = sb("x", [P, D])
        rope = sb("rope", [P, 2, P])
        first = sb("first", [P, 1 + NPR])
        keep, shift0 = first[:, 0:1], first[:, 1:]
        masks = sb("masks", [P, 2, P])
        vm, valid = masks[:, 0, :], masks[:, 1, :]
        keep_s = sb("keep_s", [P, 1])
        s_init = sb("s_init", [P, 4, VD])
        xT = sb("xT", [P, KC, P])
        pr = sb("pr", [P, NPR, P + 1])
        edge = sb("edge", [P, 2, NPR])
        u = sb("u", [P, NPR, P])
        cq = sb("cq", [P, CQ, P])
        ckv = sb("ckv", [P, CKV, P])
        msr = sb("msr", [P, 2, P])
        kpe2 = sb("kpe2", [64, P])
        kpe = sb("kpe", [32, P])
        qn = sb("qn", [P, 4, P])
        qp = sb("qp", [P, 2, P])
        ckt = sb("ckt", [P, KVL + ROPE])
        lo = sb("lo", [P, P])
        sg = sb("sg", [P, P])
        lw = sb("lw", [P, 4, P])
        cum = sb("cum", [P, 4, P + 1])
        nm = sb("nm", [P, 4])
        ep = sb("ep", [P, 4, P + 1])
        en = sb("en", [P, 4, P + 1])
        em = sb("em", [P, 4])
        aa = sb("aa", [P, 4, P])
        gg = sb("gg", [P, 4, P])
        kk = sb("kk", [P, 4, P])
        t1 = sb("t1", [P, 4, P])
        kh = sb("kh", [P, 4, P])
        AR = sb("AR", [P, 4, 2, 2, P])
        vt = sb("vt", [P, 4, P])
        RB = sb("RB", [P, H, P])
        MK = sb("MK", [P, H, 2, P])
        L = sb("L", [P, H, P])
        U = sb("U", [P, H, P])
        T = sb("T", [P, H, P])
        Z = sb("Z", [P, H, P])
        S = sb("S", [P, 4, VD])
        Sp = sb("Sp", [P, 4, VD])
        ys = sb("ys", [P, 4, P])
        bon, yq, qr, bh = aa, cum[:, :, 1:P + 1], lw[:, 0:2, :], u[:, 4:8, :]
        sq5 = T[:, 0:5, :]
        bt, kt = L[:, 0:4, :], L[:, 4:8, :]
        Gs, SA = (Z[:, 4 * k:4 * k + 4, :].rearrange("p a n -> p (a n)") for k in range(2))
        ones = sb("ones", [P, P])
        mu1 = sb("mu1", [P, NPR])
        nought, spare = sb("nought", [P, 1]), sb("spare", [P, 1])

        A = {n: Steps(nc, ctx, "project_" + n) for n in ("tensor", "vector", "scalar")}
        B = {n: Steps(nc, ctx, "rwkv_" + n) for n in ("tensor", "vector", "scalar", "gpsimd")}
        aten, avec, aact = A["tensor"], A["vector"], A["scalar"]
        ten, vec, act, pol = B["tensor"], B["vector"], B["scalar"], B["gpsimd"]
        consts = Dmas(nc, ctx, "mx_consts", 9)
        setup = ctx.enter_context(nc.semaphore("mx_setup"))
        biases = ctx.enter_context(nc.semaphore("mx_biases"))
        x_in = Dmas(nc, ctx, "mx_x_in", 1)
        a_in = Dmas(nc, ctx, "mx_a_in", 2)
        b_in = Dmas(nc, ctx, "mx_b_in", 3)
        mla_out = Dmas(nc, ctx, "mx_mla_out", 10, 1)
        rwkv_out = Dmas(nc, ctx, "mx_rwkv_out", 1, 1)
        edge_out = Dmas(nc, ctx, "mx_edge_out", 1, 1)
        state_out = Dmas(nc, ctx, "mx_state_out", 1, 1)
        block = ctx.enter_context(nc.Block())


        def row(ap, i):
            return ap[bass.ds(i, 1)].rearrange("a p n -> p (a n)")

        def odd(ap, lev):
            return ap.rearrange("p h (k two b) -> p h k two b", two=2, b=2 ** lev)[:, :, :, 1, :]

        def even(ap, lev):
            return ap.rearrange("p h (k two b) -> p h k two b", two=2, b=2 ** lev)[:, :, :, 0, :]

        @block.sync
        def _(sp):
            for dst, src in ((w_in, io["w_in"]), (w_uq, io["w_uq"]), (w_wa, io["w_wa"]), (levs, io["levs"]),
                             (cst, io["cst"]), (rmsw, io["rmsw"])):
                n = dst.shape[1]
                consts.go(sp.dma_start(dst[:], src.rearrange("p (a n) -> p a n", a=n)))
            for dst, src in ((w_g, io["w_g"]), (par, io["par"]), (ident, io["ident"])):
                consts.go(sp.dma_start(dst[:], src))
            x_in.go(sp.dma_start(x[:], io["x"][0]))
            for d in (mla_out, rwkv_out, edge_out, state_out):
                sp.sem_inc(d.sem, 16 * d.n)

            def project(t, woven_in):
                t.ahead((aten, "x_transposed1", 0), (avec, "q_rope_sin", -1), (avec, "kpe_roped", 0),
                        (aact, "ckv_tokens", 0), (aact, "q_nope", 0), (avec, "q_roped", 0), (aact, "edges", 0))
                i = t.i if isinstance(t.i, int) else sp.snap(t.i)
                after = 1 if isinstance(i, int) else sp.snap(t.i + 1)
                col = bass.ds(i * P if isinstance(i, int) else sp.snap(t.i * P), P)
                yield
                t.w0(avec, "q_rope_sin")
                a_in.go(sp.dma_start(first[:], row(io["first"], i)))
                a_in.go(sp.dma_start(rope[:], row(io["rope"], i).rearrange("p (a n) -> p a n", a=2)))
                yield
                t.w(aten, "x_transposed1")
                x_in.go(sp.dma_start(x[:], row(io["x"], after)))
                t.w(avec, "kpe_roped")
                mla_out.go(sp.dma_start(scr["kpeT"][:, col], kpe[:]))
                mla_out.go(sp.dma_start(scr["ckvT"].rearrange("(c p) n -> p c n", p=P)[:, :, col], ckv[:]))
                t.w(aact, "edges")
                edge_out.go(sp.dma_start(row(io["edge_out"], i), edge[:].rearrange("p a n -> p (a n)")))
                t.w(aact, "q_nope")
                qd = scr["qT"]
                for h2 in range(2):
                    mla_out.go(sp.dma_start(qd.rearrange("(c b) d n -> b d c n", b=2)[h2, 0:NOPE, :, col],
                                            qn[h2 * 64:h2 * 64 + 64]))
                t.w(avec, "q_roped")
                for h4 in range(4):
                    mla_out.go(sp.dma_start(qd.rearrange("(c b) d n -> b d c n", b=4)[h4, NOPE:QK, :, col],
                                            qp[h4 * 32:h4 * 32 + 32]))
                t.w(aact, "ckv_tokens")
                mla_out.go(sp.dma_start(row(io["ckv_out"], i), ckt[:, 0:KVL]))
                mla_out.go(sp.dma_start(row(io["kpe_out"], i), ckt[:, KVL:KVL + ROPE]))

            def rwkv(t, woven_in):
                t.ahead((vec, "state_in", -1), (vec, "state", 0), (vec, "gated", 0))
                i = t.i if isinstance(t.i, int) else sp.snap(t.i)
                col = bass.ds(i * P if isinstance(i, int) else sp.snap(t.i * P), P)
                yield
                t.w0(vec, "state_in")
                b_in.go(sp.dma_start(masks[:], row(io["masks"], i).rearrange("p (a n) -> p a n", a=2)))
                b_in.go(sp.dma_start(keep_s[:], row(io["keep"], i)))
                b_in.go(sp.dma_start(s_init[:], row(io["s_init"], i).rearrange("p (a n) -> p a n", a=4)))
                yield
                t.w(vec, "state")
                state_out.go(sp.dma_start(row(io["state_out"], i), S[:].rearrange("p a n -> p (a n)")))
                t.w(vec, "gated")
                rwkv_out.go(sp.dma_start(scr["rwT"].rearrange("(c p) n -> p c n", p=P)[:, :, col], ys[:]))

            woven(sp, NT, None, None, project, rwkv, "abbaab")
            for d in (mla_out, rwkv_out, edge_out, state_out):
                sp.wait_ge(d.sem, d.done(NT - 1))
            sp.wait_ge(x_in.sem, x_in.done(NT))

        @block.gpsimd
        def _(g):
            for buf, val in ((AR, 0.0), (cum, 0.0), (pr, 0.0), (S, 0.0), (ones, 1.0), (nought, 0.0)):
                g.memset(buf[:], val).then_inc(setup, 1)
            g.wait_ge(setup, 6)
            g.wait_ge(consts.sem, consts.done(0))

            def rwkv(t, woven_in):
                t.w(act, "exp_pos")
                t.w(vec, "u_r")
                t.w0(ten, "y")
                for h in range(2):
                    hs = slice(h * 64, h * 64 + 64)
                    ins = g.tensor_tensor(AR[hs, :, h, 1, :], u[hs, 0:4, :], ep[hs, :, 1:P + 1], ALU.mult)
                t.do(ins, "r_hat")
                t.w(vec, "kk_normed")
                t.do(g.tensor_tensor(t1[:], u[:, 0:4, :], kh[:], ALU.mult), "rk")
                t.do(g.tensor_tensor(t1[:], t1[:], bc(rkc, P), ALU.mult), "rkr")
                for c in range(2):
                    hs = slice(4 * c, 4 * c + 4)
                    t.w(vec, f"T_level0_{c}")
                    t.do(g.tensor_tensor(T[:, hs, :], T[:, hs, :], bm(ident[:, :], 4), ALU.add), f"T_start{c}")
                for lev in range(1, LEVELS):
                    t.w(ten, f"T{lev - 1}_1" if lev > 1 else "U0")
                    e = even(Z[:, :, :], lev)
                    zz = nought[:, 0:1].unsqueeze(2).unsqueeze(3).to_broadcast([P, H, P // 2 ** (lev + 1), 2 ** lev])
                    t.do(g.tensor_tensor(e, zz, zz, ALU.add), f"Z_clear{lev}")
                yield

            woven(g, NT, None, pol, None, rwkv, "")

        @block.scalar
        def _(a):
            a.wait_ge(consts.sem, consts.done(0))
            a.activation(negh[:], par[:, 20:28], ACT.Copy, scale=0.5).then_inc(biases, 1)
            a.activation(mu1[:], mu, ACT.Copy, scale=-1.0, bias=1.0).then_inc(biases, 1)
            a.wait_ge(biases, 2)
            a.wait_ge(setup, 6)

            def project(t, woven_in):
                for k in range(2):
                    t.w(aten, f"x_transposed{k}")
                    t.mark(a.activation(xT[:, 4 * k:4 * k + 4, :], b4[k], ACT.Copy), f"xT{k}")
                yield
                t.w(avec, "pr_edge")
                for k in range(4):
                    n = min(4, NPR - 4 * k)
                    t.w(aten, f"pr_proj{k}")
                    t.mark(a.activation(pr[:, 4 * k:4 * k + n, 1:P + 1], b4[(2, 3, 0, 1)[k]][:, 0:n, :], ACT.Copy), f"pr{k}")
                    yield
                t.w(aact, "pr3")
                t.left(edge_out)
                a.activation(edge[:, 0, :], pr[:, :, DEC], ACT.Copy)
                t.mark(a.activation(edge[:, 1, :], pr[:, :, P], ACT.Copy), "edges")
                t.w(aten, "cq_proj")
                t.mark(a.activation(sq5[:, 0:3, :], b4[2][:, 0:3, :], ACT.Square), "cq_sq")
                t.w(aten, "ckv_proj")
                t.mark(a.activation(sq5[:, 3:5, :], b4[3][:, 0:2, :], ACT.Square), "ckv_sq")
                t.w(aten, "rms_sums")
                t.w0(avec, "ckv_normed")
                t.mark(a.activation(msr[:], b4[3][:, 2:4, :], ACT.Sqrt, bias=par[:, 48:49]), "rms_root")
                yield
                t.w(aten, "q_nope")
                t.left(mla_out)
                t.mark(a.activation(qn[:], b4[2], ACT.Copy), "q_nope")
                yield
                t.w(aten, "ckv_tokens")
                t.mark(a.activation(ckt[:], bank[2][:, 0:KVL + ROPE], ACT.Copy), "ckv_tokens")

            def rwkv(t, woven_in):
                t.w(aact, "edges")
                for name, c0, c1 in (("low", 12, 14), ("k", 4, 8), ("r", 0, 4), ("v", 8, 12)):
                    if name == "low":
                        t.w0(vec, "gated")
                        t.w0(ten, "b_tokens")
                        t.w0(pol, "rk")
                    for c in range(c0, c1):
                        ins = a.activation(u[:, c, :], pr[:, c, 1:P + 1], ACT.Copy, scale=mu1[:, c:c + 1])
                    t.mark(ins, "u_own_" + name)
                t.w(vec, "u_low")
                t.w0(ten, "lora_g")
                a.activation(lo[0:64, :], u[0:64, 12, :], ACT.Tanh)
                t.do(a.activation(sg[:], u[:, 13, :], ACT.Tanh, scale=0.5), "g_lo")
                yield
                t.w(ten, "lora_w")
                t.w(avec, "q_roped")
                for c in range(4):
                    ins = a.activation(lw[:, c, :], b4[4][:, c, :], ACT.Tanh, bias=negh[:, c:c + 1], scale=0.5)
                t.mark(ins, "w_tanh")
                t.w(ten, "lora_a")
                for c in range(4):
                    ins = a.activation(aa[:, c, :], b4[5][:, c, :], ACT.Tanh, bias=negh[:, 4 + c:5 + c], scale=0.5)
                t.mark(ins, "a_tanh")
                t.w(vec, "kk")
                t.mark(a.activation(t1[:], kk[:], ACT.Square), "kk_sq")
                t.w(ten, "lora_g")
                t.mark(a.activation(gg[:], b4[6], ACT.Copy), "g_out")
                t.w(vec, "mid")
                t.w0(pol, "r_hat")
                for c in range(4):
                    ins = a.activation(ep[:, c, :], cum[:, c, :], ACT.Exp, bias=nm[:, c:c + 1])
                t.mark(ins, "exp_pos")
                for c in range(4):
                    ins = a.activation(en[:, c, :], cum[:, c, :], ACT.Exp, bias=cum[:, c, 64:65], scale=-1.0)
                t.do(ins, "exp_neg")
                t.mark(a.activation(em[:], en[:, :, 0], ACT.Copy), "em")
                yield
                t.w(vec, "kk_norm2")
                t.mark(a.activation(t1[:], t1[:], ACT.Sqrt), "kk_root")
                yield
                t.w(ten, "v_tokens")
                t.mark(a.activation(vt[:], b4[4], ACT.Copy), "v_tokens")
                t.w(ten, "U0")
                t.w0(vec, f"U{LEVELS}_1")
                for c in range(2):
                    ins = a.activation(U[:, 4 * c:4 * c + 4, :], b4[6 + c], ACT.Copy)
                t.mark(ins, "U0")
                yield
                t.w(ten, "b_tokens")
                t.mark(a.activation(bt, b4[0], ACT.Copy), "b_tokens")
                t.w(ten, "k_tokens")
                t.mark(a.activation(kt, b4[1], ACT.Copy), "k_tokens")
                t.w(ten, "G")
                t.mark(a.activation(Gs, bank[2][:, :], ACT.Copy), "G")
                t.w(ten, "SA")
                t.mark(a.activation(SA, bank[3][:, :], ACT.Copy), "SA")
                t.w(ten, "y")
                t.left(rwkv_out)
                t.mark(a.activation(ys[:], b4[4], ACT.Copy), "y")
                t.w(vec, "y_centred")
                t.mark(a.activation(yq, ys[:], ACT.Square), "y_sq")
                t.w(ten, "y_var")
                t.mark(a.activation(yq, b4[7], ACT.Sqrt, bias=par[:, 49:50]), "y_root")
                t.w(vec, "y_normed")
                for c in range(4):
                    ins = a.activation(ys[:, c, :], ys[:, c, :], ACT.Identity, bias=lxb[:, c:c + 1], scale=lxg[:, c:c + 1])
                t.mark(ins, "y_gain")

            woven(a, NT, aact, act, project, rwkv, ACT_ORDER)

        @block.tensor
        def _(pe):
            pe.wait_ge(consts.sem, consts.done(0))
            pe.wait_ge(setup, 6)

            def proj(dst, col, n=P):
                for k in range(KC):
                    ins = pe.matmul(dst, w_in[:, k, col:col + n], xT[:, k, :], start=(k == 0), stop=(k == KC - 1))
                return ins

            def project(t, woven_in):
                t.arrived(x_in)
                for k in range(2):
                    for c in range(4):
                        ins = pe.transpose(b4[k][:, c, :], x[:, (4 * k + c) * P:(4 * k + c + 1) * P], ident[:, :])
                    t.mark(ins, f"x_transposed{k}")
                t.w(aact, "xT1")
                for k in range(4):
                    if k == 3:
                        t.w(aact, "pr0")
                    for c in range(min(4, NPR - 4 * k)):
                        ins = proj(b4[(2, 3, 0, 1)[k]][:, c, :], QL + KVL + (4 * k + c) * P)
                    t.mark(ins, f"pr_proj{k}")
                    yield
                t.w(aact, "pr1")
                for c in range(CQ):
                    proj(b4[2][:, c, :], c * P)
                t.mark(proj(b4[2][0:64, 3, :], WCOL - 64, 64), "cq_proj")
                for c in range(CKV):
                    ins = proj(b4[3][:, c, :], QL + c * P)
                t.mark(ins, "ckv_proj")
                t.w(aact, "ckv_sq")
                for c in range(CQ):
                    pe.matmul(b4[3][:, 2, :], rmsw[:, 0, :], sq5[:, c, :], start=(c == 0), stop=(c == CQ - 1))
                for c in range(CKV):
                    ins = pe.matmul(b4[3][:, 3, :], rmsw[:, 1, :], sq5[:, CQ + c, :], start=(c == 0), stop=(c == CKV - 1))
                t.mark(ins, "rms_sums")
                yield
                t.w(avec, "kpe_roped")
                for c in range(4):
                    for k in range(CQ):
                        ins = pe.matmul(b4[2][:, c, :], w_uq[:, k, c * P:(c + 1) * P], cq[:, k, :],
                                        start=(k == 0), stop=(k == CQ - 1))
                    if c == 1:
                        yield
                t.mark(ins, "q_nope")
                yield
                for c in range(4):
                    for k in range(CQ):
                        ins = pe.matmul(b4[3][:, c, :], w_uq[:, k, 512 + c * P:512 + (c + 1) * P], cq[:, k, :],
                                        start=(k == 0), stop=(k == CQ - 1))
                    if c == 1:
                        yield
                t.mark(ins, "q_pe")
                yield
                t.w(aact, "q_nope")
                for c in range(CKV):
                    pe.transpose(bank[2][:, c * P:(c + 1) * P], ckv[:, c, :], ident[:, :])
                t.mark(pe.transpose(bank[2][:, KVL:KVL + ROPE], kpe[:], ident[0:32, 0:32]), "ckv_tokens")

            def rwkv(t, woven_in):
                t.w(act, "g_lo")
                t.w(vec, "g_sig")
                for c in range(4):
                    ins = pe.matmul(b4[4][:, c, :], w_wa[:, 0, c * P:(c + 1) * P], lo[:], start=True, stop=True)
                t.mark(ins, "lora_w")
                for c in range(4):
                    ins = pe.matmul(b4[5][:, c, :], w_wa[:, 1, c * P:(c + 1) * P], lo[:], start=True, stop=True)
                t.mark(ins, "lora_a")
                for c in range(4):
                    ins = pe.matmul(b4[6][:, c, :], w_g[:, c * P:(c + 1) * P], sg[:], start=True, stop=True)
                t.mark(ins, "lora_g")
                yield
                t.w(act, "kk_sq")
                t.mark(pe.matmul(bank[7][:, :], bones, t1[:].rearrange("p a n -> p (a n)"), start=True, stop=True),
                       "kk_norm")
                yield
                t.w(act, "w_tanh")
                t.w(vec, "u_v")
                for c in range(4):
                    ins = pe.transpose(b4[4][:, c, :], u[:, 8 + c, :], ident[:, :])
                t.mark(ins, "v_tokens")
                t.w(pol, "rkr")
                t.w(act, "g_out")
                t.mark(pe.matmul(bank[5][:, :], bones, t1[:].rearrange("p a n -> p (a n)"), start=True, stop=True),
                       "bonus_sum")
                t.w(vec, "b_hat")
                for g in range(2):
                    for h in range(4):
                        hh = 4 * g + h
                        ins = pe.matmul(b4[6 + g][:, h, :], AR[:, hh // 2, hh % 2, 0, :], bh[:, hh // 2, :],
                                        start=True, stop=True)
                    t.mark(ins, f"gram_l{g}")
                t.w(act, "v_tokens")
                t.w(vec, "bonus")
                for g in range(2):
                    for h in range(4):
                        hh = 4 * g + h
                        ins = pe.matmul(b4[4 + g][:, h, :], bh[:, hh // 2, :], AR[:, hh // 2, hh % 2, 1, :],
                                        start=True, stop=True)
                    t.mark(ins, f"gram_b{g}")
                if woven_in:
                    t.next_done(aact, "edges")
                for q in range(4):
                    b = (0, 1, 4, 5)[q]
                    if q == 2:
                        t.w(vec, "RB1")
                    for h in range(2):
                        ins = pe.matmul(bank[b][:, h * 256:(h + 1) * 256], kh[:, q, :],
                                        AR[:, q, h].rearrange("p a n -> p (a n)"), start=True, stop=True)
                    t.mark(ins, f"gram_k{q}")
                t.w(pol, "T_start1")
                t.w(vec, "L1")
                for h in range(H):
                    ins = pe.transpose(b4[6 + h // 4][:, h % 4, :], T[:, h, :], ident[:, :])
                t.mark(ins, "U0")
                yield
                for lev in range(1, LEVELS + 1):
                    n = 64
                    for g in range(2):
                        if lev == 1:
                            if g == 0:
                                t.w(act, "U0")
                                t.w(vec, "MK3")
                        else:
                            t.w(vec, f"U{lev - 1}_{g}")
                        for h in range(4):
                            ins = pe.matmul(bank[4 + g][:, h * n:(h + 1) * n], L[:, 4 * g + h, :],
                                            odd(U[:, 4 * g + h:4 * g + h + 1, :], lev), start=True, stop=True)
                        t.mark(ins, f"Z{lev}_{g}")
                    for g in range(2):
                        t.w(vec, f"Z{lev}_{g}")
                        for h in range(4):
                            ins = pe.matmul(bank[6 + g][:, h * n:(h + 1) * n], T[:, 4 * g + h, :],
                                            odd(Z[:, 4 * g + h:4 * g + h + 1, :], lev), start=True, stop=True)
                        t.mark(ins, f"U{lev}_{g}")
                        if lev < LEVELS:
                            if g == 0:
                                t.w(pol, f"Z_clear{lev}")
                            for h in range(4):
                                ins = pe.matmul(bank[g][:, h * n:(h + 1) * n], Z[:, 4 * g + h, :],
                                                even(T[:, 4 * g + h:4 * g + h + 1, :], lev), start=True, stop=True)
                            t.mark(ins, f"T{lev}_{g}")
                    yield
                for c in range(4):
                    ins = pe.transpose(b4[0][:, c, :], bh[:, c, :], ident[:, :])
                t.mark(ins, "b_tokens")
                for c in range(4):
                    ins = pe.transpose(b4[1][:, c, :], kh[:, c, :], ident[:, :])
                t.mark(ins, "k_tokens")
                if woven_in:
                    t.next_done(aact, "ckv_tokens")
                    t.next_done(avec, "q_roped")
                for h in range(H):
                    q, hs = h // 2, slice(h % 2 * 64, h % 2 * 64 + 64)
                    o = bank[2][:, h * 64:h * 64 + 64]
                    pe.matmul(o, AR[:, q, h % 2, 0, :], Sp[:, q, :], start=True, stop=False)
                    ins = pe.matmul(o, MK[:, h, 0, :], vt[:, q, hs], start=False, stop=True)
                t.mark(ins, "G")
                t.w(act, "G")
                t.w(vec, f"U{LEVELS}_1")
                for h in range(H):
                    ins = pe.matmul(bank[3][:, h * 64:h * 64 + 64], U[:, h, :], Gs[:, h * 64:h * 64 + 64],
                                    start=True, stop=True)
                t.mark(ins, "SA")
                t.w(act, "SA")
                for h in range(H):
                    q, hs = h // 2, slice(h % 2 * 64, h % 2 * 64 + 64)
                    o = b4[4][hs, q, :]
                    pe.matmul(o, Sp[:, q, :], AR[:, q, h % 2, 1, :], start=True, stop=False)
                    pe.matmul(o, SA[:, h * 64:h * 64 + 64], RB[:, h, :], start=False, stop=False)
                    ins = pe.matmul(o, vt[:, q, hs], MK[:, h, 1, :], start=False, stop=True)
                t.mark(ins, "y")
                for h in range(H):
                    q, hs = h // 2, slice(h % 2 * 64, h % 2 * 64 + 64)
                    o = bank[5][hs, q * 64:q * 64 + 64]
                    pe.matmul(o, bt[:, q, hs], SA[:, h * 64:h * 64 + 64], start=True, stop=False)
                    ins = pe.matmul(o, kt[:, q, hs], vt[:, q, hs], start=False, stop=True)
                t.mark(ins, "state_add")
                t.w(act, "y")
                t.mark(pe.matmul(bank[6][:, :], bmean, ys[:].rearrange("p a n -> p (a n)"), start=True, stop=True),
                       "y_mean")
                t.w(act, "y_sq")
                t.mark(pe.matmul(b4[7], bmean, yq, start=True, stop=True), "y_var")
                t.w(act, "y_root")

            woven(pe, NT, aten, ten, project, rwkv, PE_ORDER)

        @block.vector
        def _(v):
            v.wait_ge(consts.sem, consts.done(0))
            v.wait_ge(biases, 2)
            v.wait_ge(setup, 6)

            def project(t, woven_in):
                do = t.do
                t.arrived(a_in)
                t.w0(aact, "edges")
                do(v.scalar_tensor_tensor(out=pr[:, :, 0], in0=pr[:, :, P], scalar=keep, in1=shift0,
                                          op0=ALU.mult, op1=ALU.add), "pr_edge")
                yield
                t.w(aact, "rms_root")
                do(v.reciprocal(msr[:], msr[:]), "rms")
                t.w0(aten, "q_pe")
                for c in range(CQ):
                    ins = v.scalar_tensor_tensor(out=cq[:, c, :], in0=b4[2][:, c, :], scalar=qg[:, c:c + 1],
                                                 in1=msr[:, 0, :], op0=ALU.mult, op1=ALU.mult)
                do(ins, "cq_normed")
                t.left(mla_out)
                for c in range(CKV):
                    ins = v.scalar_tensor_tensor(out=ckv[:, c, :], in0=b4[3][:, c, :], scalar=kvg[:, c:c + 1],
                                                 in1=msr[:, 1, :], op0=ALU.mult, op1=ALU.mult)
                do(ins, "ckv_normed")
                do(v.tensor_tensor(kpe2[0:32, :], b4[2][0:32, 3, :], rope[0:32, 0, :], ALU.mult), "kpe_cos")
                do(v.tensor_tensor(kpe[:], b4[2][32:64, 3, :], rope[32:64, 1, :], ALU.mult), "kpe_sin")
                do(v.tensor_tensor(kpe[:], kpe[:], kpe2[0:32, :], ALU.add), "kpe_roped")
                yield
                t.w(aten, "q_pe")
                do(v.tensor_tensor(qp[:], b4[3][:, 0:2, :], bm(rope[:, 0, :], 2), ALU.mult), "q_rope_cos")
                do(v.tensor_tensor(qr, b4[3][:, 2:4, :], bm(rope[:, 1, :], 2), ALU.mult), "q_rope_sin")
                do(v.tensor_tensor(qp[:], qp[:], qr, ALU.add), "q_roped")

            def rwkv(t, woven_in):
                do = t.do
                for name, c0, c1 in (("low", 12, 14), ("k", 4, 8), ("r", 0, 4), ("v", 8, 12)):
                    t.w(act, "u_own_" + name)
                    for c in range(c0, c1):
                        ins = v.scalar_tensor_tensor(out=u[:, c, :], in0=pr[:, c, 0:P], scalar=mu[:, c:c + 1],
                                                     in1=u[:, c, :], op0=ALU.mult, op1=ALU.add)
                    do(ins, "u_" + name)
                    if name == "low":
                        t.w0(ten, "lora_a")
                        t.mark(v.tensor_copy(lo[64:128, :], u[64:128, 12, :]), "a_lo")
                    if name == "k":
                        t.w(act, "g_lo")
                        t.mark(v.tensor_scalar(sg[:], sg[:], 0.5, 0.5, ALU.mult, ALU.add), "g_sig")
                        do(v.tensor_tensor(kk[:], u[:, 4:8, :], bc(kkc, P), ALU.mult), "kk")
                yield
                t.arrived(b_in)
                t.w(act, "w_tanh")
                do(v.scalar_tensor_tensor(out=lw[:], in0=lw[:], scalar=1.0, in1=bm(vm, 4), op0=ALU.add, op1=ALU.mult),
                   "log_w")
                for c in range(4):
                    ins = v.tensor_tensor_scan(cum[:, c, 1:P + 1], ones[:], lw[:, c, :], 0.0, ALU.mult, ALU.add)
                do(ins, "cum")
                do(v.tensor_scalar(nm[:], cum[:, :, 64], -1.0, None, ALU.mult), "mid")
                t.w(act, "a_tanh")
                do(v.tensor_scalar(aa[:], aa[:], 0.5, 0.5, ALU.mult, ALU.add), "a_sig")
                do(v.scalar_tensor_tensor(out=kh[:], in0=aa[:], scalar=-1.0, in1=bc(kac, P), op0=ALU.add, op1=ALU.mult),
                   "a_ka")
                do(v.scalar_tensor_tensor(out=kh[:], in0=kh[:], scalar=1.0, in1=u[:, 4:8, :], op0=ALU.add, op1=ALU.mult),
                   "kh")
                t.w(ten, "kk_norm")
                do(v.tensor_scalar(t1[:], b4[7], 1e-24, None, ALU.max), "kk_norm2")
                t.w(act, "kk_root")
                do(v.reciprocal(t1[:], t1[:]), "kk_rs")
                do(v.tensor_tensor(kk[:], kk[:], t1[:], ALU.mult), "kk_normed")
                for h in range(2):
                    hs = slice(h * 64, h * 64 + 64)
                    ins = v.scalar_tensor_tensor(out=AR[hs, :, h, 0, :], in0=kk[hs], scalar=-1.0, in1=ep[hs, :, 0:P],
                                                 op0=ALU.mult, op1=ALU.mult)
                do(ins, "a_hat")
                do(v.tensor_tensor(en[:, :, 1:P + 1], en[:, :, 1:P + 1], bm(valid, 4), ALU.mult), "en_masked")
                do(v.tensor_tensor(bh, kk[:], aa[:], ALU.mult), "b_gate")
                do(v.tensor_tensor(bh, bh, en[:, :, 1:P + 1], ALU.mult), "b_hat")
                t.w(pol, "rk")
                do(v.tensor_tensor(kh[:], kh[:], en[:, :, 1:P + 1], ALU.mult), "k_hat")
                yield
                t.w(ten, "bonus_sum")
                do(v.tensor_tensor(bon[:], b4[5], u[:, 8:12, :], ALU.mult), "bonus")
                for g in range(2):
                    hs = slice(4 * g, 4 * g + 4)
                    t.w(ten, f"gram_l{g}")
                    v.tensor_tensor(L[:, hs, :], b4[6 + g], bm(low, 4), ALU.mult)
                    t.mark(v.tensor_tensor(T[:, hs, :], b4[6 + g], bm(lev0T, 4), ALU.mult), f"T_level0_{g}")
                t.mark(v.tensor_copy(spare[:], nm[:, 0:1]), "L1")
                for g in range(2):
                    hs = slice(4 * g, 4 * g + 4)
                    t.w(ten, f"gram_b{g}")
                    t.mark(v.tensor_tensor(RB[:, hs, :], b4[4 + g], bm(incl, 4), ALU.mult), f"RB{g}")
                t.left(state_out)
                do(v.scalar_tensor_tensor(out=S[:], in0=S[:], scalar=keep_s[:, 0:1], in1=s_init[:], op0=ALU.mult,
                                          op1=ALU.add), "state_in")
                t.w(act, "em")
                do(v.tensor_tensor(Sp[:], S[:], bc(em[:], VD), ALU.mult), "state_mid")
                for q in range(4):
                    t.w(ten, f"gram_k{q}")
                    g4 = bank[(0, 1, 4, 5)[q]][:, :].rearrange("p (h a n) -> p h a n", h=2, a=2)
                    t.mark(v.tensor_tensor(MK[:, 2 * q:2 * q + 2], g4, upper2.unsqueeze(1).to_broadcast([P, 2, 2, P]),
                                           ALU.mult), f"MK{q}")
                yield
                for lev in range(1, LEVELS + 1):
                    def view(b):
                        return b[:, 0:256].rearrange("p (h k b) -> p h k b", h=4, b=2 ** lev)

                    mask = levs[:, lev - 1, :].rearrange("p (k b) -> p k b", b=2 ** lev)
                    mask = mask.unsqueeze(1).to_broadcast([P, 4, mask.shape[1], mask.shape[2]])
                    for g in range(2):
                        hs = slice(4 * g, 4 * g + 4)
                        t.w(ten, f"Z{lev}_{g}")
                        t.mark(v.tensor_tensor(odd(Z[:, hs, :], lev), view(bank[4 + g]), mask, ALU.mult), f"Z{lev}_{g}")
                    for g in range(2):
                        hs = slice(4 * g, 4 * g + 4)
                        t.w(ten, f"U{lev}_{g}")
                        o = odd(U[:, hs, :], lev)
                        t.mark(v.tensor_tensor(o, view(bank[6 + g]), o, ALU.add), f"U{lev}_{g}")
                        if lev < LEVELS:
                            t.w(ten, f"T{lev}_{g}")
                            e = even(T[:, hs, :], lev)
                            t.mark(v.tensor_tensor(e, view(bank[g]), e, ALU.add), f"T{lev}_{g}")
                    yield
                t.w(ten, "state_add")
                do(v.tensor_tensor(S[:], bank[5][:, 0:256].rearrange("p (a n) -> p a n", a=4), Sp[:], ALU.add),
                   "state_sum")
                do(v.tensor_tensor(S[:], S[:], ep[:, :, P:P + 1].to_broadcast([P, 4, VD]), ALU.mult), "state")
                t.w(ten, "y_mean")
                do(v.tensor_tensor(ys[:], ys[:], b4[6], ALU.subtract), "y_centred")
                t.w(act, "y_root")
                do(v.reciprocal(yq, yq), "y_rs")
                do(v.tensor_tensor(ys[:], ys[:], yq, ALU.mult), "y_normed")
                t.w(act, "y_gain")
                do(v.tensor_tensor(ys[:], ys[:], bon[:], ALU.add), "y_bonus")
                do(v.tensor_tensor(ys[:], ys[:], gg[:], ALU.mult), "gated")

            woven(v, NT, avec, vec, project, rwkv, VEC_ORDER)


def attention(nc, io, scr):
    KT = SEQ // P + 2
    with ExitStack() as ctx:
        def sb(name, shape, dt=F32):
            return ctx.enter_context(nc.sbuf_tensor("at_" + name, shape, dt))

        bank = [ctx.enter_context(nc.psum_tensor(f"at_bank{b}", [P, 512], F32)) for b in range(8)]
        ident = sb("ident", [P, P])
        lat = sb("lat", [P, CKV, KT * P])
        kT = sb("kT", [P, KT * P])
        qT = sb("qT", [P, TOK])
        w = sb("w", [P, CKV, P])
        vals = sb("vals", [P, KT, VD + 1])
        mx = sb("mx", [P, 5])
        nm = sb("nm", [P, NT])
        rec = sb("rec", [P, 1])
        zero = sb("zero", [P, 64])
        NPT = 3
        PT = sb("PT", [P, NPT, 4, P])
        o_sb = sb("o_sb", [P, NT, VD])

        ten, vec, act, pol = (Steps(nc, ctx, "attention_" + n) for n in ("tensor", "vector", "scalar", "gpsimd"))
        latents = Dmas(nc, ctx, "at_latents", 7)
        setup = ctx.enter_context(nc.semaphore("at_setup"))
        w_in = Dmas(nc, ctx, "at_w_in", 1)
        q_in = Dmas(nc, ctx, "at_q_in", 1)
        o_out = Dmas(nc, ctx, "at_o_out", 1, 1)
        block = ctx.enter_context(nc.Block())

        def groups(j):
            if j == NT - 1:
                return [(KT - 2, 2, DEC)]
            return [(k, min(4, j + 1 - k), P) for k in range(0, j + 1, 4)]

        chunks = [(j, g) for j in range(NT) for g in range(len(groups(j)))]
        order = {c: n for n, c in enumerate(chunks)}

        @block.sync
        def _(sp):
            n = SEQ
            lt = scr["ckvT"].rearrange("(c p) n -> p c n", p=P)
            sp.dma_start(lat[:, :, 0:n], lt[:, :, 0:n]).then_inc(latents.sem, 16)
            sp.dma_start(lat[:, :, n:n + P], io["past_ckvT"].rearrange("p (c n) -> p c n", c=CKV)).then_inc(latents.sem, 16)
            sp.dma_start(lat[:, :, n + P:n + 2 * P], lt[:, :, n:n + P]).then_inc(latents.sem, 16)
            sp.dma_start(kT[NOPE:QK, 0:n], scr["kpeT"][:, 0:n]).then_inc(latents.sem, 16)
            sp.dma_start(kT[NOPE:QK, n:n + P], io["past_kpeT"]).then_inc(latents.sem, 16)
            sp.dma_start(kT[NOPE:QK, n + P:n + 2 * P], scr["kpeT"][:, n:n + P]).then_inc(latents.sem, 16)
            sp.dma_start(ident[:], io["ident"]).then_inc(latents.sem, 16)
            sp.sem_inc(o_out.sem, 16)

            def turn(t):
                t.ahead((ten, "V2", -1), (vec, "out_16", 0), (ten, "ST16_0", -1))
                hs = bass.ds(sp.snap(t.i * VD), VD)
                t.w0(ten, "V2")
                w_in.go(sp.dma_start(w[:], io["w_ukv"][bass.ds(t.i, 1)].rearrange("a p (c n) -> p (a c) n", c=CKV)))
                t.w0(ten, "ST16_0")
                q_in.go(sp.dma_start(qT[0:QK, :], scr["qT"][bass.ds(t.i, 1)].rearrange("a d n -> d (a n)")))
                t.w(vec, "out_16")
                o_out.go(sp.dma_start(scr["attn"].rearrange("(t p) c -> p t c", p=P)[:, :, hs], o_sb[:]))

            engine_loop(sp, None, H, turn)
            sp.wait_ge(o_out.sem, o_out.done(H - 1))

        @block.gpsimd
        def _(g):
            g.memset(kT[QK:QK + 1, :], 1.0).then_inc(setup, 1)
            g.wait_ge(setup, 1)
            g.memset(vals[:], 1.0).then_inc(setup, 1)
            g.memset(mx[:], -3e38).then_inc(setup, 1)
            g.memset(zero[:], 0.0).then_inc(setup, 1)
            g.wait_ge(setup, 4)

            def turn(t):
                for j in range(NT - 1):
                    gi = len(groups(j)) - 1
                    t.w(act, f"exp{j}_{gi}")
                    k0, k, _ = groups(j)[gi]
                    s = order[j, gi] % NPT
                    t.mark(g.tensor_tensor(PT[64:P, s, k - 1, 0:64], zero[64:P, :], zero[64:P, :], ALU.add), f"hidden{j}")

            engine_loop(g, pol, H, turn)

        @block.scalar
        def _(a):
            a.wait_ge(setup, 4)

            def turn(t):
                for n in range(5):
                    t.w(ten, f"K{n}")
                    wd = min(512, KT * P - 512 * n)
                    t.mark(a.activation(kT[0:NOPE, 512 * n:512 * n + wd], bank[n][0:NOPE, 0:wd], ACT.Copy), f"K{n}")
                for j, gi in chunks:
                    k0, k, last = groups(j)[gi]
                    n = order[j, gi]
                    t.w(ten, f"ST{j}_{gi}")
                    b = bank[3 + n % 3]
                    if last == P:
                        ins = a.activation(PT[:, n % NPT, 0:k, :], b[:, 0:k * P].rearrange("p (a n) -> p a n", a=k),
                                           ACT.Exp, scale=SCALE)
                    else:
                        a.activation(PT[:, n % NPT, 0, :], b[:, 0:P], ACT.Exp, scale=SCALE)
                        ins = a.activation(PT[0:last, n % NPT, 1, :], b[0:last, P:2 * P], ACT.Exp, scale=SCALE)
                    t.mark(ins, f"exp{j}_{gi}")

            engine_loop(a, act, H, turn)

        @block.tensor
        def _(pe):
            pe.wait_ge(latents.sem, latents.done(0))
            pe.wait_ge(setup, 4)

            def scores(t, j):
                for gi, (k0, k, last) in enumerate(groups(j)):
                    n = order[j, gi]
                    if n >= 3:
                        pj, pg = chunks[n - 3]
                        t.w(vec, f"max{pj}_{pg}")
                    wd = (k - 1) * P + last
                    t.mark(pe.matmul(bank[n % 3][:, 0:wd], qT[0:QK, j * P:(j + 1) * P], kT[0:QK, k0 * P:k0 * P + wd],
                                     start=True, stop=True), f"S{j}_{gi}")

            def turn(t):
                t.arrived(w_in)
                t.w0(vec, "out_16")
                t.w0(act, "exp16_0")
                for n in range(5):
                    wd = min(512, KT * P - 512 * n)
                    for c in range(CKV):
                        ins = pe.matmul(bank[n][0:NOPE, 0:wd], w[:, c, 0:NOPE], lat[:, c, 512 * n:512 * n + wd],
                                        start=(c == 0), stop=(c == CKV - 1))
                    t.mark(ins, f"K{n}")
                for n in range(3):
                    b = bank[5 + n]
                    for k in range(8 * n, min(8 * n + 8, KT)):
                        for c in range(CKV):
                            ins = pe.matmul(b[:, (k % 8) * VD:(k % 8 + 1) * VD], lat[:, c, k * P:(k + 1) * P],
                                            w[:, c, NOPE:P], start=(c == 0), stop=(c == CKV - 1))
                    t.mark(ins, f"V{n}")
                t.w(act, "K4")
                t.w(vec, "V2")
                t.arrived(q_in)
                scores(t, 0)
                scores(t, 1)
                for j in range(NT):
                    gs = groups(j)
                    t.w(vec, f"negmax{j}")
                    t.mark(pe.matmul(bank[7][QK:QK + 1, 0:P], nm[:, j:j + 1], ident[:, :], start=True, stop=True), f"maxrow{j}")
                    if j + 2 < NT:
                        scores(t, j + 2)
                    t.w(vec, f"maxrow{j}")

                    def pv(gi):
                        k0, k, last = gs[gi]
                        n = order[j, gi]
                        if gi == 0 and j >= 2:
                            t.w(vec, f"out_{j - 2}")
                        t.w(act, f"exp{j}_{gi}")
                        if last == P and gi == len(gs) - 1:
                            t.w(pol, f"hidden{j}")
                        for s in range(k):
                            rows = last if s == k - 1 else P
                            ins = pe.matmul(bank[6][:, 256 * (j % 2):256 * (j % 2) + VD + 1], PT[0:rows, n % NPT, s, :],
                                            vals[0:rows, k0 + s, :], start=(gi == 0 and s == 0),
                                            stop=(gi == len(gs) - 1 and s == k - 1))
                        t.mark(ins, f"PV{j}_{gi}")

                    for gi, (k0, k, last) in enumerate(gs):
                        n = order[j, gi]
                        if n >= 3:
                            pj, pg = chunks[n - 3]
                            t.w(act, f"exp{pj}_{pg}")
                        for s in range(k):
                            rows = last if s == k - 1 else P
                            c0 = (k0 + s) * P
                            ins = pe.matmul(bank[3 + n % 3][0:rows, s * P:(s + 1) * P], kT[0:QK + 1, c0:c0 + rows],
                                            qT[0:QK + 1, j * P:(j + 1) * P], start=True, stop=True)
                        t.mark(ins, f"ST{j}_{gi}")
                        if gi >= 1:
                            pv(gi - 1)
                    pv(len(gs) - 1)

            engine_loop(pe, ten, H, turn)

        @block.vector
        def _(v):
            v.wait_ge(setup, 4)

            def maxima(t, j):
                gs = groups(j)
                for gi, (k0, k, last) in enumerate(gs):
                    n = order[j, gi]
                    t.w(ten, f"S{j}_{gi}")
                    b = bank[n % 3]
                    wd = (k - 1) * P + last
                    if gi == len(gs) - 1 and j < NT - 1:
                        v.tensor_reduce(mx[64:P, 0:1], b[64:P, wd - 64:wd], AX.X, ALU.max)
                        wd -= 64
                    elif gi == 0 and j == NT - 1:
                        v.tensor_reduce(mx[64:P, 0:1], b[64:P, 0:64], AX.X, ALU.max)
                    t.mark(v.tensor_reduce(mx[:, 1 + gi:2 + gi], b[:, 0:wd], AX.X, ALU.max), f"max{j}_{gi}")
                t.w(vec, f"max{j}_{len(gs) - 1}")
                t.do(v.tensor_reduce(nm[:, j:j + 1], mx[:, 0:1 + len(gs)], AX.X, ALU.max, negate=True), f"negmax{j}")

            def turn(t):
                for n in range(3):
                    t.w(ten, f"V{n}")
                    k = min(8, KT - 8 * n)
                    t.mark(v.tensor_copy(vals[:, 8 * n:8 * n + k, 0:VD],
                                         bank[5 + n][:, 0:k * VD].rearrange("p (a n) -> p a n", a=k)), f"V{n}")
                maxima(t, 0)
                maxima(t, 1)
                for j in range(NT):
                    t.w(ten, f"maxrow{j}")
                    t.mark(v.tensor_copy(qT[QK:QK + 1, j * P:(j + 1) * P], bank[7][QK:QK + 1, 0:P]), f"maxrow{j}")
                    if j + 2 < NT:
                        maxima(t, j + 2)
                    t.w(ten, f"PV{j}_{len(groups(j)) - 1}")
                    if j == 0:
                        t.left(o_out)
                    o = bank[6][:, 256 * (j % 2):256 * (j % 2) + VD + 1]
                    t.do(v.reciprocal(rec[:], o[:, VD:VD + 1]), f"sum_{j}")
                    t.mark(v.tensor_scalar(o_sb[:, j, :], o[:, 0:VD], rec[:, 0:1], None, ALU.mult), f"out_{j}")

            engine_loop(v, vec, H, turn)


def router(nc, io, scr, keep):
    oh, rank, gate, base = keep["onehot"], keep["rank"], keep["gate"], keep["counts"]
    with ExitStack() as ctx:
        def sb(name, shape, dt=F32):
            return ctx.enter_context(nc.sbuf_tensor("ro_" + name, shape, dt))

        bank = [ctx.enter_context(nc.psum_tensor(f"ro_bank{b}", [P, 512], F32)) for b in range(8)]
        b4 = [b[:, :].rearrange("p (a n) -> p a n", a=4) for b in bank]
        w_o = sb("w_o", [P, KC, D])
        w_r = sb("w_r", [P, KC, NR])
        rows = sb("rows", [P, 2, D])
        small = sb("small", [P, NR + NG + EPG])
        bias, prio4, prio8 = small[:, 0:NR], small[:, NR:NR + NG], small[:, NR + NG:]
        cst = sb("cst", [P, 3, P])
        ident = cst[:, 0, :]
        eps = sb("eps", [P, 1])
        vcol = sb("vcol", [P, NT])
        at = sb("at", [P, 512])
        mix = sb("mix", [P, KC, P])
        x = sb("x", [P, D])
        r = sb("r", [P, D])
        h = sb("h", [P, D])
        hT = sb("hT", [P, KC, P])
        st = sb("st", [P, 2, 6])
        mv = sb("mv", [P, 2])
        rstd = sb("rstd", [P, 1])
        lg = sb("lg", [P, NR])
        t36 = sb("t36", [P, NR])
        s1 = sb("s1", [P, 16])
        ohg = sb("ohg", [P, NG])
        ein = sb("ein", [P, EPG])
        e2 = sb("e2", [P, EPG])
        pr8 = sb("pr8", [P, EPG])
        o1 = sb("o1", [P, EPG])
        o2 = sb("o2", [P, EPG])
        ohs = sb("ohs", [P, 3, NE])
        ranks = sb("ranks", [P, NE])

        ten, vec, act = (Steps(nc, ctx, "router_" + n) for n in ("tensor", "vector", "scalar"))
        consts = Dmas(nc, ctx, "ro_consts", 7)
        zeroed = ctx.enter_context(nc.semaphore("ro_zeroed"))
        mix_in = Dmas(nc, ctx, "ro_mix_in", 2)
        x_in = Dmas(nc, ctx, "ro_x_in", 1)
        h_out = Dmas(nc, ctx, "ro_h_out", 1, 1)
        block = ctx.enter_context(nc.Block())

        @block.sync
        def _(sp):
            for dst, src, n in ((w_o, io["w_o"], KC), (w_r, io["w_r"], KC), (cst, io["cst3"], 3)):
                sp.dma_start(dst[:], src.rearrange("p (a n) -> p a n", a=n)).then_inc(consts.sem, 16)
            sp.dma_start(rows[:], io["ln1"].rearrange("(o a) n -> o a n", o=1).to_broadcast([P, 2, D])).then_inc(consts.sem, 16)
            sp.dma_start(small[:], io["small"].to_broadcast([P, NR + NG + EPG])).then_inc(consts.sem, 16)
            sp.dma_start(eps[:], io["eps"]).then_inc(consts.sem, 16)
            sp.dma_start(vcol[:], io["vcol"]).then_inc(consts.sem, 16)
            sp.sem_inc(h_out.sem, 16)

            def turn(t):
                t.ahead((ten, "attn_T", -1), (ten, "out_proj", -1), (vec, "residual", -1), (vec, "h", 0))
                col = bass.ds(sp.snap(t.i * P), P)
                one = bass.ds(sp.snap(t.i), 1)
                t.w0(ten, "out_proj")
                mix_in.go(sp.dma_start(at[:], scr["attn"][col, :]))
                mix_in.go(sp.dma_start(mix[:, 4:8, :], scr["rwT"].rearrange("(c p) n -> p c n", p=P)[:, :, col]))
                t.w0(vec, "residual")
                x_in.go(sp.dma_start(x[:], io["x"][one].rearrange("a p n -> p (a n)")))
                t.w(vec, "h")
                h_out.go(sp.dma_start(scr["h"][col, :], h[:]))

            engine_loop(sp, None, NT, turn)
            sp.wait_ge(h_out.sem, h_out.done(NT - 1))

        @block.scalar
        def _(a):
            a.wait_ge(consts.sem, consts.done(0))

            def turn(t):
                t.w(ten, "attn_T")
                t.mark(a.activation(mix[:, 0:4, :], b4[0], ACT.Copy), "attn_T")
                t.w(vec, "stats")
                t.mark(a.activation(rstd[:], mv[:, 1:2], ACT.Sqrt, bias=eps[:, 0:1]), "root")
                for k in range(2):
                    t.w(ten, f"h_T{k}")
                    t.mark(a.activation(hT[:, 4 * k:4 * k + 4, :], b4[3 + k], ACT.Copy), f"h_T{k}")
                t.w(vec, "group_max")
                t.mark(a.activation(t36[:, 0:NG], lg[:, 0:NG], ACT.Exp, bias=s1[:, 0:1], accum_out=s1[:, 1:2]), "group_exp")
                t.w(vec, "gap")
                t.mark(a.activation(s1[:, 8:9], s1[:, 7:8], ACT.Exp), "gap_exp")

            engine_loop(a, act, NT, turn)

        @block.tensor
        def _(pe):
            pe.wait_ge(consts.sem, consts.done(0))

            def turn(t):
                t.arrived(mix_in)
                for c in range(4):
                    ins = pe.transpose(b4[0][:, c, :], at[:, c * P:(c + 1) * P], ident)
                t.mark(ins, "attn_T")
                t.w(act, "attn_T")
                t.w0(vec, "residual")
                for n in range(2):
                    for k in (4, 5, 6, 7, 0, 1, 2, 3):
                        ins = pe.matmul(bank[1 + n][:, :], mix[:, k, :], w_o[:, k, n * 512:(n + 1) * 512],
                                        start=(k == 4), stop=(k == 3))
                t.mark(ins, "out_proj")
                t.w(vec, "h")
                for k in range(2):
                    for c in range(4):
                        ins = pe.transpose(b4[3 + k][:, c, :], h[:, (4 * k + c) * P:(4 * k + c + 1) * P], ident)
                    t.mark(ins, f"h_T{k}")
                t.w(act, "h_T1")
                for k in range(KC):
                    ins = pe.matmul(bank[5][:, 0:NR], hT[:, k, :], w_r[:, k, :], start=(k == 0), stop=(k == KC - 1))
                t.mark(ins, "logits")
                t.w(vec, "one_hots")
                pe.matmul(bank[6][:, 0:NE], cst[:, 1, :], ohs[:, 2, :], start=True, stop=True)
                t.mark(pe.matmul(bank[6][:, NE:2 * NE], cst[:, 2, :], ohs[:, 2, :], start=True, stop=True), "counts")

            engine_loop(pe, ten, NT, turn)

        @block.vector
        def _(v):
            v.wait_ge(consts.sem, consts.done(0))
            v.memset(base[:], 0.0).then_inc(zeroed, 1)
            v.wait_ge(zeroed, 1)

            def turn(t):
                do = t.do
                t.w(ten, "out_proj")
                t.arrived(x_in)
                for n in range(2):
                    s = slice(n * 512, n * 512 + 512)
                    ins = v.scalar_tensor_tensor(out=r[:, s], in0=x[:, s], scalar=ALPHA, in1=bank[1 + n][:, :],
                                                 op0=ALU.mult, op1=ALU.add)
                do(ins, "residual")
                for n in range(2):
                    ins = v.bn_stats(st[:, n, :], r[:, n * 512:n * 512 + 512])
                do(ins, "half_stats")
                v.tensor_copy(rstd[:], st[:, 0, 0:1])
                do(v.bn_aggr(mv[:], st[:]), "stats")
                t.w(act, "root")
                do(v.reciprocal(rstd[:], rstd[:]), "rstd")
                t.left(h_out)
                t.w0(ten, "h_T1")
                do(v.tensor_scalar(r[:], r[:], mv[:, 0:1], rstd[:, 0:1], ALU.subtract, ALU.mult), "normed")
                do(v.tensor_tensor(r[:], r[:], rows[:, 0, :], ALU.mult), "gain")
                do(v.tensor_tensor(h[:], r[:], rows[:, 1, :], ALU.add), "h")
                t.w(ten, "logits")
                do(v.tensor_tensor(lg[:], bank[5][:, 0:NR], bias, ALU.add), "logits")
                do(v.tensor_reduce(s1[:, 0:1], lg[:, 0:NG], AX.X, ALU.max, negate=True), "group_max")
                do(v.tensor_reduce(s1[:, 2:3], lg[:, 0:NG], AX.X, ALU.max), "group_max_pos")
                do(v.scalar_tensor_tensor(out=ohg[:], in0=lg[:, 0:NG], scalar=s1[:, 2:3], in1=prio4,
                                          op0=ALU.is_equal, op1=ALU.mult), "group_prio")
                do(v.tensor_reduce(s1[:, 3:4], ohg[:], AX.X, ALU.max), "group_prio_max")
                do(v.tensor_scalar(ohg[:], ohg[:], s1[:, 3:4], None, ALU.is_equal), "group_one_hot")
                t.w(act, "group_exp")
                do(v.reciprocal(s1[:, 1:2], s1[:, 1:2]), "group_prob")
                g8 = t36[:, NG:NR].rearrange("p (g e) -> p g e", g=NG)
                do(v.tensor_tensor(g8, lg[:, NG:NR].rearrange("p (g e) -> p g e", g=NG), bc(ohg[:], EPG), ALU.mult),
                   "in_group")
                do(v.tensor_reduce(ein[:], g8.rearrange("p g e -> p e g"), AX.X, ALU.add), "expert_logits")
                for n, (src, dst) in enumerate(((ein, o1), (e2, o2))):
                    m = s1[:, 4 + n:5 + n]
                    do(v.tensor_reduce(m, src[:], AX.X, ALU.max), f"top{n}")
                    do(v.scalar_tensor_tensor(out=pr8[:], in0=src[:], scalar=m, in1=prio8,
                                              op0=ALU.is_equal, op1=ALU.mult), f"top_prio{n}")
                    do(v.tensor_reduce(s1[:, 6:7], pr8[:], AX.X, ALU.max), f"top_prio_max{n}")
                    do(v.tensor_scalar(dst[:], pr8[:], s1[:, 6:7], None, ALU.is_equal), f"top_one_hot{n}")
                    if n == 0:
                        do(v.scalar_tensor_tensor(out=e2[:], in0=o1[:], scalar=-1e30, in1=ein[:],
                                                  op0=ALU.mult, op1=ALU.add), "without_first")
                do(v.tensor_tensor(s1[:, 7:8], s1[:, 5:6], s1[:, 4:5], ALU.subtract), "gap")
                t.w(act, "gap_exp")
                do(v.tensor_scalar(s1[:, 9:10], s1[:, 8:9], 1.0, None, ALU.add), "gate_sum")
                do(v.reciprocal(s1[:, 9:10], s1[:, 9:10]), "gate_rec")
                do(v.tensor_tensor(gate[:, bass.ds(t.i, 1)], s1[:, 9:10], s1[:, 1:2], ALU.mult), "gate0")
                do(v.tensor_tensor(s1[:, 10:11], s1[:, 8:9], s1[:, 9:10], ALU.mult), "gate1_share")
                do(v.tensor_tensor(gate[:, bass.ds(t.i + NT, 1)], s1[:, 10:11], s1[:, 1:2], ALU.mult), "gate1")
                t.w0(ten, "counts")
                do(v.tensor_scalar(ohg[:], ohg[:], vcol[:, bass.ds(t.i, 1)], None, ALU.mult), "group_valid")
                for n, o in enumerate((o1, o2)):
                    do(v.tensor_tensor(ohs[:, n, :].rearrange("p (g e) -> p g e", g=NG), bc(ohg[:], EPG),
                                       bm(o[:], NG), ALU.mult), f"one_hot{n}")
                do(v.tensor_tensor(ohs[:, 2, :], ohs[:, 0, :], ohs[:, 1, :], ALU.add), "one_hots")
                for n in range(2):
                    ins = v.tensor_copy(oh[:, bass.ds(t.i * NE + n * NT * NE, NE)], ohs[:, n, :])
                t.mark(ins, "one_hots_kept")
                t.w(ten, "counts")
                do(v.tensor_tensor(ranks[:], bank[6][:, 0:NE], base[:], ALU.add), "ranks")
                do(v.tensor_tensor(base[:], bank[6][:, NE:2 * NE], base[:], ALU.add), "counts")
                for n in range(2):
                    do(v.tensor_tensor(t36[:, 0:NE], ranks[:], ohs[:, n, :], ALU.mult), f"rank_of{n}")
                    do(v.tensor_reduce(rank[:, bass.ds(t.i + n * NT, 1)], t36[:, 0:NE], AX.X, ALU.add), f"rank{n}")

            engine_loop(v, vec, NT, turn)


def dispatch(nc, io, scr, keep):
    oh, rank, counts = keep["onehot"], keep["rank"], keep["counts"]
    table = scr["table"]
    with ExitStack() as ctx:
        def sb(name, shape, dt=F32):
            return ctx.enter_context(nc.sbuf_tensor("di_" + name, shape, dt))

        KB = SEQ // P + 1
        ps = ctx.enter_context(nc.psum_tensor("di_ps", [P, 512], F32))
        nums = sb("nums", [P, KB + NBLK])
        cols = sb("cols", [P, 3, NT])
        ident = sb("ident", [P, P])
        ones = sb("ones", [P, NE])
        cmp1 = sb("cmp1", [P, NE, KB])
        cmp2 = sb("cmp2", [P, NBLK, NE])
        blocks = sb("blocks", [P, NE])
        ends = sb("ends", [P, NE])
        starts = sb("starts", [P, NE])
        be, be4 = sb("be", [P, NBLK]), sb("be4", [P, NBLK])
        tmp = sb("tmp", [P, NT, NE])
        dest = sb("dest", [P, 2, NT])
        desti = sb("desti", [P, 2 * NT], I32)
        zero = sb("zero", [NBLK + 2, P])
        tok = sb("tok", [NBLK, P])

        vec = ctx.enter_context(nc.semaphore("di_vec"))
        consts = ctx.enter_context(nc.semaphore("di_consts"))
        cleared = ctx.enter_context(nc.semaphore("di_cleared"))
        scattered = ctx.enter_context(nc.semaphore("di_scattered"))
        tok_in = ctx.enter_context(nc.semaphore("di_tok_in"))
        turned = ctx.enter_context(nc.semaphore("di_turned"))
        DEST = 16
        block = ctx.enter_context(nc.Block())

        @block.sync
        def _(sp):
            sp.dma_start(nums[:], io["nums"].to_broadcast([P, KB + NBLK])).then_inc(consts, 16)
            sp.dma_start(cols[:], io["cols"].rearrange("p (a n) -> p a n", a=3)).then_inc(consts, 16)
            sp.dma_start(ident[:], io["ident"]).then_inc(consts, 16)
            sp.wait_ge(vec, 1)
            sp.dma_start(table.rearrange("(b p) o -> b (p o)", p=P), zero[:]).then_inc(cleared, 16)
            sp.wait_ge(scattered, 16 * 2 * NT)
            sp.dma_start(tok[:], table[0:NBLK * P].rearrange("(b p) o -> b (p o)", p=P)).then_inc(tok_in, 16)
            sp.wait_ge(tok_in, 16)

        @block.gpsimd
        def _(g):
            g.wait_ge(cleared, 16)
            g.wait_ge(vec, DEST)
            for n in range(2 * NT):
                g.indirect_dma_start(table, bass.IndirectOffsetOnAxis(ap=desti[:, n:n + 1], axis=0),
                                     cols[:, 0, n % NT:n % NT + 1], None).then_inc(scattered, 16)
            g.wait_ge(scattered, 16 * 2 * NT)

        @block.tensor
        def _(pe):
            pe.wait_ge(tok_in, 16)
            pe.transpose(ps[:, 0:NBLK], tok[:], ident[0:NBLK, 0:NBLK]).then_inc(turned, 1)

        @block.vector
        def _(v):
            n = [0]

            def do(ins):
                n[0] += 1
                ins.then_inc(vec, 1)
                v.wait_ge(vec, n[0])

            do(v.memset(zero[:], 0.0))
            do(v.memset(ones[:], 1.0))
            v.wait_ge(consts, 48)
            do(v.tensor_tensor(cmp1[:], bc(counts[:], KB), bm(nums[:, 0:KB], NE), ALU.is_gt))
            do(v.tensor_reduce(blocks[:], cmp1[:], AX.X, ALU.add))
            do(v.tensor_tensor_scan(ends[:], ones[:], blocks[:], 0.0, ALU.mult, ALU.add))
            do(v.tensor_tensor(starts[:], ends[:], blocks[:], ALU.subtract))
            do(v.tensor_scalar(starts[:], starts[:], float(P), None, ALU.mult))
            for s in range(2):
                o = oh[:, s * NT * NE:(s + 1) * NT * NE].rearrange("p (t e) -> p t e", e=NE)
                do(v.tensor_tensor(tmp[:], o, bm(starts[:], NT), ALU.mult))
                do(v.tensor_reduce(dest[:, s, :], tmp[:], AX.X, ALU.add))
            do(v.tensor_tensor(dest[:], dest[:], rank[:].rearrange("p (a n) -> p a n", a=2), ALU.add))
            do(v.tensor_copy(keep["rows"][:], dest[:].rearrange("p a n -> p (a n)")))
            do(v.tensor_tensor(dest[:], dest[:], bm(cols[:, 1, :], 2), ALU.add))
            do(v.tensor_scalar(dest[:, 1, NT - 1:NT], dest[:, 1, NT - 1:NT], cols[:, 2, 0:1], None, ALU.add))
            do(v.tensor_copy(desti[:], dest[:].rearrange("p a n -> p (a n)")))
            assert n[0] == DEST, n[0]
            do(v.tensor_tensor(cmp2[:], bm(ends[:], NBLK), bc(nums[:, KB:KB + NBLK], NE), ALU.is_le))
            do(v.tensor_reduce(be[:], cmp2[:], AX.X, ALU.add))
            do(v.tensor_scalar(be[:], be[:], float(NE - 1), None, ALU.min))
            do(v.tensor_copy(keep["block_expert"][:], be[:]))
            v.tensor_scalar(be4[:], be[:], float(P // SLOTS), None, ALU.mult)
            do(v.memset(keep["free_at"][:, 0:SLOTS], 0))
            groups = NE // SLOTS - 1
            do(v.tensor_tensor(cmp2[:, :, 0:groups], bc(be4[:], groups), bm(nums[:, 1:1 + groups], NBLK), ALU.is_ge))
            do(v.tensor_reduce(be4[:], cmp2[:, :, 0:groups], AX.X, ALU.add))
            do(v.scalar_tensor_tensor(out=be4[:], in0=be4[:], scalar=-float(SLOTS), in1=be[:], op0=ALU.mult,
                                      op1=ALU.add))
            do(v.tensor_copy(keep["slot"][:], be4[:]))
            do(v.tensor_copy(keep["free_at"][:, SLOTS:SLOTS + NE], ends[:]))
            v.wait_ge(turned, 1)
            do(v.tensor_copy(keep["tokens"][:], ps[:, 0:NBLK]))


def experts(nc, io, scr, keep):
    with ExitStack() as ctx:
        def sb(name, shape, dt=F32):
            return ctx.enter_context(nc.sbuf_tensor("ex_" + name, shape, dt))

        FC = FE // P
        bank = [ctx.enter_context(nc.psum_tensor(f"ex_bank{b}", [P, 512], F32)) for b in range(8)]
        b4 = [b[:, :].rearrange("p (a n) -> p a n", a=4) for b in bank]
        ident = sb("ident", [P, P])
        nought = sb("nought", [P, 1])
        spare = [sb(f"spare{s}", [P, 1]) for s in range(2)]
        started = ctx.enter_context(nc.semaphore("ex_started"))
        wg, wu, wd = sb("wg", [P, SLOTS, KC * FE]), sb("wu", [P, SLOTS, KC * FE]), sb("wd", [P, SLOTS, FC * D])
        idx, x, xT, th, hid, hT, y = ([sb(f"{n}{s}", shape, dt) for s in range(2)] for n, shape, dt in (
            ("idx", [P, 1], I32), ("x", [P, D], F32), ("xT", [P, KC, P], F32), ("th", [P, FE], F32),
            ("hid", [P, FE], F32), ("hT", [P, FC, P], F32), ("y", [P, D], F32)))

        A = {n: Steps(nc, ctx, "up_" + n) for n in ("tensor", "vector", "scalar", "gpsimd")}
        B = {n: Steps(nc, ctx, "down_" + n) for n in ("tensor", "scalar")}
        aten, avec, aact, apol = A["tensor"], A["vector"], A["scalar"], A["gpsimd"]
        bten, bact = B["tensor"], B["scalar"]
        const = Dmas(nc, ctx, "ex_const", 1)
        w_in = [Dmas(nc, ctx, f"ex_w_in{s}", 3, 1) for s in range(SLOTS)]
        ready = ctx.enter_context(nc.semaphore("ex_weights_ready"))
        x_in = [Dmas(nc, ctx, f"ex_x_in{s}", 1) for s in range(2)]
        y_out = [Dmas(nc, ctx, f"ex_y_out{s}", 1, 1) for s in range(2)]
        block = ctx.enter_context(nc.Block())
        turns = NBLK // 2


        @block.sync
        def _(sp):
            sp.dma_start(ident[:], io["ident"]).then_inc(const.sem, 16)
            for s in range(SLOTS):
                sp.sem_inc(w_in[s].sem, 16 * 3)

            def turn(t):
                ends = [sp.value_load(keep["free_at"][0:1, bass.ds(t.i * SLOTS + s, 1)], min_val=0,
                                      max_val=NBLK) for s in range(SLOTS)]
                free_at = [sp.snap(e * (bten.per // 2) + bten.per) for e in ends]
                es = [bass.ds(sp.snap(t.i * SLOTS + s), 1) for s in range(SLOTS)]
                t.ahead(*[(w_in[(s - 2) % SLOTS], None, -1 if s < 2 else 0) for s in range(SLOTS)])
                for s, e in enumerate(es):
                    sp.wait_ge(bten.sem, free_at[s])
                    for dst, src, k in ((wg, io["w_eg"], KC), (wu, io["w_eu"], KC), (wd, io["w_ed"], FC)):
                        w_in[s].go(sp.dma_start(dst[:, s, :], src[e].rearrange("a (p k) n -> (a p) (k n)", k=k)))
                    t._wait(w_in[(s - 2) % SLOTS], None, -1 if s < 2 else 0)
                    sp.sem_inc(ready, 1)

            engine_loop(sp, None, NE // SLOTS, turn)
            for s in range(SLOTS - 2, SLOTS):
                sp.wait_ge(w_in[s].sem, w_in[s].done(NE // SLOTS - 1))
                sp.sem_inc(ready, 1)

        @block.gpsimd
        def _(g):
            g.memset(nought[:], 0.0).then_inc(started, 1)
            g.wait_ge(started, 1)

            def up(t, woven_in):
                for s in range(2):
                    t.w0(aten, f"x_T{s}1")
                    t.do(g.tensor_copy(idx[s][:], keep["tokens"][:, bass.ds(t.i * 2 + s, 1)]), f"idx{s}")
                    g.tensor_tensor(spare[s][:], nought[:], nought[:], ALU.add)
                    x_in[s].go(g.indirect_dma_start(x[s][:], None, scr["h"],
                                                    bass.IndirectOffsetOnAxis(ap=idx[s][:, 0:1], axis=0)))
                yield

            woven(g, turns, apol, None, up, None, "")

        @block.scalar
        def _(a):
            a.sem_inc(y_out[0].sem, 16)
            a.sem_inc(y_out[1].sem, 16)

            def up(t, woven_in):
                for s in range(2):
                    for k in range(2):
                        t.w(aten, f"x_T{s}{k}")
                        t.mark(a.activation(xT[s][:, 4 * k:4 * k + 4, :], b4[2 * s + k], ACT.Copy), f"x_T{s}{k}")
                yield
                for s in range(2):
                    t.w(aten, f"gate{s}")
                    t.w0(avec, f"hidden{s}")
                    t.mark(a.activation(th[s][:], bank[4][:, 0:FE], ACT.Tanh, scale=0.5), f"tanh{s}")
                    yield

            def down(t, woven_in):
                for s in range(2):
                    t.w(bten, f"h_T{s}")
                    t.mark(a.activation(hT[s][:], b4[2][:, 0:FC, :], ACT.Copy), f"h_T{s}")
                    yield
                    t.w(bten, f"down{s}")
                    t.left(y_out[s])
                    a.activation(y[s][:, 0:512], bank[6][:, :], ACT.Copy)
                    t.do(a.activation(y[s][:, 512:D], bank[7][:, :], ACT.Copy), f"y{s}")
                    y_out[s].go(a.dma_start(scr["ys"][bass.ds((t.i * 2 + s) * P, P), :], y[s][:]))
                    yield

            woven(a, turns, aact, bact, up, down, "bababba")
            for s in range(2):
                a.wait_ge(y_out[s].sem, y_out[s].done(turns - 1))

        @block.tensor
        def _(pe):
            pe.wait_ge(const.sem, 16)

            def value(name, t, s, top):
                return pe.value_load(keep[name][0:1, bass.ds(t.i * 2 + s, 1)], min_val=0, max_val=top)

            def up(t, woven_in):
                experts_ready = [pe.snap(value("block_expert", t, s, NE - 1) + 3) for s in range(2)]
                slots = [bass.ds(value("slot", t, s, SLOTS - 1), 1) for s in range(2)]
                yield
                for s in range(2):
                    t.arrived(x_in[s])
                    if s == 0:
                        t.w0(aact, "x_T11")
                    else:
                        t.w0(bact, "h_T0")
                    xv = x[s][:, :].rearrange("t (p k) -> t k p", k=KC)
                    for k in range(2):
                        for c in range(4):
                            ins = pe.transpose(b4[2 * s + k][:, c, :], xv[:, 4 * k + c, :], ident[:, :])
                        t.mark(ins, f"x_T{s}{k}")
                yield
                for s in range(2):
                    pe.wait_ge(ready, experts_ready[s])
                    t.w(aact, f"x_T{s}1")
                    for n, (w, name, read) in enumerate(((wg, "gate", "silu"), (wu, "up", "hidden"))):
                        (t.w0 if s == 0 else t.w)(avec, f"{read}{1 - s}")
                        wv = w[:, slots[s], :].rearrange("p a n -> p (a n)")
                        for k in range(KC):
                            ins = pe.matmul(bank[4 + n][:, 0:FE], xT[s][:, k, :],
                                            wv[:, k * FE:(k + 1) * FE], start=(k == 0), stop=(k == KC - 1))
                        t.mark(ins, f"{name}{s}")
                        yield

            def down(t, woven_in):
                slots = [bass.ds(value("slot", t, s, SLOTS - 1), 1) for s in range(2)]
                yield
                for s in range(2):
                    t.w(avec, f"hidden{s}")
                    if s == 1 and woven_in:
                        t.next_done(aact, "x_T10")
                    for m in range(FC):
                        ins = pe.transpose(b4[2][:, m, :], hid[s][:, m:FE:FC], ident[:, :])
                    t.mark(ins, f"h_T{s}")
                    yield
                    t.w(bact, f"h_T{s}")
                    wv = wd[:, slots[s], :].rearrange("p a n -> p (a n)")
                    for n in range(2):
                        for m in range(FC):
                            ins = pe.matmul(bank[6 + n][:, :], hT[s][:, m, :], wv[:, m * D + n * 512:m * D + (n + 1) * 512],
                                            start=(m == 0), stop=(m == FC - 1))
                    t.mark(ins, f"down{s}")
                    yield

            woven(pe, turns, aten, bten, up, down, "abbabababaa")

        @block.vector
        def _(v):
            def up(t, woven_in):
                for s in range(2):
                    t.w(aact, f"tanh{s}")
                    t.do(v.scalar_tensor_tensor(out=th[s][:], in0=th[s][:], scalar=1.0, in1=bank[4][:, 0:FE],
                                                op0=ALU.add, op1=ALU.mult), f"silu{s}")
                    t.w(aten, f"up{s}")
                    t.w0(bten, f"h_T{s}")
                    t.mark(v.scalar_tensor_tensor(out=hid[s][:], in0=th[s][:], scalar=0.5, in1=bank[5][:, 0:FE],
                                                  op0=ALU.mult, op1=ALU.mult), f"hidden{s}")
                yield

            woven(v, turns, avec, None, up, None, "")


def combine(nc, io, scr, keep):
    with ExitStack() as ctx:
        def sb(name, shape, dt=F32):
            return ctx.enter_context(nc.sbuf_tensor("co_" + name, shape, dt))

        rows = sb("rows", [P, 2, D])
        eps = sb("eps", [P, 1])
        idx = [sb(f"idx{s}", [P, 1], I32) for s in range(2)]
        y = [sb(f"y{s}", [P, D]) for s in range(2)]
        h = sb("h", [P, D])
        r = sb("r", [P, D])
        o = sb("o", [P, D])
        st = sb("st", [P, 2, 6])
        mv = sb("mv", [P, 2])
        rstd = sb("rstd", [P, 1])
        gates = sb("gates", [P, 2])
        nought, spare = sb("nought", [P, 1]), sb("spare", [P, 1])
        started = ctx.enter_context(nc.semaphore("co_started"))
        gate = keep["gate"]

        vec, act, pol = (Steps(nc, ctx, "combine_" + n) for n in ("vector", "scalar", "gpsimd"))
        consts = Dmas(nc, ctx, "co_consts", 2)
        y_in = Dmas(nc, ctx, "co_y_in", 2)
        h_in = Dmas(nc, ctx, "co_h_in", 1)
        out = Dmas(nc, ctx, "co_out", 1, 1)
        block = ctx.enter_context(nc.Block())

        @block.sync
        def _(sp):
            sp.dma_start(rows[:], io["ln2"].rearrange("(o a) n -> o a n", o=1).to_broadcast([P, 2, D])).then_inc(consts.sem, 16)
            sp.dma_start(eps[:], io["eps"]).then_inc(consts.sem, 16)
            sp.sem_inc(out.sem, 16)

            def turn(t):
                t.ahead((vec, "residual", -1), (vec, "y", 0))
                col = bass.ds(sp.snap(t.i * P), P)
                t.w0(vec, "residual")
                h_in.go(sp.dma_start(h[:], scr["h"][col, :]))
                t.w(vec, "y")
                out.go(sp.dma_start(io["y_out"][col, :], o[:]))

            engine_loop(sp, None, NT, turn)
            sp.wait_ge(out.sem, out.done(NT - 1))

        @block.gpsimd
        def _(g):
            g.memset(nought[:], 0.0).then_inc(started, 1)
            g.wait_ge(started, 1)

            def turn(t):
                t.w0(vec, "second")
                g.tensor_copy(idx[0][:], keep["rows"][:, bass.ds(t.i, 1)])
                t.do(g.tensor_copy(idx[1][:], keep["rows"][:, bass.ds(t.i + NT, 1)]), "idx")
                g.tensor_tensor(spare[:], nought[:], nought[:], ALU.add)
                for s in range(2):
                    y_in.go(g.indirect_dma_start(y[s][:], None, scr["ys"],
                                                 bass.IndirectOffsetOnAxis(ap=idx[s][:, 0:1], axis=0)))

            engine_loop(g, pol, NT, turn)

        @block.scalar
        def _(a):
            a.wait_ge(consts.sem, consts.done(0))

            def turn(t):
                t.w(vec, "stats")
                t.mark(a.activation(rstd[:], mv[:, 1:2], ACT.Sqrt, bias=eps[:, 0:1]), "root")

            engine_loop(a, act, NT, turn)

        @block.vector
        def _(v):
            v.wait_ge(consts.sem, consts.done(0))

            def turn(t):
                do = t.do
                v.tensor_copy(gates[:, 0:1], gate[:, bass.ds(t.i, 1)])
                do(v.tensor_copy(gates[:, 1:2], gate[:, bass.ds(t.i + NT, 1)]), "gates")
                t.arrived(y_in)
                do(v.tensor_scalar(r[:], y[0][:], gates[:, 0:1], None, ALU.mult), "first")
                do(v.scalar_tensor_tensor(out=r[:], in0=y[1][:], scalar=gates[:, 1:2], in1=r[:],
                                          op0=ALU.mult, op1=ALU.add), "second")
                t.arrived(h_in)
                do(v.scalar_tensor_tensor(out=r[:], in0=h[:], scalar=ALPHA, in1=r[:], op0=ALU.mult, op1=ALU.add),
                   "residual")
                for n in range(2):
                    ins = v.bn_stats(st[:, n, :], r[:, n * 512:n * 512 + 512])
                do(ins, "half_stats")
                v.tensor_copy(rstd[:], st[:, 0, 0:1])
                do(v.bn_aggr(mv[:], st[:]), "stats")
                t.w(act, "root")
                do(v.reciprocal(rstd[:], rstd[:]), "rstd")
                do(v.tensor_scalar(r[:], r[:], mv[:, 0:1], rstd[:, 0:1], ALU.subtract, ALU.mult), "normed")
                do(v.tensor_tensor(r[:], r[:], rows[:, 0, :], ALU.mult), "gain")
                t.left(out)
                do(v.tensor_tensor(o[:], r[:], rows[:, 1, :], ALU.add), "y")

            engine_loop(v, vec, NT, turn)


def _shape_constants():
    k, t = np.arange(P)[:, None], np.arange(P)[None, :]
    head = (k // 64 == t // 64)
    f = np.float32

    def off(size):
        return (k // size % 2 == 0) & (t // size == k // size + 1)

    cst = np.stack([head, head / 64.0, k < t, k <= t, k > t, off(1), off(1).T], 1).astype(f).reshape(P, 7 * P)
    levs = np.stack([off(2 ** n).reshape(P, -1, 2, 2 ** n)[:, :, 1].reshape(P, 64) for n in range(1, LEVELS + 1)], 1)
    levs = levs.astype(f).reshape(P, LEVELS * 64)
    rms = np.stack([np.full((P, P), 1.0 / QL), np.full((P, P), 1.0 / KVL)], 1).astype(f).reshape(P, 2 * P)
    half = ROPE // 2
    inv = (f(10000.0) ** (-np.arange(0, ROPE, 2, dtype=f) / f(ROPE))).astype(f)
    pos = np.zeros((NT, P), f)
    pos[:NT - 1] = np.arange(SEQ, dtype=f).reshape(NT - 1, P)
    pos[NT - 1] = PAST + np.arange(P, dtype=f)
    ang = (pos[:, :, None] * inv).astype(f).astype(np.float64)
    cos, sin = np.cos(ang), np.sin(ang)
    both = np.stack([np.concatenate([cos, cos], -1), np.concatenate([-sin, sin], -1)], 2)
    rope = np.tile(both.transpose(0, 3, 2, 1), (1, 4, 1, 1)).astype(f).reshape(NT, P, 2 * P)
    assert half * 2 == ROPE
    valid = np.ones((NT, P), f)
    valid[NT - 1, DEC:] = 0
    return dict(cst=cst, levs=levs, rmsw=rms, rope=rope, ident=np.eye(P, dtype=f)), valid


def _by_channel(v):
    return np.moveaxis(v.reshape(v.shape[:-1] + (v.shape[-1] // P, P)), -1, 0)


def _layout(a):
    c, valid = _shape_constants()
    f = np.float32
    w = {k: np.asarray(v) for k, v in a.items()}

    def rows(m):
        return np.ascontiguousarray(m.reshape(-1, P, m.shape[1]).transpose(1, 0, 2)).reshape(P, -1)

    x = np.zeros((NT + 1, P, D), f)
    x[:NT - 1] = w["x_prompt"].reshape(NT - 1, P, D)
    x[NT - 1, :DEC] = w["x_sample"][0]
    c["x"] = x
    wi = w["w_in"][0]
    swap = np.r_[ROPE // 2:ROPE, 0:ROPE // 2]
    kpe = wi[:, QL + KVL:QL + KVL + ROPE]
    c["w_in"] = rows(np.concatenate([wi[:, :QL + KVL], wi[:, QL + KVL + ROPE:], kpe, kpe[:, swap]], 1))
    uq = w["w_uq"][0]
    pe = uq[:, :, NOPE:]
    c["w_uq"] = rows(np.concatenate([uq[:, :, :NOPE].reshape(QL, -1), pe.reshape(QL, -1),
                                     pe[:, :, swap].reshape(QL, -1)], 1))
    wa = np.zeros((P, 2, 512), f)
    wa[:64, 0], wa[64:, 1] = w["w2"][0], w["a2"][0]
    c["w_wa"] = wa.reshape(P, 1024)
    c["w_g"] = w["g2"][0]
    par = np.zeros((P, 64), f)
    vecs = [(0, "mu_shift"), (14, "q_norm_g"), (17, "kv_norm_g"), (20, "w0"), (24, "a0"), (28, "k_k"), (32, "k_a"),
            (36, "r_k"), (40, "lnx_g"), (44, "lnx_b")]
    for at, name in vecs:
        v = _by_channel(w[name][0].reshape(-1))
        par[:, at:at + v.shape[1]] = v
    par[:, 48], par[:, 49], par[:, 50] = RMS_EPS, GN_EPS, LN_EPS
    c["par"] = par
    keep = np.ones((NT, P, 1), f)
    keep[NT - 1] = 0
    shift = np.zeros((NT, P, NPR), f)
    shift[NT - 1] = _by_channel(w["state_shift"][0, 0])
    c["first"], c["keep"] = np.concatenate([keep, shift], 2), keep
    c["masks"] = np.stack([np.tile((-LOGW / 2) * valid[:, None, :], (1, P, 1)),
                           np.tile(valid[:, None, :], (1, P, 1))], 2).astype(f).reshape(NT, P, 2 * P)
    s_init = np.zeros((NT, 2, 64, 4, 64), f)
    s_init[NT - 1] = w["state_wkv"][0, 0].reshape(4, 2, 64, 64).transpose(1, 3, 0, 2)
    c["s_init"] = s_init.reshape(NT, P, 256)
    c["past_ckvT"] = rows(w["cache_ckv"][0, 0].T)
    c["past_kpeT"] = w["cache_kpe"][0, 0].T
    c["w_ukv"] = w["w_ukv"][0].reshape(CKV, P, H, P).transpose(2, 1, 0, 3).reshape(H, P, CKV * P)
    c["w_o"] = rows(w["w_o"][0])
    c["w_r"] = rows(np.concatenate([w["w_gr"][0], w["w_er"][0]], 1))
    c["ln1"] = np.stack([w["ln1_g"][0], w["ln1_b"][0]])
    c["ln2"] = np.stack([w["ln2_g"][0], w["ln2_b"][0]])
    c["small"] = np.concatenate([w["b_gr"][0], w["b_er"][0], np.arange(NG, 0, -1, dtype=f),
                                 np.arange(EPG, 0, -1, dtype=f)])[None]
    before = (np.arange(P)[:, None] < np.arange(P)[None, :]).astype(f)
    c["eps"] = np.full((P, 1), LN_EPS, f)
    c["cst3"] = np.stack([np.eye(P, dtype=f), before, np.ones((P, P), f)], 1).reshape(P, 3 * P)
    c["vcol"] = valid.T.copy()
    kb = SEQ // P + 1
    c["nums"] = np.concatenate([P * np.arange(kb), np.arange(NBLK)]).astype(f)[None]
    tok = np.arange(TOK).reshape(NT, P).T
    dump = (1 - valid.T) * (NBLK * P + np.arange(P)[:, None])
    again = np.tile((1 - valid[NT - 1])[:, None] * P, (1, NT))
    c["cols"] = np.stack([tok, dump, again], 1).astype(f).reshape(P, 3 * NT)
    for name in ("w_eg", "w_eu", "w_ed"):
        c[name] = w[name][0]
    return c


def program(nc, io, scr):
    with ExitStack() as ctx:
        def kept(name, cols, dt=F32):
            return ctx.enter_context(nc.sbuf_tensor("kept_" + name, [P, cols], dt))

        keep = dict(onehot=kept("onehot", 2 * NT * NE), rank=kept("rank", 2 * NT), gate=kept("gate", 2 * NT),
                    counts=kept("counts", NE), rows=kept("rows", 2 * NT, I32), tokens=kept("tokens", NBLK, I32),
                    block_expert=kept("block_expert", NBLK, I32),
                    slot=kept("slot", NBLK, I32), free_at=kept("free_at", SLOTS + NE, I32))
        mixer(nc, io, scr)
        attention(nc, io, scr)
        router(nc, io, scr, keep)
        dispatch(nc, io, scr, keep)
        experts(nc, io, scr, keep)
        combine(nc, io, scr, keep)


_SCRATCH = dict(kpeT=(ROPE, TOK), ckvT=(KVL, TOK), qT=(H, QK, TOK), rwT=(512, TOK), attn=(TOK, 512), h=(TOK, D),
                table=((NBLK + 2) * P, 1), ys=(NBLK * P, D))
_OUTS = dict(y_out=(TOK, D), ckv_out=(NT, P, KVL), kpe_out=(NT, P, ROPE), edge_out=(NT, P, 2 * NPR),
             state_out=(NT, P, 256))
_SCRATCH_KIND = "Internal"


def _outputs(r):
    y, ckv, kpe, edge, state = (r["out_" + n] for n in _OUTS)
    ckv, kpe = ckv.reshape(TOK, KVL), kpe.reshape(TOK, ROPE)
    shift = [edge[t].reshape(P, 2, NPR)[:, e].T.reshape(1, 1, -1) for t, e in ((NT - 2, 1), (NT - 1, 0))]
    wkv = [state[t].reshape(2, 64, 4, 64).transpose(2, 0, 3, 1).reshape(1, 1, H, 64, 64) for t in (NT - 2, NT - 1)]
    s = slice(SEQ, SEQ + DEC)
    return (y[:SEQ][None], y[s][None], ckv[:SEQ][None, None], kpe[:SEQ][None, None], wkv[0], shift[0],
            ckv[s][None, None], kpe[s][None, None], wkv[1], shift[1])


def kernel(**inputs):
    import concourse.bacc as _bacc
    from concourse.bass_utils import run_bass_kernel_spmd as _run

    nc = _bacc.Bacc("TRN2", target_bir_lowering=False, num_devices=1)
    io, arrays = {}, {}
    for name, a in _layout(inputs).items():
        arrays["in_" + name] = np.ascontiguousarray(a)
        io[name] = nc.dram_tensor("in_" + name, a.shape, mybir.dt.from_np(a.dtype), kind="ExternalInput").ap()
    for name, shape in _OUTS.items():
        io[name] = nc.dram_tensor("out_" + name, shape, F32, kind="ExternalOutput").ap()
    scr = {name: nc.dram_tensor("scr_" + name, shape, F32, kind=_SCRATCH_KIND).ap() for name, shape in _SCRATCH.items()}
    program(nc, io, scr)
    return _outputs(_run(nc, [arrays], core_ids=[0]).results[0])
```

```python
from contextlib import ExitStack

import numpy as np

import concourse.bass as bass
from concourse import mybir

F32 = mybir.dt.float32
I32 = mybir.dt.int32
ALU = mybir.AluOpType
ACT = mybir.ActivationFunctionType
AX = mybir.AxisListType
P = 128
D = 1024
SEQ, DEC, PAST = 2048, 32, 128
NT = SEQ // P + 1
TOK = NT * P
H = 8
NOPE, ROPE, VD = 64, 32, 64
QK = NOPE + ROPE
QL, KVL = 384, 256
CQ, CKV = QL // P, KVL // P
NPR = 14
WCOL = QL + KVL + NPR * P + 2 * ROPE
KC = D // P
NG, EPG, FE = 4, 8, 256
NE = NG * EPG
NR = NG + NE
ASSIGN = 2 * (SEQ + DEC)
NBLK = (ASSIGN + NE * (P - 1)) // P
SLOTS = 4
ROUTE_GAP = 22
ALPHA = 2.0 ** 0.25
SCALE = float(QK) ** -0.5
LN_EPS, RMS_EPS, GN_EPS = 1e-5, 1e-6, 64e-5
LOGW = float(np.exp(-0.5))
LEVELS = 6

PE_ORDER = "ababaaabab" + 6 * "b" + "babaabaa" + "baa"
ACT_ORDER = "bababaaabbbabbaab"
VEC_ORDER = "babab" + 6 * "b" + "bbabb"

STEPS = {
    "project_tensor": (
        "pr_proj0 pr_proj1 pr_proj2 pr_proj3 cq_proj ckv_proj rms_sums q_nope q_pe ckv_tokens x_transposed0 "
        "x_transposed1 "
    ).split(),
    "project_vector": (
        "pr_edge rms cq_normed ckv_normed kpe_cos kpe_sin kpe_roped q_rope_cos q_rope_sin q_roped "
    ).split(),
    "project_scalar": (
        "pr0 pr1 pr2 pr3 edges cq_sq ckv_sq rms_root q_nope ckv_tokens xT0 xT1 "
    ).split(),
    "rwkv_tensor": (
        "lora_w lora_a lora_g kk_norm v_tokens bonus_sum gram_l0 gram_l1 gram_b0 gram_b1 gram_k0 gram_k1 gram_k2 "
        "gram_k3 U0 Z1_0 Z1_1 U1_0 T1_0 U1_1 T1_1 G Z2_0 Z2_1 U2_0 T2_0 U2_1 T2_1 Z3_0 Z3_1 U3_0 T3_0 U3_1 T3_1 Z4_0 "
        "Z4_1 U4_0 T4_0 U4_1 T4_1 Z5_0 Z5_1 U5_0 T5_0 U5_1 T5_1 Z6_0 Z6_1 U6_0 U6_1 b_tokens k_tokens SA y state_add "
        "y_mean y_var "
    ).split(),
    "rwkv_vector": (
        "u_low a_lo u_k g_sig kk u_r u_v log_w cum mid a_sig a_ka kh kk_norm2 kk_rs kk_normed a_hat en_masked b_gate "
        "b_hat k_hat bonus T_level0_0 T_level0_1 L1 RB0 RB1 state_in state_mid MK0 MK1 MK2 MK3 Z1_0 Z1_1 U1_0 T1_0 U1_1 "
        "T1_1 Z2_0 Z2_1 U2_0 T2_0 U2_1 T2_1 Z3_0 Z3_1 U3_0 T3_0 U3_1 T3_1 Z4_0 Z4_1 U4_0 T4_0 U4_1 T4_1 Z5_0 Z5_1 U5_0 "
        "T5_0 U5_1 T5_1 Z6_0 Z6_1 U6_0 U6_1 state_sum state y_centred y_rs y_normed y_bonus gated "
    ).split(),
    "rwkv_scalar": (
        "u_own_low u_own_k u_own_r u_own_v g_lo w_tanh a_tanh kk_sq g_out exp_pos exp_neg em kk_root v_tokens U0 G "
        "b_tokens k_tokens SA y y_sq y_root y_gain "
    ).split(),
    "rwkv_gpsimd": (
        "r_hat rk rkr T_start0 T_start1 Z_clear1 Z_clear2 Z_clear3 Z_clear4 Z_clear5 "
    ).split(),
    "attention_tensor": (
        "K0 K1 K2 K3 K4 V0 V1 V2 S0 S1 S2 S3 S4 PT0 S5 PT1 S6 PT2 S7 PV0 PT3 S8 PV1 PT4 S9 PV2 PT5 S10 PV3 PT6 S11 PV4 "
        "PT7 S12 PV5 PT8 S13 PV6 PT9 S14 PV7 PT10 S15 PV8 PT11 S16 PV9 PT12 S17 PV10 PT13 S18 PV11 PT14 S19 PV12 PT15 "
        "S20 PV13 PT16 S21 PV14 PT17 S22 PV15 PT18 S23 PV16 PT19 S24 PV17 PT20 S25 PV18 PT21 S26 PV19 PT22 S27 PV20 "
        "PT23 S28 PV21 PT24 S29 PV22 PT25 S30 PV23 PT26 S31 PV24 PT27 S32 PV25 PT28 S33 PV26 PT29 S34 PV27 PT30 S35 "
        "PV28 PT31 S36 PV29 PT32 S37 PV30 PT33 S38 PV31 PT34 S39 PV32 PT35 S40 PV33 PT36 PV34 PT37 PV35 PT38 PV36 PT39 "
        "PV37 PT40 PV38 PV39 PV40 "
    ).split(),
    "attention_vector": (
        "V0 V1 V2 max0 rowmax0 negmax0 max1 rowmax1 negmax1 max2 rowmax2 negmax2 max3 rowmax3 negmax3 max4 PT0 max5 "
        "rowmax4 negmax4 PT1 max6 PT2 max7 rowmax5 negmax5 sum0 sum_rec0 out_0 PT3 max8 sum1 sum_rec1 out_1 PT4 max9 "
        "rowmax6 negmax6 sum2 sum_rec2 out_2 PT5 max10 sum3 sum_rec3 out_3 PT6 max11 rowmax7 negmax7 PT7 max12 sum4 "
        "sum_rec4 out_4 PT8 max13 PT9 max14 rowmax8 negmax8 sum5 sum_rec5 out_5 PT10 max15 PT11 max16 sum6 sum_rec6 "
        "out_6 PT12 max17 rowmax9 negmax9 PT13 max18 sum7 sum_rec7 out_7 PT14 max19 PT15 max20 rowmax10 negmax10 PT16 "
        "max21 sum8 sum_rec8 out_8 PT17 max22 PT18 max23 rowmax11 negmax11 PT19 max24 sum9 sum_rec9 out_9 PT20 max25 "
        "PT21 max26 PT22 max27 rowmax12 negmax12 sum10 sum_rec10 out_10 PT23 max28 PT24 max29 PT25 max30 sum11 "
        "sum_rec11 out_11 PT26 max31 rowmax13 negmax13 PT27 max32 PT28 max33 PT29 max34 sum12 sum_rec12 out_12 PT30 "
        "max35 rowmax14 negmax14 PT31 max36 PT32 max37 PT33 max38 sum13 sum_rec13 out_13 PT34 max39 rowmax15 negmax15 "
        "PT35 max40 rowmax16 negmax16 PT36 PT37 sum14 sum_rec14 out_14 PT38 PT39 PT40 sum15 sum_rec15 out_15 sum16 "
        "sum_rec16 out_16 "
    ).split(),
    "attention_scalar": (
        "K0 K1 K2 K3 K4 exp0 exp1 exp2 exp3 exp4 exp5 exp6 exp7 exp8 exp9 exp10 exp11 exp12 exp13 exp14 exp15 exp16 "
        "exp17 exp18 exp19 exp20 exp21 exp22 exp23 exp24 exp25 exp26 exp27 exp28 exp29 exp30 exp31 exp32 exp33 exp34 "
        "exp35 exp36 exp37 exp38 exp39 exp40 "
    ).split(),
    "attention_gpsimd": (
        "corner0 corner1 corner2 corner3 corner5 corner7 corner9 corner11 corner14 corner17 corner20 corner23 corner27 "
        "corner31 corner35 corner39 "
    ).split(),
    "proj_tensor": (
        "attn_T first_half out_proj "
    ).split(),
    "proj_vector": (
        "residual half_stats stats rstd shift gain "
    ).split(),
    "proj_scalar": (
        "attn_T root normed "
    ).split(),
    "proj_gpsimd": (
        "h "
    ).split(),
    "route_tensor": (
        "h_T0 h_T1 logits "
    ).split(),
    "route_vector": (
        "logits "
    ).split(),
    "route_scalar": (
        "h_T0 h_T1 "
    ).split(),
    "up_tensor": (
        "x_T00 x_T01 x_T10 x_T11 gate0 up0 gate1 up1 "
    ).split(),
    "up_vector": (
        "silu0 hidden0 silu1 hidden1 "
    ).split(),
    "up_scalar": (
        "x_T00 x_T01 x_T10 x_T11 tanh0 tanh1 "
    ).split(),
    "up_gpsimd": (
        "idx0 idx1 "
    ).split(),
    "down_tensor": (
        "h_T0 down0 h_T1 down1 "
    ).split(),
    "down_scalar": (
        "h_T0 y0 h_T1 y1 "
    ).split(),
    "sum_vector": (
        "gates second residual "
    ).split(),
    "sum_scalar": (
        "first "
    ).split(),
    "sum_gpsimd": (
        "idx0 idx1 "
    ).split(),
    "norm_vector": (
        "half_stats stats rstd shift gain y "
    ).split(),
    "norm_scalar": (
        "root normed "
    ).split(),
}


class Steps:

    def __init__(self, nc, ctx, name):
        self.sem = ctx.enter_context(nc.semaphore(name))
        self.name, self.names, self.seen = name, STEPS.get(name, ()), 0
        self.per = len(self.names)

    def mark(self, ins, name):
        assert self.names[self.seen] == name, (self.name, self.seen, name)
        self.seen += 1
        ins.then_inc(self.sem, 1)

    def whole(self):
        assert self.seen == self.per, (self.name, self.seen, self.per)
        self.seen = 0

    def done(self, turn, name):
        return self.per * (turn + 1) + self.names.index(name) + 1


class Dmas:

    def __init__(self, nc, ctx, name, n, start=0):
        self.sem = ctx.enter_context(nc.semaphore(name))
        self.n, self.start = n, start

    def go(self, ins):
        ins.then_inc(self.sem, 16)

    def done(self, turn):
        return 16 * self.n * (turn + 1 + self.start)


class Turn:

    def __init__(self, eng, own, i):
        self.eng, self.own, self.i = eng, own, i
        self.known = {}

    def ahead(self, *values):
        for counts, name, turn in values if not isinstance(self.i, int) else ():
            v = counts.done(self.i + turn, name) if name else counts.done(self.i + turn)
            reg = self.eng.alloc_register(f"v{len(self.known)}_{counts.sem.name}")
            self.eng.reg_mov(reg, v)
            self.known[counts.sem.name, name, turn] = reg

    def _wait(self, counts, name, turn):
        v = self.known.get((counts.sem.name, name, turn))
        if v is None:
            v = counts.done(self.i + turn, name) if name else counts.done(self.i + turn)
        self.eng.wait_ge(counts.sem, v)

    def do(self, ins, name):
        self.own.mark(ins, name)
        self.eng.wait_ge(self.own.sem, self.own.done(self.i, name))

    def mark(self, ins, name):
        self.own.mark(ins, name)

    def w(self, steps, name):
        self._wait(steps, name, 0)

    def w0(self, steps, name):
        self._wait(steps, name, -1)

    def next_done(self, steps, name):
        self._wait(steps, name, 1)

    def arrived(self, dmas):
        self._wait(dmas, None, 0)

    def left(self, dmas):
        self._wait(dmas, None, -1)


def engine_loop(eng, own, count, body):
    if own is not None:
        eng.sem_inc(own.sem, own.per)
    with eng.Fori(0, count) as i:
        body(Turn(eng, own, i))
    if own is not None:
        own.whole()


def woven(eng, count, a_steps, b_steps, front, back, order):
    def run(gens, turns, text):
        for c in text:
            next(gens[c], None)
        for g in gens.values():
            for _ in g:
                pass
        for t in turns:
            if t.own is not None:
                t.own.whole()

    for st in (a_steps, b_steps):
        if st is not None:
            eng.sem_inc(st.sem, st.per)
    if front is not None:
        t = Turn(eng, a_steps, 0)
        run({"a": front(t, False)}, [t], "")
    with eng.Fori(0, count - 1) as i:
        gens, turns = {}, []
        if front is not None:
            turns.append(Turn(eng, a_steps, i + 1))
            gens["a"] = front(turns[-1], True)
        if back is not None:
            turns.append(Turn(eng, b_steps, i))
            gens["b"] = back(turns[-1], True)
        run(gens, turns, order)
    if back is not None:
        t = Turn(eng, b_steps, count - 1)
        run({"b": back(t, False)}, [t], "")


def bc(ap, n):
    return ap.unsqueeze(2).to_broadcast([ap.shape[0], ap.shape[1], n])


def bm(ap, n):
    return ap.unsqueeze(1).to_broadcast([ap.shape[0], n, ap.shape[1]])


def mixer(nc, io, scr):
    with ExitStack() as ctx:
        def sb(name, shape, dt=F32):
            return ctx.enter_context(nc.sbuf_tensor("mx_" + name, shape, dt))

        bank = [ctx.enter_context(nc.psum_tensor(f"mx_bank{b}", [P, 512], F32)) for b in range(8)]
        b4 = [b[:, :].rearrange("p (a n) -> p a n", a=4) for b in bank]

        w_in = sb("w_in", [P, KC, WCOL])
        w_uq = sb("w_uq", [P, CQ, 1024])
        w_wa = sb("w_wa", [P, 2, 512])
        w_g = sb("w_g", [P, 512])
        par = sb("par", [P, 64])
        ident = sb("ident", [P, P])
        cst = sb("cst", [P, 7, P])
        bones, bmean, strict, incl, low, lev0, lev0T = (cst[:, k, :] for k in range(7))
        upper2 = cst[:, 2:4, :]
        levs = sb("levs", [P, LEVELS, 64])
        negh = sb("negh", [P, 8])
        rmsw = sb("rmsw", [P, 2, P])
        mu, qg, kvg = par[:, 0:14], par[:, 14:17], par[:, 17:19]
        w0c, a0c, kkc, kac, rkc, lxg, lxb = (par[:, 20 + 4 * k:24 + 4 * k] for k in range(7))

        x = sb("x", [P, D])
        rope = sb("rope", [P, 2, P])
        first = sb("first", [P, 1 + NPR])
        keep, shift0 = first[:, 0:1], first[:, 1:]
        masks = sb("masks", [P, 2, P])
        vm, valid = masks[:, 0, :], masks[:, 1, :]
        keep_s = sb("keep_s", [P, 1])
        s_init = sb("s_init", [P, 4, VD])
        xT = sb("xT", [P, KC, P])
        pr = sb("pr", [P, NPR, P + 1])
        edge = sb("edge", [P, 2, NPR])
        u = sb("u", [P, NPR, P])
        cq = sb("cq", [P, CQ, P])
        ckv = sb("ckv", [P, CKV, P])
        msr = sb("msr", [P, 2, P])
        kpe2 = sb("kpe2", [64, P])
        kpe = sb("kpe", [32, P])
        qn = sb("qn", [P, 4, P])
        qp = sb("qp", [P, 2, P])
        ckt = sb("ckt", [P, KVL + ROPE])
        lo = sb("lo", [P, P])
        sg = sb("sg", [P, P])
        lw = sb("lw", [P, 4, P])
        cum = sb("cum", [P, 4, P + 1])
        nm = sb("nm", [P, 4])
        ep = sb("ep", [P, 4, P + 1])
        en = sb("en", [P, 4, P + 1])
        em = sb("em", [P, 4])
        aa = sb("aa", [P, 4, P])
        gg = sb("gg", [P, 4, P])
        kk = sb("kk", [P, 4, P])
        t1 = sb("t1", [P, 4, P])
        kh = sb("kh", [P, 4, P])
        AR = sb("AR", [P, 4, 2, 2, P])
        vt = sb("vt", [P, 4, P])
        RB = sb("RB", [P, H, P])
        MK = sb("MK", [P, H, 2, P])
        L = sb("L", [P, H, P])
        U = sb("U", [P, H, P])
        T = sb("T", [P, H, P])
        Z = sb("Z", [P, H, P])
        Gs = sb("Gs", [P, 512])
        S = sb("S", [P, 4, VD])
        Sp = sb("Sp", [P, 4, VD])
        ys = sb("ys", [P, 4, P])
        bon, yq, qr, bh = aa, cum[:, :, 1:P + 1], lw[:, 0:2, :], u[:, 4:8, :]
        sq5 = T[:, 0:5, :]
        bt, kt = L[:, 0:4, :], L[:, 4:8, :]
        SA = Z[:, 4:8, :].rearrange("p a n -> p (a n)")
        ones = sb("ones", [P, P])
        mu1 = sb("mu1", [P, NPR])
        nought, spare = sb("nought", [P, 1]), sb("spare", [P, 1])

        A = {n: Steps(nc, ctx, "project_" + n) for n in ("tensor", "vector", "scalar")}
        B = {n: Steps(nc, ctx, "rwkv_" + n) for n in ("tensor", "vector", "scalar", "gpsimd")}
        aten, avec, aact = A["tensor"], A["vector"], A["scalar"]
        ten, vec, act, pol = B["tensor"], B["vector"], B["scalar"], B["gpsimd"]
        consts = Dmas(nc, ctx, "mx_consts", 8)
        w_part = [ctx.enter_context(nc.semaphore(f"mx_w_part{k}")) for k in range(5)]
        setup = ctx.enter_context(nc.semaphore("mx_setup"))
        first_x, first_xT = (ctx.enter_context(nc.semaphore("mx_first_" + n)) for n in ("x", "xT"))
        biases = ctx.enter_context(nc.semaphore("mx_biases"))
        x_in = Dmas(nc, ctx, "mx_x_in", 1)
        a_in = Dmas(nc, ctx, "mx_a_in", 2)
        b_in = Dmas(nc, ctx, "mx_b_in", 3)
        mla_out = Dmas(nc, ctx, "mx_mla_out", 10, 1)
        rwkv_out = Dmas(nc, ctx, "mx_rwkv_out", 1, 1)
        edge_out = Dmas(nc, ctx, "mx_edge_out", 1, 1)
        state_out = Dmas(nc, ctx, "mx_state_out", 1, 1)
        block = ctx.enter_context(nc.Block())


        def row(ap, i):
            return ap[bass.ds(i, 1)].rearrange("a p n -> p (a n)")

        def odd(ap, lev):
            return ap.rearrange("p h (k two b) -> p h k two b", two=2, b=2 ** lev)[:, :, :, 1, :]

        def even(ap, lev):
            return ap.rearrange("p h (k two b) -> p h k two b", two=2, b=2 ** lev)[:, :, :, 0, :]

        @block.sync
        def _(sp):
            for dst, src in ((w_uq, io["w_uq"]), (w_wa, io["w_wa"]), (levs, io["levs"]),
                             (cst, io["cst"]), (rmsw, io["rmsw"])):
                n = dst.shape[1]
                consts.go(sp.dma_start(dst[:], src.rearrange("p (a n) -> p a n", a=n)))
            for dst, src in ((w_g, io["w_g"]), (par, io["par"]), (ident, io["ident"])):
                consts.go(sp.dma_start(dst[:], src))
            x_in.go(sp.dma_start(x[:], io["x"][0]))
            w_cols = [(QL + KVL + 4 * k * P, QL + KVL + min(4 * k + 4, NPR) * P) for k in range(4)]
            w_src = io["w_in"].rearrange("p (a n) -> p a n", a=KC)
            for k, (c0, c1) in enumerate(w_cols):
                sp.dma_start(w_in[:, :, c0:c1], w_src[:, :, c0:c1]).then_inc(w_part[k], 16)
            for c0, c1 in ((0, QL + KVL), (WCOL - 2 * ROPE, WCOL)):
                sp.dma_start(w_in[:, :, c0:c1], w_src[:, :, c0:c1]).then_inc(w_part[4], 16)
            sp.wait_ge(first_x, 2)
            x_in.go(sp.dma_start(x[:], io["x"][1]))
            for d in (mla_out, rwkv_out, edge_out, state_out):
                sp.sem_inc(d.sem, 16 * d.n)

            def project(t, woven_in):
                t.ahead((aten, "x_transposed1", 0), (avec, "q_rope_sin", -1), (avec, "kpe_roped", 0),
                        (aact, "ckv_tokens", 0), (aact, "q_nope", 0), (avec, "q_roped", 0), (aact, "edges", 0))
                i = t.i if isinstance(t.i, int) else sp.snap(t.i)
                after = 2 if isinstance(i, int) else sp.snap(t.i + 2)
                col = bass.ds(i * P if isinstance(i, int) else sp.snap(t.i * P), P)
                yield
                t.w0(avec, "q_rope_sin")
                a_in.go(sp.dma_start(first[:], row(io["first"], i)))
                a_in.go(sp.dma_start(rope[:], row(io["rope"], i).rearrange("p (a n) -> p a n", a=2)))
                yield
                t.w(avec, "kpe_roped")
                mla_out.go(sp.dma_start(scr["kpeT"][:, col], kpe[:]))
                mla_out.go(sp.dma_start(scr["ckvT"].rearrange("(c p) n -> p c n", p=P)[:, :, col], ckv[:]))
                t.w(aact, "edges")
                edge_out.go(sp.dma_start(row(io["edge_out"], i), edge[:].rearrange("p a n -> p (a n)")))
                t.w(aact, "q_nope")
                qd = scr["qT"]
                for h2 in range(2):
                    mla_out.go(sp.dma_start(qd.rearrange("(c b) d n -> b d c n", b=2)[h2, 0:NOPE, :, col],
                                            qn[h2 * 64:h2 * 64 + 64]))
                t.w(avec, "q_roped")
                for h4 in range(4):
                    mla_out.go(sp.dma_start(qd.rearrange("(c b) d n -> b d c n", b=4)[h4, NOPE:QK, :, col],
                                            qp[h4 * 32:h4 * 32 + 32]))
                t.w(aact, "ckv_tokens")
                mla_out.go(sp.dma_start(row(io["ckv_out"], i), ckt[:, 0:KVL]))
                mla_out.go(sp.dma_start(row(io["kpe_out"], i), ckt[:, KVL:KVL + ROPE]))
                t.w(aten, "x_transposed1")
                x_in.go(sp.dma_start(x[:], row(io["x"], after)))

            def rwkv(t, woven_in):
                t.ahead((vec, "state_in", -1), (vec, "state", 0), (vec, "gated", 0))
                i = t.i if isinstance(t.i, int) else sp.snap(t.i)
                col = bass.ds(i * P if isinstance(i, int) else sp.snap(t.i * P), P)
                yield
                t.w0(vec, "state_in")
                b_in.go(sp.dma_start(masks[:], row(io["masks"], i).rearrange("p (a n) -> p a n", a=2)))
                b_in.go(sp.dma_start(keep_s[:], row(io["keep"], i)))
                b_in.go(sp.dma_start(s_init[:], row(io["s_init"], i).rearrange("p (a n) -> p a n", a=4)))
                yield
                t.w(vec, "state")
                state_out.go(sp.dma_start(row(io["state_out"], i), S[:].rearrange("p a n -> p (a n)")))
                t.w(vec, "gated")
                rwkv_out.go(sp.dma_start(scr["rwT"].rearrange("(c p) n -> p c n", p=P)[:, :, col], ys[:]))

            woven(sp, NT, None, None, project, rwkv, "abbaab")
            for d in (mla_out, rwkv_out, edge_out, state_out):
                sp.wait_ge(d.sem, d.done(NT - 1))
            sp.wait_ge(x_in.sem, x_in.done(NT + 1))

        @block.gpsimd
        def _(g):
            for buf, val in ((AR, 0.0), (cum, 0.0), (pr, 0.0), (S, 0.0), (ones, 1.0), (nought, 0.0)):
                g.memset(buf[:], val).then_inc(setup, 1)
            g.wait_ge(setup, 6)
            g.wait_ge(consts.sem, consts.done(0))

            def rwkv(t, woven_in):
                t.w(act, "exp_pos")
                t.w(vec, "u_r")
                t.w0(ten, "y")
                for h in range(2):
                    hs = slice(h * 64, h * 64 + 64)
                    ins = g.tensor_tensor(AR[hs, :, h, 1, :], u[hs, 0:4, :], ep[hs, :, 1:P + 1], ALU.mult)
                t.do(ins, "r_hat")
                t.w(vec, "kk_normed")
                t.do(g.tensor_tensor(t1[:], u[:, 0:4, :], kh[:], ALU.mult), "rk")
                t.do(g.tensor_tensor(t1[:], t1[:], bc(rkc, P), ALU.mult), "rkr")
                for c in range(2):
                    hs = slice(4 * c, 4 * c + 4)
                    t.w(vec, f"T_level0_{c}")
                    t.do(g.tensor_tensor(T[:, hs, :], T[:, hs, :], bm(ident[:, :], 4), ALU.add), f"T_start{c}")
                for lev in range(1, LEVELS):
                    t.w(ten, f"T{lev - 1}_1" if lev > 1 else "U0")
                    e = even(Z[:, :, :], lev)
                    zz = nought[:, 0:1].unsqueeze(2).unsqueeze(3).to_broadcast([P, H, P // 2 ** (lev + 1), 2 ** lev])
                    t.do(g.tensor_tensor(e, zz, zz, ALU.add), f"Z_clear{lev}")
                yield

            woven(g, NT, None, pol, None, rwkv, "")

        @block.scalar
        def _(a):
            a.wait_ge(consts.sem, consts.done(0))
            a.activation(negh[:], par[:, 20:28], ACT.Copy, scale=0.5).then_inc(biases, 1)
            a.activation(mu1[:], mu, ACT.Copy, scale=-1.0, bias=1.0).then_inc(biases, 1)
            a.wait_ge(biases, 2)
            a.wait_ge(setup, 6)
            for k in range(2):
                a.wait_ge(first_x, k + 1)
                a.activation(xT[:, 4 * k:4 * k + 4, :], b4[k], ACT.Copy).then_inc(first_xT, 1)

            def project(t, woven_in):
                t.w(avec, "pr_edge")
                for k in range(4):
                    n = min(4, NPR - 4 * k)
                    t.w(aten, f"pr_proj{k}")
                    t.mark(a.activation(pr[:, 4 * k:4 * k + n, 1:P + 1], b4[(2, 3, 0, 1)[k]][:, 0:n, :], ACT.Copy), f"pr{k}")
                    yield
                t.w(aact, "pr3")
                t.left(edge_out)
                a.activation(edge[:, 0, :], pr[:, :, DEC], ACT.Copy)
                t.mark(a.activation(edge[:, 1, :], pr[:, :, P], ACT.Copy), "edges")
                t.w(aten, "cq_proj")
                t.mark(a.activation(sq5[:, 0:3, :], b4[2][:, 0:3, :], ACT.Square), "cq_sq")
                t.w(aten, "ckv_proj")
                t.mark(a.activation(sq5[:, 3:5, :], b4[3][:, 0:2, :], ACT.Square), "ckv_sq")
                t.w(aten, "rms_sums")
                t.w0(avec, "ckv_normed")
                t.mark(a.activation(msr[:], b4[3][:, 2:4, :], ACT.Sqrt, bias=par[:, 48:49]), "rms_root")
                yield
                t.w(aten, "q_nope")
                t.left(mla_out)
                t.mark(a.activation(qn[:], b4[2], ACT.Copy), "q_nope")
                yield
                t.w(aten, "ckv_tokens")
                t.mark(a.activation(ckt[:], bank[2][:, 0:KVL + ROPE], ACT.Copy), "ckv_tokens")
                yield
                for k in range(2):
                    t.w(aten, f"x_transposed{k}")
                    t.mark(a.activation(xT[:, 4 * k:4 * k + 4, :], b4[k], ACT.Copy), f"xT{k}")

            def rwkv(t, woven_in):
                t.w(aact, "edges")
                for name, c0, c1 in (("low", 12, 14), ("k", 4, 8), ("r", 0, 4), ("v", 8, 12)):
                    if name == "low":
                        t.w0(ten, "b_tokens")
                        t.w0(pol, "rk")
                    for c in range(c0, c1):
                        ins = a.activation(u[:, c, :], pr[:, c, 1:P + 1], ACT.Copy, scale=mu1[:, c:c + 1])
                    t.mark(ins, "u_own_" + name)
                t.w(vec, "u_low")
                t.w0(ten, "lora_g")
                a.activation(lo[0:64, :], u[0:64, 12, :], ACT.Tanh)
                t.do(a.activation(sg[:], u[:, 13, :], ACT.Tanh, scale=0.5), "g_lo")
                yield
                t.w(ten, "lora_w")
                t.w(avec, "q_roped")
                for c in range(4):
                    ins = a.activation(lw[:, c, :], b4[4][:, c, :], ACT.Tanh, bias=negh[:, c:c + 1], scale=0.5)
                t.mark(ins, "w_tanh")
                t.w(ten, "lora_a")
                t.w0(vec, "gated")
                for c in range(4):
                    ins = a.activation(aa[:, c, :], b4[5][:, c, :], ACT.Tanh, bias=negh[:, 4 + c:5 + c], scale=0.5)
                t.mark(ins, "a_tanh")
                t.w(vec, "kk")
                t.mark(a.activation(t1[:], kk[:], ACT.Square), "kk_sq")
                t.w(ten, "lora_g")
                t.mark(a.activation(gg[:], b4[6], ACT.Copy), "g_out")
                t.w(vec, "mid")
                t.w0(pol, "r_hat")
                for c in range(4):
                    ins = a.activation(ep[:, c, :], cum[:, c, :], ACT.Exp, bias=nm[:, c:c + 1])
                t.mark(ins, "exp_pos")
                for c in range(4):
                    ins = a.activation(en[:, c, :], cum[:, c, :], ACT.Exp, bias=cum[:, c, 64:65], scale=-1.0)
                t.do(ins, "exp_neg")
                t.mark(a.activation(em[:], en[:, :, 0], ACT.Copy), "em")
                yield
                t.w(vec, "kk_norm2")
                t.mark(a.activation(t1[:], t1[:], ACT.Sqrt), "kk_root")
                yield
                t.w(ten, "v_tokens")
                t.mark(a.activation(vt[:], b4[4], ACT.Copy), "v_tokens")
                t.w(ten, "U0")
                t.w0(vec, f"U{LEVELS}_1")
                for c in range(2):
                    ins = a.activation(U[:, 4 * c:4 * c + 4, :], b4[6 + c], ACT.Copy)
                t.mark(ins, "U0")
                yield
                t.w(ten, "G")
                t.mark(a.activation(Gs[:], bank[3][:, :], ACT.Copy), "G")
                yield
                t.w(ten, "b_tokens")
                t.mark(a.activation(bt, b4[0], ACT.Copy), "b_tokens")
                t.w(ten, "k_tokens")
                t.mark(a.activation(kt, b4[1], ACT.Copy), "k_tokens")
                t.w(ten, "SA")
                t.mark(a.activation(SA, bank[6][:, :], ACT.Copy), "SA")
                yield
                t.w(ten, "y")
                t.left(rwkv_out)
                t.mark(a.activation(ys[:], b4[4], ACT.Copy), "y")
                t.w(vec, "y_centred")
                t.mark(a.activation(yq, ys[:], ACT.Square), "y_sq")
                yield
                t.w(ten, "y_var")
                t.mark(a.activation(yq, b4[6], ACT.Sqrt, bias=par[:, 49:50]), "y_root")
                yield
                t.w(vec, "y_normed")
                for c in range(4):
                    ins = a.activation(ys[:, c, :], ys[:, c, :], ACT.Identity, bias=lxb[:, c:c + 1], scale=lxg[:, c:c + 1])
                t.mark(ins, "y_gain")

            woven(a, NT, aact, act, project, rwkv, ACT_ORDER)

        @block.tensor
        def _(pe):
            pe.wait_ge(consts.sem, consts.done(0))
            pe.wait_ge(setup, 6)

            def proj(dst, col, n=P):
                for k in range(KC):
                    ins = pe.matmul(dst, w_in[:, k, col:col + n], xT[:, k, :], start=(k == 0), stop=(k == KC - 1))
                return ins

            def transposed(k):
                for c in range(4):
                    ins = pe.transpose(b4[k][:, c, :], x[:, (4 * k + c) * P:(4 * k + c + 1) * P], ident[:, :])
                return ins

            pe.wait_ge(x_in.sem, x_in.done(0))
            for k in range(2):
                transposed(k).then_inc(first_x, 1)
            pe.wait_ge(first_xT, 2)

            def project(t, woven_in):
                t.w0(aact, "xT1")
                t.w0(avec, "q_roped")
                for k in range(4):
                    if k == 3:
                        t.w(aact, "pr0")
                    if not woven_in:
                        pe.wait_ge(w_part[k], 16)
                    for c in range(min(4, NPR - 4 * k)):
                        ins = proj(b4[(2, 3, 0, 1)[k]][:, c, :], QL + KVL + (4 * k + c) * P)
                    t.mark(ins, f"pr_proj{k}")
                    yield
                t.w(aact, "pr1")
                if not woven_in:
                    pe.wait_ge(w_part[4], 32)
                for c in range(CQ):
                    proj(b4[2][:, c, :], c * P)
                t.mark(proj(b4[2][0:64, 3, :], WCOL - 64, 64), "cq_proj")
                for c in range(CKV):
                    ins = proj(b4[3][:, c, :], QL + c * P)
                t.mark(ins, "ckv_proj")
                t.w(aact, "ckv_sq")
                for c in range(CQ):
                    pe.matmul(b4[3][:, 2, :], rmsw[:, 0, :], sq5[:, c, :], start=(c == 0), stop=(c == CQ - 1))
                for c in range(CKV):
                    ins = pe.matmul(b4[3][:, 3, :], rmsw[:, 1, :], sq5[:, CQ + c, :], start=(c == 0), stop=(c == CKV - 1))
                t.mark(ins, "rms_sums")
                yield
                t.w(avec, "kpe_roped")
                for c in range(4):
                    for k in range(CQ):
                        ins = pe.matmul(b4[2][:, c, :], w_uq[:, k, c * P:(c + 1) * P], cq[:, k, :],
                                        start=(k == 0), stop=(k == CQ - 1))
                    if c == 1:
                        yield
                t.mark(ins, "q_nope")
                yield
                t.w0(act, "G")
                for c in range(4):
                    for k in range(CQ):
                        ins = pe.matmul(b4[3][:, c, :], w_uq[:, k, 512 + c * P:512 + (c + 1) * P], cq[:, k, :],
                                        start=(k == 0), stop=(k == CQ - 1))
                    if c == 1:
                        yield
                t.mark(ins, "q_pe")
                yield
                t.w(aact, "q_nope")
                for c in range(CKV):
                    pe.transpose(bank[2][:, c * P:(c + 1) * P], ckv[:, c, :], ident[:, :])
                t.mark(pe.transpose(bank[2][:, KVL:KVL + ROPE], kpe[:], ident[0:32, 0:32]), "ckv_tokens")
                yield
                t._wait(x_in, None, 1)
                t.w0(act, "k_tokens")
                for k in range(2):
                    t.mark(transposed(k), f"x_transposed{k}")

            def rwkv(t, woven_in):
                t.w(act, "g_lo")
                t.w(vec, "g_sig")
                for c in range(4):
                    ins = pe.matmul(b4[4][:, c, :], w_wa[:, 0, c * P:(c + 1) * P], lo[:], start=True, stop=True)
                t.mark(ins, "lora_w")
                for c in range(4):
                    ins = pe.matmul(b4[5][:, c, :], w_wa[:, 1, c * P:(c + 1) * P], lo[:], start=True, stop=True)
                t.mark(ins, "lora_a")
                for c in range(4):
                    ins = pe.matmul(b4[6][:, c, :], w_g[:, c * P:(c + 1) * P], sg[:], start=True, stop=True)
                t.mark(ins, "lora_g")
                yield
                t.w(act, "kk_sq")
                t.mark(pe.matmul(bank[7][:, :], bones, t1[:].rearrange("p a n -> p (a n)"), start=True, stop=True),
                       "kk_norm")
                yield
                t.w(act, "w_tanh")
                t.w(vec, "u_v")
                for c in range(4):
                    ins = pe.transpose(b4[4][:, c, :], u[:, 8 + c, :], ident[:, :])
                t.mark(ins, "v_tokens")
                t.w(pol, "rkr")
                t.w(act, "g_out")
                t.mark(pe.matmul(bank[5][:, :], bones, t1[:].rearrange("p a n -> p (a n)"), start=True, stop=True),
                       "bonus_sum")
                t.w(vec, "b_hat")
                for g in range(2):
                    for h in range(4):
                        hh = 4 * g + h
                        ins = pe.matmul(b4[6 + g][:, h, :], AR[:, hh // 2, hh % 2, 0, :], bh[:, hh // 2, :],
                                        start=True, stop=True)
                    t.mark(ins, f"gram_l{g}")
                t.w(act, "v_tokens")
                t.w(vec, "bonus")
                for g in range(2):
                    for h in range(4):
                        hh = 4 * g + h
                        ins = pe.matmul(b4[4 + g][:, h, :], bh[:, hh // 2, :], AR[:, hh // 2, hh % 2, 1, :],
                                        start=True, stop=True)
                    t.mark(ins, f"gram_b{g}")
                if woven_in:
                    t.next_done(aact, "edges")
                for q in range(4):
                    b = (0, 1, 4, 5)[q]
                    if q == 2:
                        t.w(vec, "RB1")
                    for h in range(2):
                        ins = pe.matmul(bank[b][:, h * 256:(h + 1) * 256], kh[:, q, :],
                                        AR[:, q, h].rearrange("p a n -> p (a n)"), start=True, stop=True)
                    t.mark(ins, f"gram_k{q}")
                t.w(pol, "T_start1")
                t.w(vec, "L1")
                for h in range(H):
                    ins = pe.transpose(b4[6 + h // 4][:, h % 4, :], T[:, h, :], ident[:, :])
                t.mark(ins, "U0")
                yield
                for lev in range(1, LEVELS + 1):
                    n = 64
                    for g in range(2):
                        if lev == 1:
                            if g == 0:
                                t.w(act, "U0")
                                t.w(vec, "MK3")
                        else:
                            t.w(vec, f"U{lev - 1}_{g}")
                        for h in range(4):
                            ins = pe.matmul(bank[4 + g][:, h * n:(h + 1) * n], L[:, 4 * g + h, :],
                                            odd(U[:, 4 * g + h:4 * g + h + 1, :], lev), start=True, stop=True)
                        t.mark(ins, f"Z{lev}_{g}")
                    for g in range(2):
                        t.w(vec, f"Z{lev}_{g}")
                        for h in range(4):
                            ins = pe.matmul(bank[6 + g][:, h * n:(h + 1) * n], T[:, 4 * g + h, :],
                                            odd(Z[:, 4 * g + h:4 * g + h + 1, :], lev), start=True, stop=True)
                        t.mark(ins, f"U{lev}_{g}")
                        if lev < LEVELS:
                            if g == 0:
                                t.w(pol, f"Z_clear{lev}")
                            for h in range(4):
                                ins = pe.matmul(bank[g][:, h * n:(h + 1) * n], Z[:, 4 * g + h, :],
                                                even(T[:, 4 * g + h:4 * g + h + 1, :], lev), start=True, stop=True)
                            t.mark(ins, f"T{lev}_{g}")
                    yield
                    if lev == 1:
                        for h in range(H):
                            q, hs = h // 2, slice(h % 2 * 64, h % 2 * 64 + 64)
                            o = bank[3][:, h * 64:h * 64 + 64]
                            pe.matmul(o, AR[:, q, h % 2, 0, :], Sp[:, q, :], start=True, stop=False)
                            ins = pe.matmul(o, MK[:, h, 0, :], vt[:, q, hs], start=False, stop=True)
                        t.mark(ins, "G")
                        yield
                for c in range(4):
                    ins = pe.transpose(b4[0][:, c, :], bh[:, c, :], ident[:, :])
                t.mark(ins, "b_tokens")
                for c in range(4):
                    ins = pe.transpose(b4[1][:, c, :], kh[:, c, :], ident[:, :])
                t.mark(ins, "k_tokens")
                t.w(act, "G")
                t.w(vec, f"U{LEVELS}_1")
                for h in range(H):
                    ins = pe.matmul(bank[6][:, h * 64:h * 64 + 64], U[:, h, :], Gs[:, h * 64:h * 64 + 64],
                                    start=True, stop=True)
                t.mark(ins, "SA")
                yield
                t.w(act, "SA")
                for h in range(H):
                    q, hs = h // 2, slice(h % 2 * 64, h % 2 * 64 + 64)
                    o = b4[4][hs, q, :]
                    pe.matmul(o, Sp[:, q, :], AR[:, q, h % 2, 1, :], start=True, stop=False)
                    pe.matmul(o, SA[:, h * 64:h * 64 + 64], RB[:, h, :], start=False, stop=False)
                    ins = pe.matmul(o, vt[:, q, hs], MK[:, h, 1, :], start=False, stop=True)
                t.mark(ins, "y")
                for h in range(H):
                    q, hs = h // 2, slice(h % 2 * 64, h % 2 * 64 + 64)
                    o = bank[5][hs, q * 64:q * 64 + 64]
                    pe.matmul(o, bt[:, q, hs], SA[:, h * 64:h * 64 + 64], start=True, stop=False)
                    ins = pe.matmul(o, kt[:, q, hs], vt[:, q, hs], start=False, stop=True)
                t.mark(ins, "state_add")
                yield
                t.w(act, "y")
                t.mark(pe.matmul(bank[7][:, :], bmean, ys[:].rearrange("p a n -> p (a n)"), start=True, stop=True),
                       "y_mean")
                yield
                t.w(act, "y_sq")
                t.mark(pe.matmul(b4[6], bmean, yq, start=True, stop=True), "y_var")

            woven(pe, NT, aten, ten, project, rwkv, PE_ORDER)

        @block.vector
        def _(v):
            v.wait_ge(consts.sem, consts.done(0))
            v.wait_ge(biases, 2)
            v.wait_ge(setup, 6)

            def project(t, woven_in):
                do = t.do
                t.arrived(a_in)
                t.w0(aact, "edges")
                do(v.scalar_tensor_tensor(out=pr[:, :, 0], in0=pr[:, :, P], scalar=keep, in1=shift0,
                                          op0=ALU.mult, op1=ALU.add), "pr_edge")
                yield
                t.w(aact, "rms_root")
                do(v.reciprocal(msr[:], msr[:]), "rms")
                t.w0(aten, "q_pe")
                for c in range(CQ):
                    ins = v.scalar_tensor_tensor(out=cq[:, c, :], in0=b4[2][:, c, :], scalar=qg[:, c:c + 1],
                                                 in1=msr[:, 0, :], op0=ALU.mult, op1=ALU.mult)
                do(ins, "cq_normed")
                t.left(mla_out)
                for c in range(CKV):
                    ins = v.scalar_tensor_tensor(out=ckv[:, c, :], in0=b4[3][:, c, :], scalar=kvg[:, c:c + 1],
                                                 in1=msr[:, 1, :], op0=ALU.mult, op1=ALU.mult)
                do(ins, "ckv_normed")
                do(v.tensor_tensor(kpe2[0:32, :], b4[2][0:32, 3, :], rope[0:32, 0, :], ALU.mult), "kpe_cos")
                do(v.tensor_tensor(kpe[:], b4[2][32:64, 3, :], rope[32:64, 1, :], ALU.mult), "kpe_sin")
                do(v.tensor_tensor(kpe[:], kpe[:], kpe2[0:32, :], ALU.add), "kpe_roped")
                yield
                t.w(aten, "q_pe")
                do(v.tensor_tensor(qp[:], b4[3][:, 0:2, :], bm(rope[:, 0, :], 2), ALU.mult), "q_rope_cos")
                do(v.tensor_tensor(qr, b4[3][:, 2:4, :], bm(rope[:, 1, :], 2), ALU.mult), "q_rope_sin")
                do(v.tensor_tensor(qp[:], qp[:], qr, ALU.add), "q_roped")

            def rwkv(t, woven_in):
                do = t.do
                for name, c0, c1 in (("low", 12, 14), ("k", 4, 8), ("r", 0, 4), ("v", 8, 12)):
                    t.w(act, "u_own_" + name)
                    for c in range(c0, c1):
                        ins = v.scalar_tensor_tensor(out=u[:, c, :], in0=pr[:, c, 0:P], scalar=mu[:, c:c + 1],
                                                     in1=u[:, c, :], op0=ALU.mult, op1=ALU.add)
                    do(ins, "u_" + name)
                    if name == "low":
                        t.w0(ten, "lora_a")
                        t.mark(v.tensor_copy(lo[64:128, :], u[64:128, 12, :]), "a_lo")
                    if name == "k":
                        t.w(act, "g_lo")
                        t.mark(v.tensor_scalar(sg[:], sg[:], 0.5, 0.5, ALU.mult, ALU.add), "g_sig")
                        do(v.tensor_tensor(kk[:], u[:, 4:8, :], bc(kkc, P), ALU.mult), "kk")
                yield
                t.arrived(b_in)
                t.w(act, "w_tanh")
                do(v.scalar_tensor_tensor(out=lw[:], in0=lw[:], scalar=1.0, in1=bm(vm, 4), op0=ALU.add, op1=ALU.mult),
                   "log_w")
                for c in range(4):
                    ins = v.tensor_tensor_scan(cum[:, c, 1:P + 1], ones[:], lw[:, c, :], 0.0, ALU.mult, ALU.add)
                do(ins, "cum")
                do(v.tensor_scalar(nm[:], cum[:, :, 64], -1.0, None, ALU.mult), "mid")
                t.w(act, "a_tanh")
                do(v.tensor_scalar(aa[:], aa[:], 0.5, 0.5, ALU.mult, ALU.add), "a_sig")
                do(v.scalar_tensor_tensor(out=kh[:], in0=aa[:], scalar=-1.0, in1=bc(kac, P), op0=ALU.add, op1=ALU.mult),
                   "a_ka")
                do(v.scalar_tensor_tensor(out=kh[:], in0=kh[:], scalar=1.0, in1=u[:, 4:8, :], op0=ALU.add, op1=ALU.mult),
                   "kh")
                t.w(ten, "kk_norm")
                do(v.tensor_scalar(t1[:], b4[7], 1e-24, None, ALU.max), "kk_norm2")
                t.w(act, "kk_root")
                do(v.reciprocal(t1[:], t1[:]), "kk_rs")
                do(v.tensor_tensor(kk[:], kk[:], t1[:], ALU.mult), "kk_normed")
                for h in range(2):
                    hs = slice(h * 64, h * 64 + 64)
                    ins = v.scalar_tensor_tensor(out=AR[hs, :, h, 0, :], in0=kk[hs], scalar=-1.0, in1=ep[hs, :, 0:P],
                                                 op0=ALU.mult, op1=ALU.mult)
                do(ins, "a_hat")
                do(v.tensor_tensor(en[:, :, 1:P + 1], en[:, :, 1:P + 1], bm(valid, 4), ALU.mult), "en_masked")
                do(v.tensor_tensor(bh, kk[:], aa[:], ALU.mult), "b_gate")
                do(v.tensor_tensor(bh, bh, en[:, :, 1:P + 1], ALU.mult), "b_hat")
                t.w(pol, "rk")
                do(v.tensor_tensor(kh[:], kh[:], en[:, :, 1:P + 1], ALU.mult), "k_hat")
                yield
                t.w(ten, "bonus_sum")
                do(v.tensor_tensor(bon[:], b4[5], u[:, 8:12, :], ALU.mult), "bonus")
                for g in range(2):
                    hs = slice(4 * g, 4 * g + 4)
                    t.w(ten, f"gram_l{g}")
                    v.tensor_tensor(L[:, hs, :], b4[6 + g], bm(low, 4), ALU.mult)
                    t.mark(v.tensor_tensor(T[:, hs, :], b4[6 + g], bm(lev0T, 4), ALU.mult), f"T_level0_{g}")
                t.mark(v.tensor_copy(spare[:], nm[:, 0:1]), "L1")
                for g in range(2):
                    hs = slice(4 * g, 4 * g + 4)
                    t.w(ten, f"gram_b{g}")
                    t.mark(v.tensor_tensor(RB[:, hs, :], b4[4 + g], bm(incl, 4), ALU.mult), f"RB{g}")
                t.left(state_out)
                do(v.scalar_tensor_tensor(out=S[:], in0=S[:], scalar=keep_s[:, 0:1], in1=s_init[:], op0=ALU.mult,
                                          op1=ALU.add), "state_in")
                t.w(act, "em")
                do(v.tensor_tensor(Sp[:], S[:], bc(em[:], VD), ALU.mult), "state_mid")
                for q in range(4):
                    t.w(ten, f"gram_k{q}")
                    g4 = bank[(0, 1, 4, 5)[q]][:, :].rearrange("p (h a n) -> p h a n", h=2, a=2)
                    t.mark(v.tensor_tensor(MK[:, 2 * q:2 * q + 2], g4, upper2.unsqueeze(1).to_broadcast([P, 2, 2, P]),
                                           ALU.mult), f"MK{q}")
                yield
                for lev in range(1, LEVELS + 1):
                    def view(b):
                        return b[:, 0:256].rearrange("p (h k b) -> p h k b", h=4, b=2 ** lev)

                    mask = levs[:, lev - 1, :].rearrange("p (k b) -> p k b", b=2 ** lev)
                    mask = mask.unsqueeze(1).to_broadcast([P, 4, mask.shape[1], mask.shape[2]])
                    for g in range(2):
                        hs = slice(4 * g, 4 * g + 4)
                        t.w(ten, f"Z{lev}_{g}")
                        t.mark(v.tensor_tensor(odd(Z[:, hs, :], lev), view(bank[4 + g]), mask, ALU.mult), f"Z{lev}_{g}")
                    for g in range(2):
                        hs = slice(4 * g, 4 * g + 4)
                        t.w(ten, f"U{lev}_{g}")
                        o = odd(U[:, hs, :], lev)
                        t.mark(v.tensor_tensor(o, view(bank[6 + g]), o, ALU.add), f"U{lev}_{g}")
                        if lev < LEVELS:
                            t.w(ten, f"T{lev}_{g}")
                            e = even(T[:, hs, :], lev)
                            t.mark(v.tensor_tensor(e, view(bank[g]), e, ALU.add), f"T{lev}_{g}")
                    yield
                t.w(ten, "state_add")
                do(v.tensor_tensor(S[:], bank[5][:, 0:256].rearrange("p (a n) -> p a n", a=4), Sp[:], ALU.add),
                   "state_sum")
                do(v.tensor_tensor(S[:], S[:], ep[:, :, P:P + 1].to_broadcast([P, 4, VD]), ALU.mult), "state")
                yield
                t.w(ten, "y_mean")
                do(v.tensor_tensor(ys[:], ys[:], b4[7], ALU.subtract), "y_centred")
                yield
                t.w(act, "y_root")
                do(v.reciprocal(yq, yq), "y_rs")
                do(v.tensor_tensor(ys[:], ys[:], yq, ALU.mult), "y_normed")
                yield
                t.w(act, "y_gain")
                do(v.tensor_tensor(ys[:], ys[:], bon[:], ALU.add), "y_bonus")
                do(v.tensor_tensor(ys[:], ys[:], gg[:], ALU.mult), "gated")

            woven(v, NT, avec, vec, project, rwkv, VEC_ORDER)


def attention(nc, io, scr):
    KT = SEQ // P + 2
    with ExitStack() as ctx:
        def sb(name, shape, dt=F32):
            return ctx.enter_context(nc.sbuf_tensor("at_" + name, shape, dt))

        bank = [ctx.enter_context(nc.psum_tensor(f"at_bank{b}", [P, 512], F32)) for b in range(8)]
        ident = sb("ident", [P, P])
        lat = sb("lat", [P, CKV, KT * P])
        kT = sb("kT", [P, KT * P])
        qT = sb("qT", [P, TOK])
        w = sb("w", [P, CKV, P])
        vals = sb("vals", [P, KT, VD])
        mx = sb("mx", [P, 5])
        nm = sb("nm", [P, NT])
        nms = sb("nms", [P, NT])
        sums = sb("sums", [P, NT, 5])
        total = sb("total", [P, 1])
        rec = sb("rec", [P, 1])
        zero = sb("zero", [P, 64])
        AHEAD, SB, TB = 4, 5, 2
        LAG = 3
        NP = 4
        PQ = sb("PQ", [P, NP, 4 * P])
        PT = sb("PT", [P, NP, 4, P])
        o_sb = sb("o_sb", [P, NT, VD])

        ten, vec, act, pol = (Steps(nc, ctx, "attention_" + n) for n in ("tensor", "vector", "scalar", "gpsimd"))
        latents = Dmas(nc, ctx, "at_latents", 7)
        setup = ctx.enter_context(nc.semaphore("at_setup"))
        w_in = Dmas(nc, ctx, "at_w_in", 1)
        q_in = Dmas(nc, ctx, "at_q_in", 1)
        o_out = Dmas(nc, ctx, "at_o_out", 1, 1)
        block = ctx.enter_context(nc.Block())

        def groups(j):
            if j == NT - 1:
                return [(KT - 2, 2, DEC)]
            return [(k, min(4, j + 1 - k), P) for k in range(0, j + 1, 4)]

        chunks = [(j, g) for j in range(NT) for g in range(len(groups(j)))]
        count = len(chunks)

        def width(n):
            j, g = chunks[n]
            k0, k, last = groups(j)[g]
            return (k - 1) * P + last, g == len(groups(j)) - 1 and j < NT - 1

        last_use = {n: max(m for m in range(count) if m % NP == n % NP) for n in range(NP)}

        def ends(n):
            return n == count - 1 or chunks[n + 1][0] != chunks[n][0]

        @block.sync
        def _(sp):
            n = SEQ
            lt = scr["ckvT"].rearrange("(c p) n -> p c n", p=P)
            sp.dma_start(lat[:, :, 0:n], lt[:, :, 0:n]).then_inc(latents.sem, 16)
            sp.dma_start(lat[:, :, n:n + P], io["past_ckvT"].rearrange("p (c n) -> p c n", c=CKV)).then_inc(latents.sem, 16)
            sp.dma_start(lat[:, :, n + P:n + 2 * P], lt[:, :, n:n + P]).then_inc(latents.sem, 16)
            sp.dma_start(kT[NOPE:QK, 0:n], scr["kpeT"][:, 0:n]).then_inc(latents.sem, 16)
            sp.dma_start(kT[NOPE:QK, n:n + P], io["past_kpeT"]).then_inc(latents.sem, 16)
            sp.dma_start(kT[NOPE:QK, n + P:n + 2 * P], scr["kpeT"][:, n:n + P]).then_inc(latents.sem, 16)
            sp.dma_start(ident[:], io["ident"]).then_inc(latents.sem, 16)
            sp.sem_inc(o_out.sem, 16)

            last_scores = f"S{count - 1}"

            def loads(t, woven_in):
                t.ahead((ten, "V2", -1), (ten, last_scores, -1))
                i = bass.ds(t.i if isinstance(t.i, int) else sp.snap(t.i), 1)
                yield
                t.w0(ten, "V2")
                w_in.go(sp.dma_start(w[:], io["w_ukv"][i].rearrange("a p (c n) -> p (a c) n", c=CKV)))
                t.w0(ten, last_scores)
                q_in.go(sp.dma_start(qT[0:QK, :], scr["qT"][i].rearrange("a d n -> d (a n)")))

            def stores(t, woven_in):
                t.ahead((vec, "out_16", 0))
                hs = bass.ds(t.i * VD if isinstance(t.i, int) else sp.snap(t.i * VD), VD)
                yield
                t.w(vec, "out_16")
                o_out.go(sp.dma_start(scr["attn"].rearrange("(t p) c -> p t c", p=P)[:, :, hs], o_sb[:]))

            woven(sp, H, None, None, loads, stores, "abab")
            sp.wait_ge(o_out.sem, o_out.done(H - 1))

        @block.gpsimd
        def _(g):
            g.memset(sums[:], 0.0).then_inc(setup, 1)
            g.memset(mx[:], -3e38).then_inc(setup, 1)
            g.memset(zero[:], 0.0).then_inc(setup, 1)
            g.wait_ge(setup, 3)

            def turn(t):
                for n in range(count):
                    wd, corner = width(n)
                    if corner:
                        if n >= NP:
                            t.w(ten, f"PT{n - NP}")
                        else:
                            t.w0(ten, f"PT{last_use[n]}")
                        t.mark(g.tensor_tensor(PQ[0:64, n % NP, wd - 64:wd], zero[0:64, :], zero[0:64, :], ALU.add), f"corner{n}")

            engine_loop(g, pol, H, turn)

        @block.scalar
        def _(a):
            a.wait_ge(setup, 3)

            def turn(t):
                for n in range(5):
                    t.w(ten, f"K{n}")
                    wd = min(512, KT * P - 512 * n)
                    t.mark(a.activation(kT[0:NOPE, 512 * n:512 * n + wd], bank[n][0:NOPE, 0:wd], ACT.Copy), f"K{n}")
                for n in range(count):
                    j, gi = chunks[n]
                    wd, corner = width(n)
                    if gi == 0:
                        t.w(vec, f"negmax{j}")
                    if n >= NP:
                        t.w(ten, f"PT{n - NP}")
                    bias = nms[:, j:j + 1]
                    b = bank[n % SB]
                    full = wd - 64 if corner else wd
                    ins = a.activation(PQ[:, n % NP, 0:full], b[:, 0:full], ACT.Exp, bias=bias, scale=SCALE,
                                       accum_out=sums[:, j, 1 + gi:2 + gi])
                    if corner:
                        ins = a.activation(PQ[64:P, n % NP, full:wd], b[64:P, full:wd], ACT.Exp, bias=bias[64:P],
                                           scale=SCALE, accum_out=sums[64:P, j, 0:1])
                    t.mark(ins, f"exp{n}")

            engine_loop(a, act, H, turn)

        @block.tensor
        def _(pe):
            pe.wait_ge(latents.sem, latents.done(0))
            pe.wait_ge(setup, 3)

            def scores(t, n):
                j, gi = chunks[n]
                k0 = groups(j)[gi][0]
                wd, _ = width(n)
                if n >= SB:
                    t.w(act, f"exp{n - SB}")
                t.mark(pe.matmul(bank[n % SB][:, 0:wd], qT[0:QK, j * P:(j + 1) * P], kT[0:QK, k0 * P:k0 * P + wd],
                                 start=True, stop=True), f"S{n}")

            def transposes(t, n):
                wd, corner = width(n)
                t.w(act, f"exp{n}")
                if n >= TB:
                    t.w(vec, f"PT{n - TB}")
                if corner:
                    t.w(pol, f"corner{n}")
                for c in range(0, wd, P):
                    rows = min(P, wd - c)
                    ins = pe.transpose(bank[SB + n % TB][0:rows, c:c + P], PQ[:, n % NP, c:c + rows], ident[:, :])
                t.mark(ins, f"PT{n}")

            def values(t, n):
                j, gi = chunks[n]
                k0, k, last = groups(j)[gi]
                t.w(vec, f"PT{n}" if gi > 0 or j == 0 else f"out_{j - 1}")
                for s in range(k):
                    rows = last if s == k - 1 else P
                    ins = pe.matmul(bank[7][:, VD * (j % 2):VD * (j % 2) + VD], PT[0:rows, n % NP, s, :],
                                    vals[0:rows, k0 + s, :], start=(gi == 0 and s == 0), stop=(ends(n) and s == k - 1))
                t.mark(ins, f"PV{n}")

            def turn(t):
                t.arrived(w_in)
                t.w0(vec, "out_16")
                t.w0(act, f"exp{count - 1}")
                for n in range(5):
                    wd = min(512, KT * P - 512 * n)
                    for c in range(CKV):
                        ins = pe.matmul(bank[n][0:NOPE, 0:wd], w[:, c, 0:NOPE], lat[:, c, 512 * n:512 * n + wd],
                                        start=(c == 0), stop=(c == CKV - 1))
                    t.mark(ins, f"K{n}")
                for n in range(3):
                    b = bank[5 + n]
                    for k in range(8 * n, min(8 * n + 8, KT)):
                        for c in range(CKV):
                            ins = pe.matmul(b[:, (k % 8) * VD:(k % 8 + 1) * VD], lat[:, c, k * P:(k + 1) * P],
                                            w[:, c, NOPE:P], start=(c == 0), stop=(c == CKV - 1))
                    t.mark(ins, f"V{n}")
                t.w(act, "K4")
                t.w(vec, "V2")
                t.arrived(q_in)
                for n in range(AHEAD):
                    scores(t, n)
                for n in range(count):
                    if n + AHEAD < count:
                        scores(t, n + AHEAD)
                    if n >= LAG:
                        values(t, n - LAG)
                    transposes(t, n)
                for n in range(count - LAG, count):
                    values(t, n)

            engine_loop(pe, ten, H, turn)

        @block.vector
        def _(v):
            v.wait_ge(setup, 3)

            def maxima(t, n):
                j, gi = chunks[n]
                wd, corner = width(n)
                t.w(ten, f"S{n}")
                b = bank[n % SB]
                if corner:
                    v.tensor_reduce(mx[64:P, 0:1], b[64:P, wd - 64:wd], AX.X, ALU.max)
                    wd -= 64
                elif j == NT - 1:
                    v.tensor_reduce(mx[64:P, 0:1], b[64:P, 0:64], AX.X, ALU.max)
                t.do(v.tensor_reduce(mx[:, 1 + gi:2 + gi], b[:, 0:wd], AX.X, ALU.max), f"max{n}")
                if ends(n):
                    t.do(v.tensor_reduce(nm[:, j:j + 1], mx[:, 0:2 + gi], AX.X, ALU.max, negate=True), f"rowmax{j}")
                    t.mark(v.tensor_scalar(nms[:, j:j + 1], nm[:, j:j + 1], SCALE, None, ALU.mult), f"negmax{j}")

            def output(t, n):
                j, gi = chunks[n]
                t.w(ten, f"PV{n}")
                t.w(act, f"exp{n}")
                if j == 0:
                    t.left(o_out)
                t.do(v.tensor_reduce(total[:], sums[:, j, 0:2 + gi], AX.X, ALU.add), f"sum{j}")
                t.do(v.reciprocal(rec[:], total[:]), f"sum_rec{j}")
                t.mark(v.tensor_scalar(o_sb[:, j, :], bank[7][:, VD * (j % 2):VD * (j % 2) + VD], rec[:, 0:1], None,
                                       ALU.mult), f"out_{j}")

            def turn(t):
                for n in range(3):
                    t.w(ten, f"V{n}")
                    k = min(8, KT - 8 * n)
                    t.mark(v.tensor_copy(vals[:, 8 * n:8 * n + k, :],
                                         bank[5 + n][:, 0:k * VD].rearrange("p (a n) -> p a n", a=k)), f"V{n}")
                for n in range(AHEAD):
                    maxima(t, n)
                for n in range(count):
                    if n + AHEAD < count:
                        maxima(t, n + AHEAD)
                    if n >= LAG and ends(n - LAG):
                        output(t, n - LAG)
                    t.w(ten, f"PT{n}")
                    wd, _ = width(n)
                    full, rest = wd // P, wd % P
                    b = bank[SB + n % TB]
                    ins = v.tensor_copy(PT[:, n % NP, 0:full, :], b[:, 0:full * P].rearrange("p (a n) -> p a n", a=full))
                    if rest:
                        ins = v.tensor_copy(PT[0:rest, n % NP, full, :], b[0:rest, full * P:(full + 1) * P])
                    t.mark(ins, f"PT{n}")
                for n in range(count - LAG, count):
                    if ends(n):
                        output(t, n)

            engine_loop(v, vec, H, turn)


def router(nc, io, scr, keep):
    oh, gate, lgs = keep["onehot"], keep["gate"], keep["logits"]
    with ExitStack() as ctx:
        def sb(name, shape, dt=F32):
            return ctx.enter_context(nc.sbuf_tensor("ro_" + name, shape, dt))

        bank = [ctx.enter_context(nc.psum_tensor(f"ro_bank{b}", [P, 512], F32)) for b in range(8)]
        b4 = [b[:, :].rearrange("p (a n) -> p a n", a=4) for b in bank]
        w_o = sb("w_o", [P, KC, D])
        w_r = sb("w_r", [P, KC, NR])
        rows = sb("rows", [P, 2, D])
        small = sb("small", [P, NR + NG + EPG])
        bias, prio4, prio8 = small[:, 0:NR], small[:, NR:NR + NG], small[:, NR + NG:]
        ident = sb("ident", [P, P])
        eps = sb("eps", [P, 1])
        vcol = sb("vcol", [P, NT])
        at = sb("at", [P, 512])
        mix_a = sb("mix_a", [P, 4, P])
        mix_r = sb("mix_r", [P, 4, P])
        x = sb("x", [P, D])
        r = sb("r", [P, D])
        n = sb("n", [P, D])
        h = sb("h", [P, D])
        hT = sb("hT", [P, KC, P])
        st = sb("st", [P, 2, 6])
        mv = sb("mv", [P, 2])
        rstd, nmr = sb("rstd", [P, 1]), sb("nmr", [P, 1])
        one = sb("one", [P, 8, NT])
        ohg = sb("ohg", [P, NT, NG])
        eg = sb("eg", [P, NT, NG])
        ing = sb("ing", [P, NT, NE])
        ein, e2, pr8, o1, o2 = (sb(name, [P, NT, EPG]) for name in ("ein", "e2", "pr8", "o1", "o2"))

        A = {e: Steps(nc, ctx, "proj_" + e) for e in ("tensor", "vector", "scalar", "gpsimd")}
        B = {e: Steps(nc, ctx, "route_" + e) for e in ("tensor", "vector", "scalar")}
        aten, avec, aact, apol = A["tensor"], A["vector"], A["scalar"], A["gpsimd"]
        bten, bvec, bact = B["tensor"], B["vector"], B["scalar"]
        chosen = ctx.enter_context(nc.semaphore("ro_chosen"))
        exps = ctx.enter_context(nc.semaphore("ro_exps"))
        consts = Dmas(nc, ctx, "ro_consts", 7)
        at_in = Dmas(nc, ctx, "ro_at_in", 1)
        mix_in = Dmas(nc, ctx, "ro_mix_in", 1)
        x_in = Dmas(nc, ctx, "ro_x_in", 1)
        h_out = Dmas(nc, ctx, "ro_h_out", 1, 1)
        block = ctx.enter_context(nc.Block())

        @block.sync
        def _(sp):
            for dst, src, k in ((w_o, io["w_o"], KC), (w_r, io["w_r"], KC)):
                sp.dma_start(dst[:], src.rearrange("p (a n) -> p a n", a=k)).then_inc(consts.sem, 16)
            sp.dma_start(rows[:], io["ln1"].rearrange("(o a) n -> o a n", o=1).to_broadcast([P, 2, D])).then_inc(consts.sem, 16)
            sp.dma_start(small[:], io["small"].to_broadcast([P, NR + NG + EPG])).then_inc(consts.sem, 16)
            sp.dma_start(ident[:], io["ident"]).then_inc(consts.sem, 16)
            sp.dma_start(eps[:], io["eps"]).then_inc(consts.sem, 16)
            sp.dma_start(vcol[:], io["vcol"]).then_inc(consts.sem, 16)
            sp.sem_inc(h_out.sem, 16)

            def tile(t):
                static = isinstance(t.i, int)
                return (bass.ds(t.i * P if static else sp.snap(t.i * P), P), bass.ds(t.i if static else sp.snap(t.i), 1))

            def proj(t, woven_in):
                t.ahead((aten, "first_half", -1), (avec, "residual", -1))
                col, i = tile(t)
                yield
                t.w0(aten, "first_half")
                at_in.go(sp.dma_start(at[:], scr["attn"][col, :]))
                mix_in.go(sp.dma_start(mix_r[:], scr["rwT"].rearrange("(c p) n -> p c n", p=P)[:, :, col]))
                t.w0(avec, "residual")
                x_in.go(sp.dma_start(x[:], io["x"][i].rearrange("a p n -> p (a n)")))

            def route(t, woven_in):
                t.ahead((apol, "h", 0))
                col, _ = tile(t)
                yield
                t.w(apol, "h")
                h_out.go(sp.dma_start(scr["h"][col, :], h[:]))

            woven(sp, NT, None, None, proj, route, "abab")
            sp.wait_ge(h_out.sem, h_out.done(NT - 1))

        @block.gpsimd
        def _(g):
            g.wait_ge(consts.sem, consts.done(0))

            def proj(t, woven_in):
                t.w(avec, "gain")
                t.w0(bten, "h_T1")
                t.left(h_out)
                t.mark(g.tensor_tensor(h[:], n[:], rows[:, 1, :], ALU.add), "h")
                yield

            woven(g, NT, apol, None, proj, None, "")

        @block.scalar
        def _(a):
            a.wait_ge(consts.sem, consts.done(0))

            def proj(t, woven_in):
                t.w(aten, "attn_T")
                t.mark(a.activation(mix_a[:], b4[0], ACT.Copy), "attn_T")
                yield
                t.w(avec, "stats")
                t.mark(a.activation(rstd[:], mv[:, 1:2], ACT.Sqrt, bias=eps[:, 0:1]), "root")
                t.w(avec, "shift")
                t.w0(apol, "h")
                t.mark(a.activation(n[:], r[:], ACT.Identity, bias=nmr[:, 0:1], scale=rstd[:, 0:1]), "normed")

            def route(t, woven_in):
                for k in range(2):
                    t.w(bten, f"h_T{k}")
                    t.mark(a.activation(hT[:, 4 * k:4 * k + 4, :], b4[3 + k], ACT.Copy), f"h_T{k}")
                yield

            woven(a, NT, aact, bact, proj, route, "aba")
            a.wait_ge(chosen, 2)
            a.activation(eg[:], eg[:], ACT.Exp).then_inc(exps, 1)
            a.wait_ge(chosen, ROUTE_GAP)
            a.activation(one[:, 4, :], one[:, 3, :], ACT.Exp).then_inc(exps, 1)

        @block.tensor
        def _(pe):
            pe.wait_ge(consts.sem, consts.done(0))

            def half(b, mix, k0, start):
                for k in range(4):
                    ins = pe.matmul(bank[1 + b][:, :], mix[:, k, :], w_o[:, k0 + k, b * 512:(b + 1) * 512],
                                    start=(start and k == 0), stop=(not start and k == 3))
                return ins

            def proj(t, woven_in):
                t.arrived(at_in)
                t.w0(aact, "attn_T")
                for c in range(4):
                    ins = pe.transpose(b4[0][:, c, :], at[:, c * P:(c + 1) * P], ident[:, :])
                t.mark(ins, "attn_T")
                t.arrived(mix_in)
                t.w0(avec, "residual")
                half(0, mix_r, 4, True)
                t.mark(half(1, mix_r, 4, True), "first_half")
                t.w(aact, "attn_T")
                half(0, mix_a, 0, False)
                yield
                t.mark(half(1, mix_a, 0, False), "out_proj")
                yield

            def route(t, woven_in):
                t.w(apol, "h")
                for k in range(2):
                    for c in range(4):
                        ins = pe.transpose(b4[3 + k][:, c, :], h[:, (4 * k + c) * P:(4 * k + c + 1) * P], ident[:, :])
                    t.mark(ins, f"h_T{k}")
                yield
                t.w(bact, "h_T1")
                t.w0(bvec, "logits")
                for k in range(KC):
                    ins = pe.matmul(bank[5][:, 0:NR], hT[:, k, :], w_r[:, k, :], start=(k == 0), stop=(k == KC - 1))
                t.mark(ins, "logits")

            woven(pe, NT, aten, bten, proj, route, "abab")

        @block.vector
        def _(v):
            v.wait_ge(consts.sem, consts.done(0))

            def proj(t, woven_in):
                do = t.do
                t.w(aten, "out_proj")
                t.arrived(x_in)
                for b in range(2):
                    s = slice(b * 512, b * 512 + 512)
                    ins = v.scalar_tensor_tensor(out=r[:, s], in0=x[:, s], scalar=ALPHA, in1=bank[1 + b][:, :],
                                                 op0=ALU.mult, op1=ALU.add)
                do(ins, "residual")
                for b in range(2):
                    ins = v.bn_stats(st[:, b, :], r[:, b * 512:b * 512 + 512])
                do(ins, "half_stats")
                v.tensor_copy(rstd[:], st[:, 0, 0:1])
                do(v.bn_aggr(mv[:], st[:]), "stats")
                t.w(aact, "root")
                do(v.reciprocal(rstd[:], rstd[:]), "rstd")
                do(v.scalar_tensor_tensor(out=nmr[:], in0=mv[:, 0:1], scalar=-1.0, in1=rstd[:], op0=ALU.mult,
                                          op1=ALU.mult), "shift")
                t.w(aact, "normed")
                do(v.tensor_tensor(n[:], n[:], rows[:, 0, :], ALU.mult), "gain")
                yield

            def route(t, woven_in):
                t.w(bten, "logits")
                t.mark(v.tensor_tensor(lgs[:, bass.ds(t.i * NR, NR)], bank[5][:, 0:NR], bias, ALU.add), "logits")
                yield

            woven(v, NT, avec, bvec, proj, route, "ba")
            v.wait_ge(bvec.sem, bvec.done(NT - 1, "logits"))

            count = [0]

            def do(ins):
                count[0] += 1
                ins.then_inc(chosen, 1)
                v.wait_ge(chosen, count[0])

            def tt(out, a, b, op):
                do(v.tensor_tensor(out, a, b, op))

            lg = lgs[:].rearrange("p (t n) -> p t n", n=NR)
            groups, experts_ = lg[:, :, 0:NG], lg[:, :, NG:NR]
            top, first, prob, gap, egap, share = (one[:, k, :] for k in range(6))
            do(v.tensor_reduce(top, groups, AX.X, ALU.max))
            tt(eg[:], groups, bc(top, NG), ALU.subtract)
            tt(ohg[:], groups, bc(top, NG), ALU.is_equal)
            tt(ohg[:], ohg[:], bm(prio4, NT), ALU.mult)
            do(v.tensor_reduce(first, ohg[:], AX.X, ALU.max))
            tt(ohg[:], ohg[:], bc(first, NG), ALU.is_equal)
            v.wait_ge(exps, 1)
            do(v.tensor_reduce(prob, eg[:], AX.X, ALU.add))
            do(v.reciprocal(prob, prob))
            tt(ing[:].rearrange("p t (g e) -> p t g e", g=NG), experts_.rearrange("p t (g e) -> p t g e", g=NG),
               ohg[:].unsqueeze(3).to_broadcast([P, NT, NG, EPG]), ALU.mult)
            do(v.tensor_reduce(ein[:], ing[:].rearrange("p t (g e) -> p t e g", g=NG), AX.X, ALU.add))
            for k, (src, dst) in enumerate(((ein, o1), (e2, o2))):
                m = one[:, 6 + k, :]
                do(v.tensor_reduce(m, src[:], AX.X, ALU.max))
                tt(pr8[:], src[:], bc(m, EPG), ALU.is_equal)
                tt(pr8[:], pr8[:], bm(prio8, NT), ALU.mult)
                do(v.tensor_reduce(first, pr8[:], AX.X, ALU.max))
                tt(dst[:], pr8[:], bc(first, EPG), ALU.is_equal)
                if k == 0:
                    do(v.scalar_tensor_tensor(out=e2[:], in0=o1[:], scalar=-1e30, in1=ein[:], op0=ALU.mult, op1=ALU.add))
            tt(gap, one[:, 7, :], one[:, 6, :], ALU.subtract)
            assert count[0] == ROUTE_GAP, count[0]
            v.wait_ge(exps, 2)
            do(v.tensor_scalar(share, egap, 1.0, None, ALU.add))
            do(v.reciprocal(share, share))
            tt(share, share, prob, ALU.mult)
            do(v.tensor_copy(gate[:, 0:NT], share))
            tt(gate[:, NT:2 * NT], egap, share, ALU.mult)
            tt(ohg[:], ohg[:], bc(vcol[:, :], NG), ALU.mult)
            for k, o in enumerate((o1, o2)):
                out = oh[:, k * NT * NE:(k + 1) * NT * NE]
                tt(out.rearrange("p (t g e) -> p t g e", g=NG, e=EPG),
                   ohg[:].unsqueeze(3).to_broadcast([P, NT, NG, EPG]),
                   o[:].unsqueeze(2).to_broadcast([P, NT, NG, EPG]), ALU.mult)


def dispatch(nc, io, scr, keep):
    oh = keep["onehot"]
    table = scr["table"]
    with ExitStack() as ctx:
        def sb(name, shape, dt=F32):
            return ctx.enter_context(nc.sbuf_tensor("di_" + name, shape, dt))

        KB = SEQ // P + 1
        ps = ctx.enter_context(nc.psum_tensor("di_ps", [P, 512], F32))
        SPLIT = (NT - 1) * NE
        pb = [ctx.enter_context(nc.psum_tensor(f"di_pb{b}", [P, 512], F32)) for b in range(4)]
        nums = sb("nums", [P, KB + NBLK])
        cols = sb("cols", [P, 3, NT])
        cst = sb("cst", [P, 3, P])
        ident = cst[:, 0, :]
        both = sb("both", [P, NT * NE])
        base = sb("base", [P, NT + 1, NE])
        ranks = sb("ranks", [P, NT, NE])
        ones = sb("ones", [P, NE])
        cmp1 = sb("cmp1", [P, NE, KB])
        cmp2 = sb("cmp2", [P, NBLK, NE])
        blocks = sb("blocks", [P, NE])
        ends = sb("ends", [P, NE])
        starts = sb("starts", [P, NE])
        be, be4 = sb("be", [P, NBLK]), sb("be4", [P, NBLK])
        tmp = sb("tmp", [P, NT, NE])
        dest = sb("dest", [P, 2, NT])
        desti = sb("desti", [P, 2 * NT], I32)
        zero = sb("zero", [NBLK + 2, P])
        tok = sb("tok", [NBLK, P])

        vec = ctx.enter_context(nc.semaphore("di_vec"))
        consts = ctx.enter_context(nc.semaphore("di_consts"))
        cleared = ctx.enter_context(nc.semaphore("di_cleared"))
        scattered = ctx.enter_context(nc.semaphore("di_scattered"))
        tok_in = ctx.enter_context(nc.semaphore("di_tok_in"))
        counted = ctx.enter_context(nc.semaphore("di_counted"))
        turned = ctx.enter_context(nc.semaphore("di_turned"))
        SUMMED = 3
        DEST = NT + 20
        block = ctx.enter_context(nc.Block())

        @block.sync
        def _(sp):
            sp.dma_start(nums[:], io["nums"].to_broadcast([P, KB + NBLK])).then_inc(consts, 16)
            sp.dma_start(cols[:], io["cols"].rearrange("p (a n) -> p a n", a=3)).then_inc(consts, 16)
            sp.dma_start(cst[:], io["cst3"].rearrange("p (a n) -> p a n", a=3)).then_inc(consts, 16)
            sp.wait_ge(vec, 1)
            sp.dma_start(table.rearrange("(b p) o -> b (p o)", p=P), zero[:]).then_inc(cleared, 16)
            sp.wait_ge(scattered, 16 * 2 * NT)
            sp.dma_start(tok[:], table[0:NBLK * P].rearrange("(b p) o -> b (p o)", p=P)).then_inc(tok_in, 16)
            sp.wait_ge(tok_in, 16)

        @block.gpsimd
        def _(g):
            g.wait_ge(cleared, 16)
            g.wait_ge(vec, DEST)
            for n in range(2 * NT):
                g.indirect_dma_start(table, bass.IndirectOffsetOnAxis(ap=desti[:, n:n + 1], axis=0),
                                     cols[:, 0, n % NT:n % NT + 1], None).then_inc(scattered, 16)
            g.wait_ge(scattered, 16 * 2 * NT)

        @block.tensor
        def _(pe):
            pe.wait_ge(consts, 48)
            pe.wait_ge(vec, SUMMED)
            for k in range(2):
                pe.matmul(pb[2 * k][:, 0:SPLIT], cst[:, 1 + k, :], both[:, 0:SPLIT], start=True, stop=True)
                ins = pe.matmul(pb[2 * k + 1][:, 0:NE], cst[:, 1 + k, :], both[:, SPLIT:], start=True, stop=True)
            ins.then_inc(counted, 1)
            pe.wait_ge(tok_in, 16)
            pe.transpose(ps[:, 0:NBLK], tok[:], ident[0:NBLK, 0:NBLK]).then_inc(turned, 1)

        @block.vector
        def _(v):
            n = [0]

            def do(ins):
                n[0] += 1
                ins.then_inc(vec, 1)
                v.wait_ge(vec, n[0])

            do(v.memset(zero[:], 0.0))
            do(v.memset(ones[:], 1.0))
            do(v.tensor_tensor(both[:], oh[:, 0:NT * NE], oh[:, NT * NE:], ALU.add))
            assert n[0] == SUMMED, n[0]
            do(v.memset(base[:, 0, :], 0.0))
            v.wait_ge(consts, 48)
            v.wait_ge(counted, 1)
            for t in range(NT):
                c = pb[2][:, t * NE:(t + 1) * NE] if t < NT - 1 else pb[3][:, 0:NE]
                do(v.tensor_tensor(base[:, t + 1, :], base[:, t, :], c, ALU.add))
            b = pb[0][:, 0:SPLIT].rearrange("p (t e) -> p t e", e=NE)
            do(v.tensor_tensor(ranks[:, 0:NT - 1, :], base[:, 0:NT - 1, :], b, ALU.add))
            do(v.tensor_tensor(ranks[:, NT - 1, :], base[:, NT - 1, :], pb[1][:, 0:NE], ALU.add))
            counts = base[:, NT, :]
            do(v.tensor_tensor(cmp1[:], bc(counts, KB), bm(nums[:, 0:KB], NE), ALU.is_gt))
            do(v.tensor_reduce(blocks[:], cmp1[:], AX.X, ALU.add))
            do(v.tensor_tensor_scan(ends[:], ones[:], blocks[:], 0.0, ALU.mult, ALU.add))
            do(v.tensor_tensor(starts[:], ends[:], blocks[:], ALU.subtract))
            do(v.tensor_scalar(starts[:], starts[:], float(P), None, ALU.mult))
            do(v.tensor_tensor(ranks[:], ranks[:], bm(starts[:], NT), ALU.add))
            for s in range(2):
                o = oh[:, s * NT * NE:(s + 1) * NT * NE].rearrange("p (t e) -> p t e", e=NE)
                do(v.tensor_tensor(tmp[:], o, ranks[:], ALU.mult))
                do(v.tensor_reduce(dest[:, s, :], tmp[:], AX.X, ALU.add))
            do(v.tensor_copy(keep["rows"][:], dest[:].rearrange("p a n -> p (a n)")))
            do(v.tensor_tensor(dest[:], dest[:], bm(cols[:, 1, :], 2), ALU.add))
            do(v.tensor_scalar(dest[:, 1, NT - 1:NT], dest[:, 1, NT - 1:NT], cols[:, 2, 0:1], None, ALU.add))
            do(v.tensor_copy(desti[:], dest[:].rearrange("p a n -> p (a n)")))
            assert n[0] == DEST, n[0]
            do(v.tensor_tensor(cmp2[:], bm(ends[:], NBLK), bc(nums[:, KB:KB + NBLK], NE), ALU.is_le))
            do(v.tensor_reduce(be[:], cmp2[:], AX.X, ALU.add))
            do(v.tensor_scalar(be[:], be[:], float(NE - 1), None, ALU.min))
            do(v.tensor_copy(keep["block_expert"][:], be[:]))
            v.tensor_scalar(be4[:], be[:], float(P // SLOTS), None, ALU.mult)
            do(v.memset(keep["free_at"][:, 0:SLOTS], 0))
            groups = NE // SLOTS - 1
            do(v.tensor_tensor(cmp2[:, :, 0:groups], bc(be4[:], groups), bm(nums[:, 1:1 + groups], NBLK), ALU.is_ge))
            do(v.tensor_reduce(be4[:], cmp2[:, :, 0:groups], AX.X, ALU.add))
            do(v.scalar_tensor_tensor(out=be4[:], in0=be4[:], scalar=-float(SLOTS), in1=be[:], op0=ALU.mult,
                                      op1=ALU.add))
            do(v.tensor_copy(keep["slot"][:], be4[:]))
            do(v.tensor_copy(keep["free_at"][:, SLOTS:SLOTS + NE], ends[:]))
            v.wait_ge(turned, 1)
            do(v.tensor_copy(keep["tokens"][:], ps[:, 0:NBLK]))


def experts(nc, io, scr, keep):
    with ExitStack() as ctx:
        def sb(name, shape, dt=F32):
            return ctx.enter_context(nc.sbuf_tensor("ex_" + name, shape, dt))

        FC = FE // P
        bank = [ctx.enter_context(nc.psum_tensor(f"ex_bank{b}", [P, 512], F32)) for b in range(8)]
        b4 = [b[:, :].rearrange("p (a n) -> p a n", a=4) for b in bank]
        ident = sb("ident", [P, P])
        nought = sb("nought", [P, 1])
        spare = [sb(f"spare{s}", [P, 1]) for s in range(2)]
        started = ctx.enter_context(nc.semaphore("ex_started"))
        wg, wu, wd = sb("wg", [P, SLOTS, KC * FE]), sb("wu", [P, SLOTS, KC * FE]), sb("wd", [P, SLOTS, FC * D])
        idx, x, xT, th, hid, hT, y = ([sb(f"{n}{s}", shape, dt) for s in range(2)] for n, shape, dt in (
            ("idx", [P, 1], I32), ("x", [P, D], F32), ("xT", [P, KC, P], F32), ("th", [P, FE], F32),
            ("hid", [P, FE], F32), ("hT", [P, FC, P], F32), ("y", [P, D], F32)))

        A = {n: Steps(nc, ctx, "up_" + n) for n in ("tensor", "vector", "scalar", "gpsimd")}
        B = {n: Steps(nc, ctx, "down_" + n) for n in ("tensor", "scalar")}
        aten, avec, aact, apol = A["tensor"], A["vector"], A["scalar"], A["gpsimd"]
        bten, bact = B["tensor"], B["scalar"]
        const = Dmas(nc, ctx, "ex_const", 1)
        w_in = [Dmas(nc, ctx, f"ex_w_in{s}", 3, 1) for s in range(SLOTS)]
        ready = ctx.enter_context(nc.semaphore("ex_weights_ready"))
        x_in = [Dmas(nc, ctx, f"ex_x_in{s}", 1) for s in range(2)]
        y_out = [Dmas(nc, ctx, f"ex_y_out{s}", 1, 1) for s in range(2)]
        block = ctx.enter_context(nc.Block())
        turns = NBLK // 2


        @block.sync
        def _(sp):
            sp.dma_start(ident[:], io["ident"]).then_inc(const.sem, 16)
            for s in range(SLOTS):
                sp.sem_inc(w_in[s].sem, 16 * 3)

            def turn(t):
                ends = [sp.value_load(keep["free_at"][0:1, bass.ds(t.i * SLOTS + s, 1)], min_val=0,
                                      max_val=NBLK) for s in range(SLOTS)]
                free_at = [sp.snap(e * (bten.per // 2) + bten.per) for e in ends]
                es = [bass.ds(sp.snap(t.i * SLOTS + s), 1) for s in range(SLOTS)]
                t.ahead(*[(w_in[(s - 2) % SLOTS], None, -1 if s < 2 else 0) for s in range(SLOTS)])
                for s, e in enumerate(es):
                    t._wait(w_in[(s - 2) % SLOTS], None, -1 if s < 2 else 0)
                    sp.sem_inc(ready, 1)
                    sp.wait_ge(bten.sem, free_at[s])
                    for dst, src, k in ((wg, io["w_eg"], KC), (wu, io["w_eu"], KC), (wd, io["w_ed"], FC)):
                        w_in[s].go(sp.dma_start(dst[:, s, :], src[e].rearrange("a (p k) n -> (a p) (k n)", k=k)))

            engine_loop(sp, None, NE // SLOTS, turn)
            for s in range(SLOTS - 2, SLOTS):
                sp.wait_ge(w_in[s].sem, w_in[s].done(NE // SLOTS - 1))
                sp.sem_inc(ready, 1)

        @block.gpsimd
        def _(g):
            g.memset(nought[:], 0.0).then_inc(started, 1)
            g.wait_ge(started, 1)

            def up(t, woven_in):
                for s in range(2):
                    t.w0(aten, f"x_T{s}1")
                    t.do(g.tensor_copy(idx[s][:], keep["tokens"][:, bass.ds(t.i * 2 + s, 1)]), f"idx{s}")
                    g.tensor_tensor(spare[s][:], nought[:], nought[:], ALU.add)
                    x_in[s].go(g.indirect_dma_start(x[s][:], None, scr["h"],
                                                    bass.IndirectOffsetOnAxis(ap=idx[s][:, 0:1], axis=0)))
                yield

            woven(g, turns, apol, None, up, None, "")

        @block.scalar
        def _(a):
            a.sem_inc(y_out[0].sem, 16)
            a.sem_inc(y_out[1].sem, 16)

            def up(t, woven_in):
                for s in range(2):
                    for k in range(2):
                        t.w(aten, f"x_T{s}{k}")
                        t.mark(a.activation(xT[s][:, 4 * k:4 * k + 4, :], b4[2 * s + k], ACT.Copy), f"x_T{s}{k}")
                yield
                for s in range(2):
                    t.w(aten, f"gate{s}")
                    t.w0(avec, f"hidden{s}")
                    t.mark(a.activation(th[s][:], bank[4][:, 0:FE], ACT.Tanh, scale=0.5), f"tanh{s}")
                    yield

            def down(t, woven_in):
                for s in range(2):
                    t.w(bten, f"h_T{s}")
                    t.mark(a.activation(hT[s][:], b4[2][:, 0:FC, :], ACT.Copy), f"h_T{s}")
                    yield
                    t.w(bten, f"down{s}")
                    t.left(y_out[s])
                    a.activation(y[s][:, 0:512], bank[6][:, :], ACT.Copy)
                    t.do(a.activation(y[s][:, 512:D], bank[7][:, :], ACT.Copy), f"y{s}")
                    y_out[s].go(a.dma_start(scr["ys"][bass.ds((t.i * 2 + s) * P, P), :], y[s][:]))
                    yield

            woven(a, turns, aact, bact, up, down, "bababba")
            for s in range(2):
                a.wait_ge(y_out[s].sem, y_out[s].done(turns - 1))

        @block.tensor
        def _(pe):
            pe.wait_ge(const.sem, 16)

            def value(name, t, s, top):
                return pe.value_load(keep[name][0:1, bass.ds(t.i * 2 + s, 1)], min_val=0, max_val=top)

            def up(t, woven_in):
                experts_ready = [pe.snap(value("block_expert", t, s, NE - 1) + 3) for s in range(2)]
                slots = [bass.ds(value("slot", t, s, SLOTS - 1), 1) for s in range(2)]
                yield
                for s in range(2):
                    t.arrived(x_in[s])
                    if s == 0:
                        t.w0(aact, "x_T11")
                    else:
                        t.w0(bact, "h_T0")
                    xv = x[s][:, :].rearrange("t (p k) -> t k p", k=KC)
                    for k in range(2):
                        for c in range(4):
                            ins = pe.transpose(b4[2 * s + k][:, c, :], xv[:, 4 * k + c, :], ident[:, :])
                        t.mark(ins, f"x_T{s}{k}")
                yield
                for s in range(2):
                    pe.wait_ge(ready, experts_ready[s])
                    t.w(aact, f"x_T{s}1")
                    for n, (w, name, read) in enumerate(((wg, "gate", "silu"), (wu, "up", "hidden"))):
                        (t.w0 if s == 0 else t.w)(avec, f"{read}{1 - s}")
                        wv = w[:, slots[s], :].rearrange("p a n -> p (a n)")
                        for k in range(KC):
                            ins = pe.matmul(bank[4 + n][:, 0:FE], xT[s][:, k, :],
                                            wv[:, k * FE:(k + 1) * FE], start=(k == 0), stop=(k == KC - 1))
                        t.mark(ins, f"{name}{s}")
                        yield

            def down(t, woven_in):
                slots = [bass.ds(value("slot", t, s, SLOTS - 1), 1) for s in range(2)]
                yield
                for s in range(2):
                    t.w(avec, f"hidden{s}")
                    if s == 1 and woven_in:
                        t.next_done(aact, "x_T10")
                    for m in range(FC):
                        ins = pe.transpose(b4[2][:, m, :], hid[s][:, m:FE:FC], ident[:, :])
                    t.mark(ins, f"h_T{s}")
                    yield
                    t.w(bact, f"h_T{s}")
                    wv = wd[:, slots[s], :].rearrange("p a n -> p (a n)")
                    for n in range(2):
                        for m in range(FC):
                            ins = pe.matmul(bank[6 + n][:, :], hT[s][:, m, :], wv[:, m * D + n * 512:m * D + (n + 1) * 512],
                                            start=(m == 0), stop=(m == FC - 1))
                    t.mark(ins, f"down{s}")
                    yield

            woven(pe, turns, aten, bten, up, down, "abbabababaa")

        @block.vector
        def _(v):
            def up(t, woven_in):
                for s in range(2):
                    t.w(aact, f"tanh{s}")
                    t.do(v.scalar_tensor_tensor(out=th[s][:], in0=th[s][:], scalar=1.0, in1=bank[4][:, 0:FE],
                                                op0=ALU.add, op1=ALU.mult), f"silu{s}")
                    t.w(aten, f"up{s}")
                    t.w0(bten, f"h_T{s}")
                    t.mark(v.scalar_tensor_tensor(out=hid[s][:], in0=th[s][:], scalar=0.5, in1=bank[5][:, 0:FE],
                                                  op0=ALU.mult, op1=ALU.mult), f"hidden{s}")
                yield

            woven(v, turns, avec, None, up, None, "")


def combine(nc, io, scr, keep):
    with ExitStack() as ctx:
        def sb(name, shape, dt=F32):
            return ctx.enter_context(nc.sbuf_tensor("co_" + name, shape, dt))

        rows = sb("rows", [P, 2, D])
        eps = sb("eps", [P, 1])
        idx = [sb(f"idx{s}", [P, 1], I32) for s in range(2)]
        y = [sb(f"y{s}", [P, D]) for s in range(2)]
        h = sb("h", [P, D])
        r = sb("r", [P, D])
        r2 = sb("r2", [P, D])
        both = sb("both", [P, D])
        n = sb("n", [P, D])
        o = sb("o", [P, D])
        st = sb("st", [P, 2, 6])
        mv = sb("mv", [P, 2])
        rstd, nmr = sb("rstd", [P, 1]), sb("nmr", [P, 1])
        gates = sb("gates", [P, 2])
        nought, spare = sb("nought", [P, 1]), sb("spare", [P, 1])
        started = ctx.enter_context(nc.semaphore("co_started"))
        gate = keep["gate"]

        A = {e: Steps(nc, ctx, "sum_" + e) for e in ("vector", "scalar", "gpsimd")}
        B = {e: Steps(nc, ctx, "norm_" + e) for e in ("vector", "scalar")}
        avec, aact, apol = A["vector"], A["scalar"], A["gpsimd"]
        bvec, bact = B["vector"], B["scalar"]
        consts = Dmas(nc, ctx, "co_consts", 2)
        y_in = [Dmas(nc, ctx, f"co_y_in{s}", 1) for s in range(2)]
        h_in = Dmas(nc, ctx, "co_h_in", 1)
        out = Dmas(nc, ctx, "co_out", 1, 1)
        block = ctx.enter_context(nc.Block())

        @block.sync
        def _(sp):
            sp.dma_start(rows[:], io["ln2"].rearrange("(o a) n -> o a n", o=1).to_broadcast([P, 2, D])).then_inc(consts.sem, 16)
            sp.dma_start(eps[:], io["eps"]).then_inc(consts.sem, 16)
            sp.sem_inc(out.sem, 16)

            def col(t):
                return bass.ds(t.i * P if isinstance(t.i, int) else sp.snap(t.i * P), P)

            def add(t, woven_in):
                t.ahead((avec, "residual", -1))
                c = col(t)
                yield
                t.w0(avec, "residual")
                h_in.go(sp.dma_start(h[:], scr["h"][c, :]))

            def norm(t, woven_in):
                t.ahead((bvec, "y", 0))
                c = col(t)
                yield
                t.w(bvec, "y")
                out.go(sp.dma_start(io["y_out"][c, :], o[:]))

            woven(sp, NT, None, None, add, norm, "abab")
            sp.wait_ge(out.sem, out.done(NT - 1))

        @block.gpsimd
        def _(g):
            g.memset(nought[:], 0.0).then_inc(started, 1)
            g.wait_ge(started, 1)
            g.wait_ge(consts.sem, consts.done(0))

            def add(t, woven_in):
                t.w0(aact, "first")
                for s in range(2):
                    if s == 1:
                        t.w0(avec, "second")
                    t.do(g.tensor_copy(idx[s][:], keep["rows"][:, bass.ds(t.i + s * NT, 1)]), f"idx{s}")
                    g.tensor_tensor(spare[:], nought[:], nought[:], ALU.add)
                    y_in[s].go(g.indirect_dma_start(y[s][:], None, scr["ys"],
                                                    bass.IndirectOffsetOnAxis(ap=idx[s][:, 0:1], axis=0)))
                yield

            woven(g, NT, apol, None, add, None, "")

        @block.scalar
        def _(a):
            a.wait_ge(consts.sem, consts.done(0))

            def add(t, woven_in):
                t.arrived(y_in[0])
                t.w(avec, "gates")
                t.mark(a.activation(both[:], y[0][:], ACT.Copy, scale=gates[:, 0:1]), "first")
                yield

            def norm(t, woven_in):
                t.w(bvec, "stats")
                t.mark(a.activation(rstd[:], mv[:, 1:2], ACT.Sqrt, bias=eps[:, 0:1]), "root")
                t.w(bvec, "shift")
                t.mark(a.activation(n[:], r[:], ACT.Identity, bias=nmr[:, 0:1], scale=rstd[:, 0:1]), "normed")
                yield

            woven(a, NT, aact, bact, add, norm, "ab")

        @block.vector
        def _(v):
            v.wait_ge(consts.sem, consts.done(0))

            def add(t, woven_in):
                do = t.do
                t.w0(aact, "first")
                v.tensor_copy(gates[:, 0:1], gate[:, bass.ds(t.i, 1)])
                do(v.tensor_copy(gates[:, 1:2], gate[:, bass.ds(t.i + NT, 1)]), "gates")
                yield
                t.arrived(y_in[1])
                t.w(aact, "first")
                do(v.scalar_tensor_tensor(out=both[:], in0=y[1][:], scalar=gates[:, 1:2], in1=both[:],
                                          op0=ALU.mult, op1=ALU.add), "second")
                t.arrived(h_in)
                t.w0(bact, "normed")
                do(v.scalar_tensor_tensor(out=r[:], in0=h[:], scalar=ALPHA, in1=both[:], op0=ALU.mult, op1=ALU.add),
                   "residual")

            def norm(t, woven_in):
                do = t.do
                for c in range(2):
                    ins = v.bn_stats(st[:, c, :], r[:, c * 512:c * 512 + 512])
                do(ins, "half_stats")
                t.w0(bact, "normed")
                v.tensor_copy(rstd[:], st[:, 0, 0:1])
                do(v.bn_aggr(mv[:], st[:]), "stats")
                t.w(bact, "root")
                do(v.reciprocal(rstd[:], rstd[:]), "rstd")
                do(v.scalar_tensor_tensor(out=nmr[:], in0=mv[:, 0:1], scalar=-1.0, in1=rstd[:], op0=ALU.mult,
                                          op1=ALU.mult), "shift")
                yield
                t.w(bact, "normed")
                do(v.tensor_tensor(r2[:], n[:], rows[:, 0, :], ALU.mult), "gain")
                t.left(out)
                do(v.tensor_tensor(o[:], r2[:], rows[:, 1, :], ALU.add), "y")

            woven(v, NT, avec, bvec, add, norm, "abab")


def _shape_constants():
    k, t = np.arange(P)[:, None], np.arange(P)[None, :]
    head = (k // 64 == t // 64)
    f = np.float32

    def off(size):
        return (k // size % 2 == 0) & (t // size == k // size + 1)

    cst = np.stack([head, head / 64.0, k < t, k <= t, k > t, off(1), off(1).T], 1).astype(f).reshape(P, 7 * P)
    levs = np.stack([off(2 ** n).reshape(P, -1, 2, 2 ** n)[:, :, 1].reshape(P, 64) for n in range(1, LEVELS + 1)], 1)
    levs = levs.astype(f).reshape(P, LEVELS * 64)
    rms = np.stack([np.full((P, P), 1.0 / QL), np.full((P, P), 1.0 / KVL)], 1).astype(f).reshape(P, 2 * P)
    half = ROPE // 2
    inv = (f(10000.0) ** (-np.arange(0, ROPE, 2, dtype=f) / f(ROPE))).astype(f)
    pos = np.zeros((NT, P), f)
    pos[:NT - 1] = np.arange(SEQ, dtype=f).reshape(NT - 1, P)
    pos[NT - 1] = PAST + np.arange(P, dtype=f)
    ang = (pos[:, :, None] * inv).astype(f).astype(np.float64)
    cos, sin = np.cos(ang), np.sin(ang)
    both = np.stack([np.concatenate([cos, cos], -1), np.concatenate([-sin, sin], -1)], 2)
    rope = np.tile(both.transpose(0, 3, 2, 1), (1, 4, 1, 1)).astype(f).reshape(NT, P, 2 * P)
    assert half * 2 == ROPE
    valid = np.ones((NT, P), f)
    valid[NT - 1, DEC:] = 0
    return dict(cst=cst, levs=levs, rmsw=rms, rope=rope, ident=np.eye(P, dtype=f)), valid


def _by_channel(v):
    return np.moveaxis(v.reshape(v.shape[:-1] + (v.shape[-1] // P, P)), -1, 0)


def _layout(a):
    c, valid = _shape_constants()
    f = np.float32
    w = {k: np.asarray(v) for k, v in a.items()}

    def rows(m):
        return np.ascontiguousarray(m.reshape(-1, P, m.shape[1]).transpose(1, 0, 2)).reshape(P, -1)

    x = np.zeros((NT + 2, P, D), f)
    x[:NT - 1] = w["x_prompt"].reshape(NT - 1, P, D)
    x[NT - 1, :DEC] = w["x_sample"][0]
    c["x"] = x
    wi = w["w_in"][0]
    swap = np.r_[ROPE // 2:ROPE, 0:ROPE // 2]
    kpe = wi[:, QL + KVL:QL + KVL + ROPE]
    c["w_in"] = rows(np.concatenate([wi[:, :QL + KVL], wi[:, QL + KVL + ROPE:], kpe, kpe[:, swap]], 1))
    uq = w["w_uq"][0]
    pe = uq[:, :, NOPE:]
    c["w_uq"] = rows(np.concatenate([uq[:, :, :NOPE].reshape(QL, -1), pe.reshape(QL, -1),
                                     pe[:, :, swap].reshape(QL, -1)], 1))
    wa = np.zeros((P, 2, 512), f)
    wa[:64, 0], wa[64:, 1] = w["w2"][0], w["a2"][0]
    c["w_wa"] = wa.reshape(P, 1024)
    c["w_g"] = w["g2"][0]
    par = np.zeros((P, 64), f)
    vecs = [(0, "mu_shift"), (14, "q_norm_g"), (17, "kv_norm_g"), (20, "w0"), (24, "a0"), (28, "k_k"), (32, "k_a"),
            (36, "r_k"), (40, "lnx_g"), (44, "lnx_b")]
    for at, name in vecs:
        v = _by_channel(w[name][0].reshape(-1))
        par[:, at:at + v.shape[1]] = v
    par[:, 48], par[:, 49], par[:, 50] = RMS_EPS, GN_EPS, LN_EPS
    c["par"] = par
    keep = np.ones((NT, P, 1), f)
    keep[NT - 1] = 0
    shift = np.zeros((NT, P, NPR), f)
    shift[NT - 1] = _by_channel(w["state_shift"][0, 0])
    c["first"], c["keep"] = np.concatenate([keep, shift], 2), keep
    c["masks"] = np.stack([np.tile((-LOGW / 2) * valid[:, None, :], (1, P, 1)),
                           np.tile(valid[:, None, :], (1, P, 1))], 2).astype(f).reshape(NT, P, 2 * P)
    s_init = np.zeros((NT, 2, 64, 4, 64), f)
    s_init[NT - 1] = w["state_wkv"][0, 0].reshape(4, 2, 64, 64).transpose(1, 3, 0, 2)
    c["s_init"] = s_init.reshape(NT, P, 256)
    c["past_ckvT"] = rows(w["cache_ckv"][0, 0].T)
    c["past_kpeT"] = w["cache_kpe"][0, 0].T
    c["w_ukv"] = w["w_ukv"][0].reshape(CKV, P, H, P).transpose(2, 1, 0, 3).reshape(H, P, CKV * P)
    c["w_o"] = rows(w["w_o"][0])
    c["w_r"] = rows(np.concatenate([w["w_gr"][0], w["w_er"][0]], 1))
    c["ln1"] = np.stack([w["ln1_g"][0], w["ln1_b"][0]])
    c["ln2"] = np.stack([w["ln2_g"][0], w["ln2_b"][0]])
    c["small"] = np.concatenate([w["b_gr"][0], w["b_er"][0], np.arange(NG, 0, -1, dtype=f),
                                 np.arange(EPG, 0, -1, dtype=f)])[None]
    before = (np.arange(P)[:, None] < np.arange(P)[None, :]).astype(f)
    c["eps"] = np.full((P, 1), LN_EPS, f)
    c["cst3"] = np.stack([np.eye(P, dtype=f), before, np.ones((P, P), f)], 1).reshape(P, 3 * P)
    c["vcol"] = valid.T.copy()
    kb = SEQ // P + 1
    c["nums"] = np.concatenate([P * np.arange(kb), np.arange(NBLK)]).astype(f)[None]
    tok = np.arange(TOK).reshape(NT, P).T
    dump = (1 - valid.T) * (NBLK * P + np.arange(P)[:, None])
    again = np.tile((1 - valid[NT - 1])[:, None] * P, (1, NT))
    c["cols"] = np.stack([tok, dump, again], 1).astype(f).reshape(P, 3 * NT)
    for name in ("w_eg", "w_eu", "w_ed"):
        c[name] = w[name][0]
    return c


def program(nc, io, scr):
    mixer(nc, io, scr)
    attention(nc, io, scr)
    with ExitStack() as ctx:
        def kept(name, cols, dt=F32):
            return ctx.enter_context(nc.sbuf_tensor("kept_" + name, [P, cols], dt))

        keep = dict(onehot=kept("onehot", 2 * NT * NE), gate=kept("gate", 2 * NT), logits=kept("logits", NT * NR),
                    rows=kept("rows", 2 * NT, I32), tokens=kept("tokens", NBLK, I32),
                    block_expert=kept("block_expert", NBLK, I32),
                    slot=kept("slot", NBLK, I32), free_at=kept("free_at", SLOTS + NE, I32))
        router(nc, io, scr, keep)
        dispatch(nc, io, scr, keep)
        experts(nc, io, scr, keep)
        combine(nc, io, scr, keep)


_SCRATCH = dict(kpeT=(ROPE, TOK), ckvT=(KVL, TOK), qT=(H, QK, TOK), rwT=(512, TOK), attn=(TOK, 512), h=(TOK, D),
                table=((NBLK + 2) * P, 1), ys=(NBLK * P, D))
_OUTS = dict(y_out=(TOK, D), ckv_out=(NT, P, KVL), kpe_out=(NT, P, ROPE), edge_out=(NT, P, 2 * NPR),
             state_out=(NT, P, 256))
_SCRATCH_KIND = "Internal"


def _outputs(r):
    y, ckv, kpe, edge, state = (r["out_" + n] for n in _OUTS)
    ckv, kpe = ckv.reshape(TOK, KVL), kpe.reshape(TOK, ROPE)
    shift = [edge[t].reshape(P, 2, NPR)[:, e].T.reshape(1, 1, -1) for t, e in ((NT - 2, 1), (NT - 1, 0))]
    wkv = [state[t].reshape(2, 64, 4, 64).transpose(2, 0, 3, 1).reshape(1, 1, H, 64, 64) for t in (NT - 2, NT - 1)]
    s = slice(SEQ, SEQ + DEC)
    return (y[:SEQ][None], y[s][None], ckv[:SEQ][None, None], kpe[:SEQ][None, None], wkv[0], shift[0],
            ckv[s][None, None], kpe[s][None, None], wkv[1], shift[1])


def kernel(**inputs):
    import concourse.bacc as _bacc
    from concourse.bass_utils import run_bass_kernel_spmd as _run

    nc = _bacc.Bacc("TRN2", target_bir_lowering=False, num_devices=1)
    io, arrays = {}, {}
    for name, a in _layout(inputs).items():
        arrays["in_" + name] = np.ascontiguousarray(a)
        io[name] = nc.dram_tensor("in_" + name, a.shape, mybir.dt.from_np(a.dtype), kind="ExternalInput").ap()
    for name, shape in _OUTS.items():
        io[name] = nc.dram_tensor("out_" + name, shape, F32, kind="ExternalOutput").ap()
    scr = {name: nc.dram_tensor("scr_" + name, shape, F32, kind=_SCRATCH_KIND).ap() for name, shape in _SCRATCH.items()}
    program(nc, io, scr)
    return _outputs(_run(nc, [arrays], core_ids=[0]).results[0])
```
